# Optimizing a Trainium2 kernel written in Bass

```python
import math
import jax, jax.numpy as jnp
from jax import lax
import numpy as np

D_MODEL = 1024
BATCH = 1
SEQ = 256
DEPTH = 1

N_META = 16
NORM_EPS = 1e-6
HG_HEADS = 8
HG_DK = D_MODEL // HG_HEADS
HG_DV = D_MODEL // HG_HEADS
HG_WIDTH = HG_HEADS * HG_DK
HG_CHUNK = 16
MLA_HEADS = 8
QK_NOPE = 128
QK_ROPE = 64
V_HEAD = 128
Q_LORA = 256
KV_LORA = 256
ROPE_THETA = 10000.0
ATTN_BLOCK = 128
FFN_HIDDEN = ((8 * D_MODEL + 3 * 256 - 1) // (3 * 256)) * 256
IN_SIZES = (HG_WIDTH, HG_WIDTH, HG_WIDTH, HG_WIDTH,
            Q_LORA, KV_LORA, QK_ROPE,
            D_MODEL, D_MODEL)
IN_COLS = sum(IN_SIZES)


def rms_norm(x, g):
    xf = x.astype(jnp.float32)
    y = xf * lax.rsqrt(jnp.mean(xf * xf, axis=-1, keepdims=True) + NORM_EPS)
    return (y * g.astype(jnp.float32)).astype(x.dtype)

def rope_tables(length):
    pos = jnp.arange(length, dtype=jnp.float32)
    inv_freq = 1.0 / (ROPE_THETA ** (jnp.arange(0, QK_ROPE, 2, dtype=jnp.float32) / QK_ROPE))
    ang = pos[:, None] * inv_freq[None, :]
    return jnp.cos(ang), jnp.sin(ang)

def apply_rope(t, cos, sin):
    t32 = t.astype(jnp.float32)
    t1, t2 = jnp.split(t32, 2, axis=-1)
    return jnp.concatenate([t1 * cos - t2 * sin, t2 * cos + t1 * sin], axis=-1).astype(t.dtype)

def hgrn2_chunk_scan(q, k, v, logf):
    B, L, H, _ = q.shape
    n = L // HG_CHUNK

    def to_chunks(t):
        return t.reshape(B, n, HG_CHUNK, H, t.shape[-1]).transpose(1, 0, 3, 2, 4)

    xs = (to_chunks(q), to_chunks(k), to_chunks(v), to_chunks(logf))
    causal = jnp.tril(jnp.ones((HG_CHUNK, HG_CHUNK), dtype=bool))[:, :, None]

    def step(S, inp):
        qb, kb, vb, gb = inp
        b = jnp.cumsum(gb, axis=2)
        o_inter = jnp.einsum('bhtk,bhkv->bhtv', qb * jnp.exp(b), S)
        diff = b[:, :, :, None, :] - b[:, :, None, :, :]
        decay = jnp.exp(jnp.where(causal, diff, -jnp.inf))
        A = jnp.einsum('bhtsk,bhsk->bhts', decay * qb[:, :, :, None, :], kb)
        o_intra = jnp.einsum('bhts,bhsv->bhtv', A, vb)
        b_last = b[:, :, -1:, :]
        S_new = jnp.exp(b_last[:, :, 0, :])[..., None] * S + jnp.einsum(
            'bhsk,bhsv->bhkv', kb * jnp.exp(b_last - b), vb)
        return S_new, o_inter + o_intra

    S0 = jnp.zeros((B, H, q.shape[-1], v.shape[-1]), jnp.float32)
    _, ys = lax.scan(step, S0, xs)
    return ys.transpose(1, 0, 3, 2, 4).reshape(B, L, H, v.shape[-1])

def hgrn2_mixer(q, f_pre, i, g, lb, norm_g):
    B, L, _ = q.shape
    split = lambda t: t.reshape(B, L, HG_HEADS, -1).astype(jnp.float32)
    qh = jax.nn.silu(split(q))
    lbh = lb.astype(jnp.float32).reshape(HG_HEADS, HG_DK)
    fgate = lbh + (1.0 - lbh) * jax.nn.sigmoid(split(f_pre))
    o = hgrn2_chunk_scan(qh, 1.0 - fgate, split(i), jnp.log(fgate))
    o = rms_norm(o, norm_g) * jax.nn.silu(split(g))
    return o.reshape(B, L, HG_WIDTH).astype(q.dtype)

def mla_mixer(c_q, c_kv, k_pe, q_norm_g, w_q_b, kv_norm_g, w_kv_b, cos, sin):
    B, L, _ = c_q.shape
    q = (rms_norm(c_q, q_norm_g) @ w_q_b).reshape(B, L, MLA_HEADS, QK_NOPE + QK_ROPE)
    q_nope = q[..., :QK_NOPE]
    q_pe = apply_rope(q[..., QK_NOPE:], cos[:, None, :], sin[:, None, :])
    kv = (rms_norm(c_kv, kv_norm_g) @ w_kv_b).reshape(B, L, MLA_HEADS, QK_NOPE + V_HEAD)
    k_nope, v = kv[..., :QK_NOPE], kv[..., QK_NOPE:]
    k_pe = apply_rope(k_pe, cos, sin)
    scale = (QK_NOPE + QK_ROPE) ** -0.5
    bounds = [(0, N_META)] + [(N_META + s, min(N_META + s + ATTN_BLOCK, L))
                              for s in range(0, L - N_META, ATTN_BLOCK)]
    outs = []
    for start, end in bounds:
        s = (jnp.einsum('bqhd,bkhd->bhqk', q_nope[:, start:end], k_nope[:, :end])
             + jnp.einsum('bqhr,bkr->bhqk', q_pe[:, start:end], k_pe[:, :end]))
        s = s.astype(jnp.float32) * scale
        qpos = jnp.arange(start, end)[:, None]
        kpos = jnp.arange(end)[None, :]
        s = jnp.where(kpos <= qpos, s, -jnp.inf)
        p = jax.nn.softmax(s, axis=-1).astype(v.dtype)
        outs.append(jnp.einsum('bhqk,bkhd->bqhd', p, v[:, :end]))
    o = jnp.concatenate(outs, axis=1)
    return o.reshape(B, L, MLA_HEADS * V_HEAD)

def first_inputs(seed: int = 0) -> dict:
    key = jax.random.key(seed)
    ks = jax.random.split(key, 20)
    nrm = lambda k, shape, scale: jax.random.normal(k, shape, jnp.float32) * scale
    gain = lambda k, shape: 1.0 + 0.02 * jax.random.normal(k, shape, jnp.float32)
    return {
        "x": nrm(ks[0], (BATCH, SEQ, D_MODEL), 1.0),
        "meta_tokens": nrm(ks[1], (N_META, D_MODEL), 1.0),
        "w_in": nrm(ks[2], (DEPTH, D_MODEL, IN_COLS), D_MODEL ** -0.5),
        "b_gate": nrm(ks[3], (DEPTH, 2 * D_MODEL), 0.01),
        "lb_logits": nrm(ks[4], (DEPTH + 1, HG_WIDTH), 0.1),
        "hg_norm_g": gain(ks[5], (DEPTH, HG_DV)),
        "w_hg_o": nrm(ks[6], (DEPTH, HG_WIDTH, D_MODEL), HG_WIDTH ** -0.5),
        "q_a_norm_g": gain(ks[7], (DEPTH, Q_LORA)),
        "w_q_b": nrm(ks[8], (DEPTH, Q_LORA, MLA_HEADS * (QK_NOPE + QK_ROPE)), Q_LORA ** -0.5),
        "kv_a_norm_g": gain(ks[9], (DEPTH, KV_LORA)),
        "w_kv_b": nrm(ks[10], (DEPTH, KV_LORA, MLA_HEADS * (QK_NOPE + V_HEAD)), KV_LORA ** -0.5),
        "w_mla_o": nrm(ks[11], (DEPTH, MLA_HEADS * V_HEAD, D_MODEL), (MLA_HEADS * V_HEAD) ** -0.5),
        "w_out": nrm(ks[12], (DEPTH, D_MODEL, D_MODEL), D_MODEL ** -0.5),
        "mix_pre_g": gain(ks[13], (DEPTH, D_MODEL)),
        "mix_post_g": gain(ks[14], (DEPTH, D_MODEL)),
        "ffn_pre_g": gain(ks[15], (DEPTH, D_MODEL)),
        "ffn_post_g": gain(ks[16], (DEPTH, D_MODEL)),
        "w_ffn_in": nrm(ks[17], (DEPTH, D_MODEL, 2 * FFN_HIDDEN), D_MODEL ** -0.5),
        "w_ffn_out": nrm(ks[18], (DEPTH, FFN_HIDDEN, D_MODEL), FFN_HIDDEN ** -0.5),
    }

def first_block(x, meta_tokens, w_in, b_gate, lb_logits, hg_norm_g, w_hg_o, q_a_norm_g, w_q_b,
              kv_a_norm_g, w_kv_b, w_mla_o, w_out, mix_pre_g, mix_post_g, ffn_pre_g, ffn_post_g,
              w_ffn_in, w_ffn_out):
    B = x.shape[0]
    meta = jnp.broadcast_to(meta_tokens[None].astype(x.dtype), (B, N_META, D_MODEL))
    h = jnp.concatenate([meta, x], axis=1)
    L = h.shape[1]
    cos, sin = rope_tables(L)
    lower_bounds = jnp.cumsum(jax.nn.softmax(lb_logits.astype(jnp.float32), axis=0), axis=0)
    splits = []
    acc = 0
    for sz in IN_SIZES[:-2]:
        acc += sz
        splits.append(acc)
    for l in range(DEPTH):
        u = rms_norm(h, mix_pre_g[l])
        proj = u @ w_in[l]
        hq, hf, hi, hg, cq, ckv, kpe, gates = jnp.split(proj, splits, axis=-1)
        y_a = hgrn2_mixer(hq, hf, hi, hg, lower_bounds[l], hg_norm_g[l]) @ w_hg_o[l]
        y_b = mla_mixer(cq, ckv, kpe, q_a_norm_g[l], w_q_b[l], kv_a_norm_g[l], w_kv_b[l],
                        cos, sin) @ w_mla_o[l]
        gate_a, gate_b = jnp.split(jax.nn.sigmoid(gates + b_gate[l]), 2, axis=-1)
        mixed = (gate_a * y_a + gate_b * y_b) @ w_out[l]
        h = h + rms_norm(mixed, mix_post_g[l])
        u = rms_norm(h, ffn_pre_g[l])
        gt, up = jnp.split(u @ w_ffn_in[l], 2, axis=-1)
        h = h + rms_norm((jax.nn.silu(gt) * up) @ w_ffn_out[l], ffn_post_g[l])
    return h[:, N_META:, :]


DEPTH_2 = 2

D_MIX = D_MODEL
D_CONV = D_MIX // 2
CONV_WIDTH = 31
N_HEADS = 8
HEAD_DIM = 64
D_ATTN = N_HEADS * HEAD_DIM
N_IDX_HEADS = 8
IDX_DIM = 64
TOPK_MAX = 256
Q_BLOCK = 64
POS_BLOCK = 128
LN_EPS = 1e-5
IDX_SCALE = IDX_DIM ** -0.5
IDX_W_SCALE = N_IDX_HEADS ** -0.5
DEEPNORM_ALPHA = (2.0 * DEPTH_2) ** 0.25
DEEPNORM_BETA = (8.0 * DEPTH_2) ** -0.25

IN_SIZES_2 = [D_CONV, D_CONV, D_CONV, D_ATTN, D_ATTN, D_ATTN, D_ATTN,
            N_IDX_HEADS * IDX_DIM, IDX_DIM, N_IDX_HEADS]
D_IN = sum(IN_SIZES_2)
IN_SPLITS = [sum(IN_SIZES_2[:i + 1]) for i in range(len(IN_SIZES_2) - 1)]


def layer_norm(x, g, b):
    xf = x.astype(jnp.float32)
    mu = jnp.mean(xf, axis=-1, keepdims=True)
    var = jnp.mean(jnp.square(xf - mu), axis=-1, keepdims=True)
    y = (xf - mu) * lax.rsqrt(var + LN_EPS) * g.astype(jnp.float32) + b.astype(jnp.float32)
    return y.astype(x.dtype)

def rope_tables_2(length, dim):
    inv_freq = ROPE_THETA ** (-jnp.arange(0, dim, 2, dtype=jnp.float32) / dim)
    ang = jnp.arange(length, dtype=jnp.float32)[:, None] * inv_freq[None, :]
    return jnp.cos(ang), jnp.sin(ang)

def apply_rope_2(x, cos, sin):
    half = x.shape[-1] // 2
    x1, x2 = x[..., :half], x[..., half:]
    out = jnp.concatenate([x1 * cos - x2 * sin, x2 * cos + x1 * sin], axis=-1)
    return out.astype(x.dtype)

def conformer_conv_branch(a, g, z, w_dw, b_dw, ln_g, ln_b):
    u = a * jax.nn.sigmoid(g)
    u = lax.conv_general_dilated(
        u, w_dw[:, None, :].astype(u.dtype), window_strides=(1,),
        padding=[(CONV_WIDTH - 1, 0)],
        dimension_numbers=('NWC', 'WIO', 'NWC'),
        feature_group_count=D_CONV) + b_dw
    u = jax.nn.silu(layer_norm(u, ln_g, ln_b))
    return u * jax.nn.silu(z)

def dsa_sparse_attention(q, k, v, qi, ki, wi, topk):
    B, L = q.shape[0], q.shape[1]
    nb = L // Q_BLOCK
    key_pos = jnp.arange(L)
    ki32 = ki.astype(jnp.float32)

    def to_blocks(t):
        return jnp.moveaxis(t.reshape((B, nb, Q_BLOCK) + t.shape[2:]), 1, 0)

    def one_block(args):
        qb, qib, wib, start = args
        q_pos = start + jnp.arange(Q_BLOCK)
        causal = key_pos[None, :] <= q_pos[:, None]
        logits = jnp.einsum('bqhd,bsd->bqhs', qib.astype(jnp.float32), ki32) * IDX_SCALE
        score = jnp.einsum('bqhs,bqh->bqs', jax.nn.relu(logits),
                           wib.astype(jnp.float32) * IDX_W_SCALE)
        score = jnp.where(causal[None], score, -jnp.inf)
        _, idx = lax.top_k(score, topk)
        valid = idx <= q_pos[None, :, None]
        kg = jax.vmap(lambda kk, ii: kk[ii])(k, idx)
        vg = jax.vmap(lambda vv, ii: vv[ii])(v, idx)
        s = jnp.einsum('bqhd,bqkhd->bqhk', qb, kg).astype(jnp.float32) * (HEAD_DIM ** -0.5)
        s = jnp.where(valid[:, :, None, :], s, -jnp.inf)
        p = jax.nn.softmax(s, axis=-1).astype(v.dtype)
        return jnp.einsum('bqhk,bqkhd->bqhd', p, vg)

    starts = jnp.arange(nb) * Q_BLOCK
    out = lax.map(one_block, (to_blocks(q), to_blocks(qi), to_blocks(wi), starts))
    return jnp.moveaxis(out, 0, 1).reshape(B, L, D_ATTN)

def second_inputs(seed: int = 0) -> dict:
    key = jax.random.key(seed)
    ks = jax.random.split(key, 10)
    f32 = jnp.float32
    x = jax.random.normal(ks[0], (BATCH, SEQ, D_MODEL), f32)
    meta_tokens = jax.random.normal(ks[1], (N_META, D_MODEL), f32)
    w_in = jax.random.normal(ks[2], (DEPTH_2, D_MODEL, D_IN), f32) * D_MODEL ** -0.5
    conv_w = jax.random.normal(ks[3], (DEPTH_2, CONV_WIDTH, D_CONV), f32) * CONV_WIDTH ** -0.5
    conv_b = 0.01 * jax.random.normal(ks[4], (DEPTH_2, D_CONV), f32)
    conv_ln_g = 1.0 + 0.01 * jax.random.normal(ks[5], (DEPTH_2, D_CONV), f32)
    conv_ln_b = 0.01 * jax.random.normal(ks[6], (DEPTH_2, D_CONV), f32)
    w_out = jax.random.normal(ks[7], (DEPTH_2, D_MIX, D_MODEL), f32) * (D_MIX ** -0.5) * DEEPNORM_BETA
    post_ln_g = 1.0 + 0.01 * jax.random.normal(ks[8], (DEPTH_2, D_MODEL), f32)
    post_ln_b = 0.01 * jax.random.normal(ks[9], (DEPTH_2, D_MODEL), f32)
    return {"x": x, "meta_tokens": meta_tokens, "w_in": w_in, "conv_w": conv_w,
            "conv_b": conv_b, "conv_ln_g": conv_ln_g, "conv_ln_b": conv_ln_b,
            "w_out": w_out, "post_ln_g": post_ln_g, "post_ln_b": post_ln_b}

def second_block(x, meta_tokens, w_in, conv_w, conv_b, conv_ln_g, conv_ln_b, w_out,
              post_ln_g, post_ln_b):
    B, S, D = x.shape
    L = S + N_META
    topk = min(TOPK_MAX, L // 4)
    Lp = -(-L // POS_BLOCK) * POS_BLOCK
    meta = jnp.broadcast_to(meta_tokens[None].astype(x.dtype), (B, N_META, D))
    h = jnp.concatenate([meta, x, jnp.zeros((B, Lp - L, D), x.dtype)], axis=1)
    cos, sin = rope_tables_2(Lp, HEAD_DIM)
    cos_h, sin_h = cos[:, None, :], sin[:, None, :]

    for l in range(DEPTH_2):
        proj = jnp.einsum('bld,de->ble', h, w_in[l])
        a, g, zc, q, k, v, za, qi, ki, wi = jnp.split(proj, IN_SPLITS, axis=-1)
        y_conv = conformer_conv_branch(a, g, zc, conv_w[l], conv_b[l], conv_ln_g[l], conv_ln_b[l])
        q = apply_rope_2(q.reshape(B, Lp, N_HEADS, HEAD_DIM), cos_h, sin_h)
        k = apply_rope_2(k.reshape(B, Lp, N_HEADS, HEAD_DIM), cos_h, sin_h)
        v = v.reshape(B, Lp, N_HEADS, HEAD_DIM)
        qi = apply_rope_2(qi.reshape(B, Lp, N_IDX_HEADS, IDX_DIM), cos_h, sin_h)
        ki = apply_rope_2(ki, cos, sin)
        y_attn = dsa_sparse_attention(q, k, v, qi, ki, wi, topk) * jax.nn.silu(za)
        y = jnp.einsum('ble,ed->bld', jnp.concatenate([y_conv, y_attn], axis=-1), w_out[l])
        h = layer_norm(DEEPNORM_ALPHA * h + y, post_ln_g[l], post_ln_b[l])

    return h[:, N_META:L]


def setup_inputs(seed=0):
    out = dict(first_inputs(seed))
    for name, value in second_inputs(seed + 1).items():
        if name != "x":
            out[name + "_2"] = value
    return out


def reference(
    x, meta_tokens, w_in, b_gate, lb_logits, hg_norm_g, w_hg_o, q_a_norm_g, w_q_b, kv_a_norm_g,
    w_kv_b, w_mla_o, w_out, mix_pre_g, mix_post_g, ffn_pre_g, ffn_post_g, w_ffn_in, w_ffn_out,
    meta_tokens_2, w_in_2, conv_w_2, conv_b_2, conv_ln_g_2, conv_ln_b_2, w_out_2, post_ln_g_2,
    post_ln_b_2,
):
    x = first_block(
        x, meta_tokens, w_in, b_gate, lb_logits, hg_norm_g, w_hg_o, q_a_norm_g, w_q_b,
        kv_a_norm_g, w_kv_b, w_mla_o, w_out, mix_pre_g, mix_post_g, ffn_pre_g, ffn_post_g,
        w_ffn_in, w_ffn_out,
    )
    return second_block(
        x, meta_tokens_2, w_in_2, conv_w_2, conv_b_2, conv_ln_g_2, conv_ln_b_2, w_out_2,
        post_ln_g_2, post_ln_b_2,
    )


_drawn_inputs = setup_inputs


def setup_inputs(seed=0):
    import zlib

    import numpy as np

    out = dict(_drawn_inputs(seed))
    spreads = {}
    factors = {'b_gate': 6.228,
     'lb_logits': 2.87,
     'q_a_norm_g': 4.014,
     'kv_a_norm_g': 3.595,
     'ffn_post_g': 2.691,
     'conv_b_2': 8.0,
     'conv_ln_g_2': 8.0,
     'conv_ln_b_2': 8.0,
     'post_ln_g_2': 3.706,
     'post_ln_b_2': 4.009}
    for name, (base, spread) in spreads.items():
        noise = np.random.default_rng([zlib.crc32(name.encode()), seed]).standard_normal(out[name].shape)
        drawn = base * np.exp(spread * noise) if base else spread * noise
        out[name] = __import__('jax').numpy.asarray(drawn.astype(out[name].dtype))
    for name, factor in factors.items():
        out[name] = (out[name] * factor).astype(out[name].dtype)
    return out
```

```python
from contextlib import ExitStack

import numpy as np

import concourse.bass as bass
from concourse import mybir

F32 = mybir.dt.float32
U32 = mybir.dt.uint32
ALU = mybir.AluOpType
ACT = mybir.ActivationFunctionType

P = 128
META = 16
SEQ = 256
L = META + SEQ
D = 1024
DC = D // P
HEADS = 8
EPS_RMS = 1e-6
EPS_LN = 1e-5
NEG = -3.0e38
BIG = 3.0e38

LORA = 256
NOPE, ROPE, VDIM = 128, 64, 128
MLA_SCALE = float(NOPE + ROPE) ** -0.5
FFN = 2816
FC = FFN // P
FFN_ITEMS = FFN // 256
LEVELS = 7
GATE_COL = 4 * D + 2 * LORA + ROPE

DEPTH2 = 2
CONV_C = 512
CC = CONV_C // P
TAPS = 31
HD = 64
TOPK = min(256, L // 4)
ROUNDS = -(-TOPK // 8)
IDX_SCALE = float(HD) ** -0.5
IDX_W_SCALE = float(HEADS) ** -0.5
ATT_SCALE = float(HD) ** -0.5
ALPHA = (2.0 * DEPTH2) ** 0.25
COL2 = dict(a=0, g=512, zc=1024, q=1536, k=2048, v=2560, za=3072, qi=3584, ki=4096)

KEY_CHUNKS = [(0, 128), (128, 128), (256, 16)]

CONST = {}
_at = 0
for _name, _n in (("ident", P), ("rot", P), ("cos", L), ("sin", L), ("level", (LEVELS + 1) * P),
                  ("causal_m", META), ("causal_0", META + P), ("causal_1", L)):
    CONST[_name] = (_at, _n)
    _at += _n
N_CONST = _at


def shape_constants():
    c = np.zeros((P, N_CONST), np.float32)

    def put(name, a):
        at, n = CONST[name]
        c[:a.shape[0], at:at + n] = a

    put("ident", np.eye(P, dtype=np.float32))
    rot = np.zeros((P, P), np.float32)
    for m in range(P):
        if m % 64 < 32:
            rot[m + 32, m] = -1.0
        else:
            rot[m - 32, m] = 1.0
    put("rot", rot)
    inv = (1.0 / (np.float32(10000.0) ** (np.arange(0, 64, 2, dtype=np.float32) / np.float32(64)))).astype(np.float32)
    ang = np.arange(L, dtype=np.float32)[None, :] * inv[np.arange(P) % 32][:, None]
    put("cos", np.cos(ang).astype(np.float32))
    put("sin", np.sin(ang).astype(np.float32))
    s, t = np.arange(P)[:, None], np.arange(P)[None, :]
    masks = [s == t]
    for lv in range(LEVELS):
        b = 1 << lv
        masks.append((s // (2 * b) == t // (2 * b)) & (s // b % 2 == 0) & (t // b % 2 == 1))
    put("level", np.concatenate(masks, 1).astype(np.float32))
    for name, first, rows in (("causal_m", 0, META), ("causal_0", META, P), ("causal_1", META + P, P)):
        n = CONST[name][1]
        put(name, np.where(np.arange(n)[None, :] <= first + np.arange(rows)[:, None], 0.0, NEG).astype(np.float32))
    return c


VEC_LIST = [("mix_pre_g", 8), ("mix_post_g", 8), ("ffn_pre_g", 8), ("ffn_post_g", 8), ("b_gate", 16),
            ("lb_logits", 16), ("hg_norm_g", 1), ("q_a_norm_g", 2), ("kv_a_norm_g", 2),
            ("conv_b_2", 8), ("conv_ln_g_2", 8), ("conv_ln_b_2", 8), ("post_ln_g_2", 16), ("post_ln_b_2", 16)]
VEC = {}
_at = 0
for _name, _n in VEC_LIST:
    VEC[_name] = _at
    _at += _n
N_VEC = _at
TAP_COL = [N_VEC, N_VEC + TAPS * CC]
N_COLS = N_VEC + 2 * TAPS * CC

STREAM = ([("c", 4), ("kpe", 1), ("wqb", 12), ("wkvb", 14)]
          + [(f"hg{i}", 4) for i in range(8)] + [(f"gate{i}", 4) for i in range(4)]
          + [(f"hgo{i}", 4) for i in range(2)] + [(f"mlo{i}", 4) for i in range(2)]
          + [(f"mix{i}", 4) for i in range(2)] + [None, None]
          + [(f"ffi{i}", 4) for i in range(FFN_ITEMS)] + [None]
          + [(f"ffo{i}", 1) for i in range(DC)])
for _l in range(DEPTH2):
    STREAM += [(f"L{_l}kw", 2), (f"L{_l}qi", 4), (f"L{_l}a", 4), (f"L{_l}g", 4), (f"L{_l}q", 4), (f"L{_l}k", 4),
               (f"L{_l}v", 3), (f"L{_l}zc", 4), (f"L{_l}za", 4), (f"L{_l}wo0", 4), (f"L{_l}wo1", 4), None]
SLOTS = 4
EXTRA = {"c": [("start", 12)], "hgo0": [("vT", 8), ("kT", 8), ("S", 8), ("o", 8)], "end": [("out", 4)]}
ITEM, CHUNK, USE, PREV = {}, {}, {}, {}
_g, _uses, _last = 0, [0] * SLOTS, [None] * SLOTS
for _i, _it in enumerate(STREAM + [("end", 0)]):
    if _it is None:
        continue
    for _n, _c in EXTRA.get(_it[0], []):
        CHUNK[_n] = _g
        _g += _c
    _s = _i % SLOTS
    ITEM[_it[0]], CHUNK[_it[0]] = _i, _g
    _uses[_s] += not _it[0].startswith("ffi")
    USE[_it[0]] = _uses[_s]
    PREV[_it[0]] = _last[_s]
    _g += _it[1]
    _last[_s] = _g


def bass_blocks(nc, a, out):
    ctx = ExitStack()
    with ctx:
        def sb(name, shape, dt=F32):
            return ctx.enter_context(nc.sbuf_tensor(name, shape, dt))

        sems = {}

        def sem(name):
            if name not in sems:
                sems[name] = ctx.enter_context(nc.semaphore(name))
            return sems[name]

        ring = sb("ring", [P, SLOTS, 4096])
        const = sb("const", [P, N_CONST])
        ones = sb("ones", [P, P])
        vec_rows = sb("vec_rows", [P, 3, P])
        cols = sb("cols", [P, N_COLS])
        small = sb("small", [P, 64])
        hT = sb("hT", [P, DC, L])
        uT = sb("uT", [P, DC, L])
        keep = sb("keep", [P, 2048])
        zoneA = sb("zoneA", [P, 10752])
        zoneB = sb("zoneB", [P, 13440])
        sq = sb("sq", [P, 2, L])
        nrm = sb("nrm", [P, 2, L])

        class Zone:
            def __init__(self, t, at=0):
                self.t, self.at = t, at

            def __call__(self, *shape):
                n = int(np.prod(shape))
                v = self.t[:, self.at:self.at + n]
                self.at += n
                if len(shape) == 2:
                    v = v.rearrange("p (a b) -> p a b", b=shape[1])
                if len(shape) == 3:
                    v = v.rearrange("p (a b c) -> p a b c", b=shape[1], c=shape[2])
                return v

        PS = ctx.enter_context(nc.psum_tensor("PS", [P, 8, 512], F32))

        def cst(name, rows=P):
            at, n = CONST[name]
            return const[0:rows, at:at + n]

        ident, rotm, cosT, sinT = cst("ident"), cst("rot"), cst("cos"), cst("sin")

        def vec(name, c):
            return cols[:, VEC[name] + c:VEC[name] + c + 1]

        eps_rms, eps_ln = small[:, 0:1], small[:, 1:2]
        lb, oml = small[:, 8:16], small[:, 16:24]
        lb_e0, lb_e1, lb_m = small[:, 24:32], small[:, 32:40], small[:, 40:48]

        z = Zone(zoneA)
        hq, hk, hf, hi = z(HEADS, L), z(HEADS, L), z(HEADS, L), z(HEADS, L)
        hg = z(HEADS, SEQ)
        scoresT = Zone(zoneA, 3 * HEADS * L)(HEADS * 2, P)
        flat = {n: v.rearrange("p h t -> p (h t)") for n, v in (("q", hq), ("k", hk), ("f", hf))}
        z = Zone(zoneB)
        c_raw, c_nrm = z(4, L), z(4, L)
        qn, qpe, qpr = z(HEADS, SEQ), z(4, SEQ), z(4, SEQ)
        kn, kpe, kpr = z(HEADS, L), z(L), z(L)
        vM = z(3, HEADS * VDIM)
        att_s, att_p, att_r = z(2, L), z(2, L), z(2, 2)
        rope_a, rope_b = att_s, att_p
        att_pt = Zone(zoneB)(2, 3 * P)
        assert z.at <= 13440
        z = Zone(zoneB)
        tree = z(HEADS * L)
        v_tok, v_meta = z(2, HEADS * P), z(HEADS * P)
        S1, S2 = z(HEADS, P), z(HEADS, P)
        kT_tok, kT_meta = z(HEADS, P), z(HEADS, P)
        o_h = Zone(zoneB, z.at - 2 * HEADS * P)(HEADS, SEQ)
        gates = z(2 * DC, SEQ)
        assert z.at <= 13440
        o_mla = keep[:, :].rearrange("p (h t) -> p h t", h=HEADS)
        z = Zone(zoneA)
        ya, yb = z(DC, SEQ), z(DC, SEQ)
        y_hg, mixed = z(HEADS, SEQ), z(DC, SEQ)
        z = Zone(zoneB)
        hid = z(FC, SEQ)
        up = z(2, SEQ)
        ffo = z(DC, SEQ)
        z = Zone(zoneA)
        kiT, kir, qiT, qir = z(L), z(L), z(4, L), z(4, L)
        idx_w = z(2, 8)
        upad, gsig = z(CC, TAPS - 1 + L), z(CC, L)
        acc = z(CC, L)
        q2, k2 = z(4, L), z(4, L)
        assert z.at <= 10752
        z = Zone(zoneB)
        q2r, k2r = z(4, L), z(4, L)
        v2 = z(3, HEADS * HD)
        szc, sza = z(CC, L), z(CC, L)
        relu = z(2, L)
        score = z(2, L)
        sel = z(2, L)
        top8 = z(2, 8)
        at2_s, at2_p, at2_pt, at2_r = z(2, L), z(2, L), z(2, 3 * P), z(2, 2)
        rope2_a, rope2_b = z(2, L), z(2, L)
        ycat = z(DC, L)
        zT = uT
        assert z.at <= 13440, z.at
        out_tok = zoneA[:, 0:2 * D].rearrange("p (t d) -> p t d", t=2)
        x_tok = zoneA[:, 0:2 * D].rearrange("p (t d) -> p t d", t=2)
        m_tok = zoneA[:, 2 * D:4 * D].rearrange("p (t d) -> p t d", t=2)

        def slot(name):
            return ring[:, ITEM[name] % SLOTS, :]

        def w_ready(eng, name):
            eng.wait_ge(sem(f"slot{ITEM[name] % SLOTS}_full"), 16 * USE[name])

        Q_TILES = [(META, P, META + P), (META + P, P, L)]
        MLA_STEPS = [(h, *t) for h in range(HEADS) for t in Q_TILES]
        DSA_STEPS = [[(h, *t) for h in range(HEADS) for t in ([(0, META, META)] if l == 0 else []) + Q_TILES]
                     for l in range(DEPTH2)]
        CAUSAL = {0: "causal_m", META: "causal_0", META + P: "causal_1"}

        block = ctx.enter_context(nc.Block())

        @block.sync
        def _(sp):
            sp.dma_start(const[:, :], a["constants"]).then_inc(sem("const_in"), 16)
            x2 = a["x"][0].rearrange("(t p) d -> p t d", p=P)
            sp.dma_start(x_tok, x2).then_inc(sem("x_in"), 16)
            sp.dma_start(m_tok[0:META, 0, :], a["meta_tokens"]).then_inc(sem("x_in"), 16)
            sp.dma_start(m_tok[0:META, 1, :], a["meta_tokens_2"]).then_inc(sem("x_in"), 16)

            def free(name):
                if PREV[name] is not None:
                    sp.wait_ge(sem("chunk_done"), PREV[name])

            def full(name, ins):
                ins.then_inc(sem(f"slot{ITEM[name] % SLOTS}_full"), 16)

            def kview(w):
                return w.rearrange("(k p) n -> p k n", p=P)

            def load(name, w, n):
                k = w.shape[1]
                free(name)
                full(name, sp.dma_start(slot(name)[:, 0:k * n].rearrange("p (k n) -> p k n", k=k), w))

            w_in = kview(a["w_in"][0])
            load("c", w_in[:, :, 4 * D:4 * D + 512], 512)
            load("kpe", w_in[:, :, 4 * D + 512:4 * D + 576], ROPE)
            load("wqb", kview(a["w_q_b"][0]), 1536)
            load("wkvb", kview(a["w_kv_b"][0]), 2048)

            def load_loop(first, count, src):
                assert ITEM[first] % SLOTS == 0 and count % SLOTS == 0
                with sp.Fori(0, count // SLOTS) as it:
                    for s in range(SLOTS):
                        sp.wait_ge(sem("chunk_done"), PREV_AT[first][s][0] + it * PREV_AT[first][s][1])
                        sp.dma_start(ring[:, s, :].rearrange("p (k n) -> p k n", k=DC),
                                     src(it * SLOTS + s)).then_inc(sem(f"slot{s}_full"), 16)

            for i in range(8):
                load(f"hg{i}", w_in[:, :, i * 512:(i + 1) * 512], 512)
            for i in range(4):
                load(f"gate{i}", w_in[:, :, GATE_COL + i * 512:GATE_COL + (i + 1) * 512], 512)
            for n, w in (("hgo", "w_hg_o"), ("mlo", "w_mla_o"), ("mix", "w_out")):
                for i in range(2):
                    load(f"{n}{i}", kview(a[w][0])[:, :, i * 512:(i + 1) * 512], 512)
            w_fi = a["w_ffn_in"][0].rearrange("(k p) (u n) -> p k u n", p=P, u=2)
            for i in range(FFN_ITEMS):
                free(f"ffi{i}")
                for u in range(2):
                    dst = slot(f"ffi{i}").rearrange("p (k u n) -> p k u n", k=DC, u=2)[:, :, u, :]
                    sp.dma_start(dst, w_fi[:, :, u, i * 256:(i + 1) * 256])\
                        .then_inc(sem(f"ffn{u}_slot{ITEM[f'ffi{i}'] % SLOTS}"), 16)
            for i in range(DC):
                load(f"ffo{i}", kview(a["w_ffn_out"][0])[:, :, i * P:(i + 1) * P], P)
            for l in range(DEPTH2):
                w2 = kview(a["w_in_2"][l])
                load(f"L{l}kw", w2[:, :, COL2["ki"]:COL2["ki"] + HD + HEADS], HD + HEADS)
                for n in ("qi", "a", "g", "q", "k", "v", "zc", "za"):
                    load(f"L{l}{n}", w2[:, :, COL2[n]:COL2[n] + 512], 512)
                for i in range(2):
                    load(f"L{l}wo{i}", kview(a["w_out_2"][l])[:, :, i * 512:(i + 1) * 512], 512)
            for t in range(2):
                sp.wait_ge(sem("chunk_out"), CHUNK["out"] + 2 * t + 2)
                sp.dma_start(out[0, t * P:(t + 1) * P, :], out_tok[:, t, :]).then_inc(sem("stored"), 16)
            sp.wait_ge(sem("stored"), 32)

        @block.tensor
        def _(pe):
            mm = nc.tensor.matmul

            def bank_free(g):
                if g >= 2:
                    pe.wait_ge(sem("chunk_out"), g - 1)

            def done(ins):
                ins.then_inc(sem("chunk_done"), 1)

            def linear(g, lhs, rhs, n, k=DC, rows=P):
                bank_free(g)
                for i in range(k):
                    last = mm(PS[0:rows, g % 2, 0:n], lhs(i), rhs(i), start=(i == 0), stop=(i == k - 1))
                done(last)

            def item_cols(name, n=512, k=DC):
                w = slot(name)[:, 0:k * n].rearrange("p (k n) -> p k n", k=k)
                return lambda c0, nc_=P: (lambda i: w[:, i, c0:c0 + nc_])

            def linear_item(name, src, c0=0, n=L, chunks=4):
                w_ready(pe, name)
                w = item_cols(name)
                for m in range(chunks):
                    linear(CHUNK[name] + m, w(m * P), src, n)

            def norm_step(tag, c, count, bank, n, first=0):
                pe.wait_ge(sem(f"sq_{tag}"), first + c + 1)
                mm(PS[:, bank, 0:n], ones[:, :], sq[:, (first + c) % 2, 0:n], start=(c == 0),
                   stop=(c == count - 1)).then_inc(sem(f"sum_{tag}"), 1)

            def norm_sum(tag, count, bank, n, first=0):
                for c in range(count):
                    norm_step(tag, c, count, bank, n, first)

            def linear_norm(tag, chunks, n):
                for c, chunk in enumerate(chunks):
                    chunk()
                    if c:
                        norm_step(tag, c - 1, len(chunks), 2, n)
                norm_step(tag, len(chunks) - 1, len(chunks), 2, n)

            u = lambda k: uT[:, k, :]
            u_real = lambda k: uT[:, k, META:L]

            pe.wait_ge(sem("const_in"), 16)
            pe.wait_ge(sem("x_in"), 48)
            g = CHUNK["start"]
            for c in range(DC):
                bank_free(g)
                b = PS[:, g % 2, :]
                nc.tensor.transpose(b[:, 0:META], m_tok[0:META, 0, c * P:(c + 1) * P], ident[0:META, 0:META])
                for t in range(2):
                    last = nc.tensor.transpose(b[:, META + t * P:META + (t + 1) * P],
                                               x_tok[:, t, c * P:(c + 1) * P], ident)
                done(last)
                g += 1
            pe.wait_ge(sem("vec_in"), 16 * (len(VEC_LIST) + 2))
            for j, n in enumerate((N_VEC, TAPS * CC, TAPS * CC)):
                bank_free(g)
                done(nc.tensor.transpose(PS[:, g % 2, 0:n], vec_rows[0:n, j, :], ident[0:n, 0:n]))
                g += 1
            bank_free(g)
            for c in range(DC):
                last = nc.tensor.transpose(PS[:, g % 2, c * META:(c + 1) * META],
                                           m_tok[0:META, 1, c * P:(c + 1) * P], ident[0:META, 0:META])
            done(last)

            pe.wait_ge(sem("ones"), 1)
            norm_sum("pre", DC, 2, L)
            pe.wait_ge(sem("u_pre"), DC)

            linear_item("c", u)
            w_ready(pe, "kpe")
            w = item_cols("kpe", ROPE)
            for half in range(2):
                if half == 0:
                    bank_free(CHUNK["kpe"])
                for i in range(DC):
                    last = mm(PS[half * 64:half * 64 + 64, CHUNK["kpe"] % 2, 0:L], w(0, ROPE)(i), u(i),
                              start=(i == 0), stop=(i == DC - 1))
            done(last)
            norm_sum("cq", 2, 2, L)
            norm_sum("ckv", 2, 3, L)
            pe.wait_ge(sem("c_nrm"), 4)
            w_ready(pe, "wqb")
            wq = slot("wqb")[:, 0:2 * 1536].rearrange("p (k h c) -> p k h c", k=2, h=HEADS)
            g = CHUNK["wqb"]
            for h in range(HEADS):
                linear(g, lambda i: wq[:, i, h, 0:NOPE], lambda i: c_nrm[:, i, META:L], SEQ, k=2)
                g += 1
            for hp in range(HEADS // 2):
                bank_free(g)
                for half in range(2):
                    for i in range(2):
                        last = mm(PS[half * 64:half * 64 + 64, g % 2, 0:SEQ], wq[:, i, 2 * hp + half, NOPE:NOPE + ROPE],
                                  c_nrm[:, i, META:L], start=(i == 0), stop=(i == 1))
                done(last)
                g += 1
            w_ready(pe, "wkvb")
            wkv = slot("wkvb").rearrange("p (k h c) -> p k h c", k=2, h=HEADS)
            g = CHUNK["wkvb"]
            for h in range(HEADS):
                linear(g, lambda i: wkv[:, i, h, 0:NOPE], lambda i: c_nrm[:, 2 + i, :], L, k=2)
                g += 1
            for t0, n in KEY_CHUNKS:
                for half in range(2):
                    linear(g, lambda i: c_nrm[:, 2 + i, t0:t0 + n],
                           lambda i: wkv[:, i, 4 * half:4 * half + 4, NOPE:NOPE + VDIM], 4 * VDIM, k=2, rows=n)
                    g += 1

            def rope(tag, i, src):
                if i >= 2:
                    pe.wait_ge(sem(f"{tag}_rope_out"), i - 1)
                mm(PS[:, 6 + i % 2, 0:src.shape[1]], rotm, src, start=True, stop=True)\
                    .then_inc(sem(f"{tag}_rope"), 1)

            pe.wait_ge(sem("chunk_out"), CHUNK["wkvb"])
            for i in range(5):
                rope("mla", i, qpe[:, i, :] if i < 4 else kpe[:, :])

            def attention(tag, steps, s_mm, v_of, p_buf, pt_buf, o_rows):
                n = len(steps)
                for i in range(n + 2):
                    if i < n:
                        if i >= 2:
                            pe.wait_ge(sem(f"{tag}_masked"), i - 1)
                        s_mm(steps[i], PS[:, 2 + i % 2, :]).then_inc(sem(f"{tag}_scores"), 1)
                    j = i - 1
                    if 0 <= j < n:
                        h, q0, nq, nk = steps[j]
                        pe.wait_ge(sem(f"{tag}_probs"), j + 1)
                        if j >= 2:
                            pe.wait_ge(sem(f"{tag}_pt_out"), j - 1)
                        for x, (k0, kn_) in enumerate(KEY_CHUNKS):
                            m = min(kn_, nk - k0)
                            if m > 0:
                                last = nc.tensor.transpose(PS[0:m, 4 + j % 2, x * P:x * P + nq],
                                                           p_buf[0:nq, j % 2, k0:k0 + m], ident[0:nq, 0:nq])
                        last.then_inc(sem(f"{tag}_pt"), 1)
                    j = i - 2
                    if 0 <= j < n:
                        h, q0, nq, nk = steps[j]
                        pe.wait_ge(sem(f"{tag}_pt_out"), j + 1)
                        if j >= 2:
                            pe.wait_ge(sem(f"{tag}_o_out"), j - 1)
                        rows = o_rows(h)
                        used = [(x, min(kn_, nk - k0)) for x, (k0, kn_) in enumerate(KEY_CHUNKS) if nk > k0]
                        for x, m in used:
                            last = mm(PS[rows, 6 + j % 2, 0:nq], v_of(h, x, m), pt_buf[0:m, j % 2, x * P:x * P + nq],
                                      start=(x == 0), stop=(x == used[-1][0]))
                        last.then_inc(sem(f"{tag}_o"), 1)

            def mla_scores(step, b):
                h, q0, nq, nk = step
                r = slice(64 * (h % 2), 64 * (h % 2) + 64)
                mm(b[:, 0:nk], qn[:, h, q0 - META:q0 - META + nq], kn[:, h, 0:nk], start=True, stop=False)
                return mm(b[:, 0:nk], qpr[r, h // 2, q0 - META:q0 - META + nq], kpr[r, 0:nk], start=False, stop=True)

            pe.wait_ge(sem("mla_roped"), 5)
            pe.wait_ge(sem("chunk_out"), CHUNK["hg0"])
            attention("mla", MLA_STEPS, mla_scores, lambda h, x, m: vM[0:m, x, h * VDIM:(h + 1) * VDIM],
                      att_p, att_pt, lambda h: slice(0, P))

            for i in range(8):
                linear_item(f"hg{i}", u)
            for i in range(4):
                linear_item(f"gate{i}", u_real, n=SEQ)

            pe.wait_ge(sem("chunk_out"), CHUNK["gate0"])
            for h in range(HEADS):
                g = CHUNK["vT"] + h
                bank_free(g)
                b = PS[:, g % 2, :]
                for t in range(2):
                    nc.tensor.transpose(b[:, t * P:(t + 1) * P], hi[:, h, META + t * P:META + (t + 1) * P], ident)
                done(nc.tensor.transpose(b[0:META, 2 * P:3 * P], hi[:, h, 0:META], ident))
            for lv in range(LEVELS + 1):
                for half in range(2):
                    pe.wait_ge(sem("level_ready"), 2 * lv + half + 1)
                    for b in range(2):
                        if lv:
                            pe.wait_ge(sem("level_masked"), 4 * (lv - 1) + 2 * half + b + 1)
                        for j in range(4):
                            h, t = divmod(8 * half + 4 * b + j, 2)
                            tok = slice(META + t * P, META + (t + 1) * P)
                            last = mm(PS[:, 2 + 2 * half + b, j * P:(j + 1) * P], hk[:, h, tok], hq[:, h, tok],
                                      start=True, stop=True)
                        last.then_inc(sem("level_done"), 1)
            pe.wait_ge(sem("level_ready"), 2 * LEVELS + 4)
            for h in range(HEADS):
                g = CHUNK["kT"] + h
                bank_free(g)
                nc.tensor.transpose(PS[:, g % 2, 0:P], hk[:, h, META:META + P], ident)
                done(nc.tensor.transpose(PS[0:META, g % 2, P:2 * P], hk[:, h, 0:META], ident))
            for h in range(HEADS):
                g = CHUNK["S"] + h
                bank_free(g)
                pe.wait_ge(sem("chunk_out"), CHUNK["kT"] + h + 1)
                mm(PS[:, g % 2, 0:P], kT_meta[0:META, h, :], v_meta[0:META, h * P:(h + 1) * P], start=True, stop=True)
                done(mm(PS[:, g % 2, P:2 * P], kT_tok[:, h, :], v_tok[:, 0, h * P:(h + 1) * P], start=True, stop=True))
            for h in range(HEADS):
                g = CHUNK["o"] + h
                bank_free(g)
                pe.wait_ge(sem("state"), h + 1)
                for t in range(2):
                    b = PS[:, g % 2, t * P:(t + 1) * P]
                    mm(b, v_tok[:, t, h * P:(h + 1) * P], scoresT[:, 2 * h + t, :], start=True, stop=False)
                    last = mm(b, (S1, S2)[t][:, h, :], hq[:, h, META + t * P:META + (t + 1) * P], start=False, stop=True)
                done(last)
            for h in range(HEADS):
                if h >= 2:
                    pe.wait_ge(sem("std_hg"), h - 1)
                norm_sum("hg", 1, 2 + h % 2, SEQ, first=h)

            pe.wait_ge(sem("y_hg"), HEADS)
            for i in range(2):
                linear_item(f"hgo{i}", lambda k: y_hg[:, k, :], n=SEQ)
            for i in range(2):
                linear_item(f"mlo{i}", lambda k: o_mla[:, k, :], n=SEQ)
            pe.wait_ge(sem("mixed"), DC)

            def mix_chunk(c):
                name, m = f"mix{c // 4}", c % 4
                if m == 0:
                    w_ready(pe, name)
                linear(CHUNK[name] + m, item_cols(name)(m * P), lambda k: ya[:, k, :], SEQ)

            linear_norm("post", [lambda c=c: mix_chunk(c) for c in range(DC)], SEQ)
            norm_sum("fpre", DC, 3, SEQ)

            pe.wait_ge(sem("u_fpre"), DC)
            for i in range(FFN_ITEMS):
                n = f"ffi{i}"
                w = item_cols(n)
                for m in range(4):
                    j, part = divmod(m, 2)
                    if j == 0:
                        use = sum(1 for x in range(i + 1) if ITEM[f"ffi{x}"] % SLOTS == ITEM[n] % SLOTS)
                        pe.wait_ge(sem(f"ffn{part}_slot{ITEM[n] % SLOTS}"), 16 * use)
                    linear(CHUNK[n] + m, w(part * 256 + j * P), u_real, SEQ)
            pe.wait_ge(sem("hidden"), FC)

            def ffo_chunk(c):
                n = f"ffo{c}"
                w_ready(pe, n)
                w = slot(n)[:, 0:FC * P].rearrange("p (k n) -> p k n", k=FC)
                linear(CHUNK[n], lambda k: w[:, k, :], lambda k: hid[:, k, :], SEQ, k=FC)

            linear_norm("fpost", [lambda c=c: ffo_chunk(c) for c in range(DC)], SEQ)

            h_in = lambda k: hT[:, k, :]
            for l in range(DEPTH2):
                T = f"L{l}"
                q_from = 0 if l == 0 else META
                pe.wait_ge(sem("h_post" if l else "h_ready"), DC)
                w_ready(pe, f"{T}kw")
                w = item_cols(f"{T}kw", HD + HEADS)
                g = CHUNK[f"{T}kw"]
                bank_free(g)
                for half in range(2):
                    for i in range(DC):
                        last = mm(PS[half * 64:half * 64 + 64, g % 2, 0:L], w(0, HD)(i), h_in(i),
                                  start=(i == 0), stop=(i == DC - 1))
                done(last)
                g += 1
                bank_free(g)
                for t in range(2):
                    for i in range(DC):
                        last = mm(PS[:, g % 2, 8 * t:8 * t + 8], hT[:, i, META + t * P:META + (t + 1) * P],
                                  w(HD, HEADS)(i), start=(i == 0), stop=(i == DC - 1))
                done(last)
                linear_item(f"{T}qi", h_in)
                pe.wait_ge(sem("chunk_out"), CHUNK[f"{T}a"])
                for i in range(5):
                    rope(f"{T}i", i, qiT[:, i, :] if i < 4 else kiT[:, :])
                pe.wait_ge(sem(f"{T}i_roped"), 5)
                for s in range(16):
                    t, h = divmod(s, HEADS)
                    q0, nq, nk = Q_TILES[t]
                    r = slice(64 * (h % 2), 64 * (h % 2) + 64)
                    if s >= 2:
                        pe.wait_ge(sem(f"{T}relu"), s - 1)
                    mm(PS[:, 2 + s % 2, 0:nk], qir[r, h // 2, q0:q0 + nq], kir[r, 0:nk], start=True, stop=True)\
                        .then_inc(sem(f"{T}idx"), 1)
                for n in ("a", "g", "q", "k"):
                    linear_item(f"{T}{n}", h_in)
                w_ready(pe, f"{T}v")
                w = item_cols(f"{T}v")
                for x, (t0, n) in enumerate(KEY_CHUNKS):
                    linear(CHUNK[f"{T}v"] + x, lambda i: hT[:, i, t0:t0 + n], w(0, 512), 512, rows=n)
                linear_item(f"{T}zc", h_in)
                linear_item(f"{T}za", h_in)
                for i in range(8):
                    rope(f"{T}q", i, q2[:, i, :] if i < 4 else k2[:, i - 4, :])

                def dsa_scores(step, b):
                    h, q0, nq, nk = step
                    r = slice(64 * (h % 2), 64 * (h % 2) + 64)
                    return mm(b[0:nq, 0:nk], q2r[r, h // 2, q0:q0 + nq], k2r[r, h // 2, 0:nk], start=True, stop=True)

                pe.wait_ge(sem(f"{T}q_roped"), 8)
                attention(f"{T}att", DSA_STEPS[l], dsa_scores, lambda h, x, m: v2[0:m, x, h * HD:(h + 1) * HD],
                          at2_p, at2_pt, lambda h: slice(64 * (h % 2), 64 * (h % 2) + 64))

                def ln_sums(tag, count, bank, src, n, ready):
                    for c in range(count):
                        ready(c)
                        last = mm(PS[:, bank, 0:n], ones[:, :], src(c), start=(c == 0), stop=(c == count - 1))
                    last.then_inc(sem(f"{tag}_mean"), 1)
                    norm_sum(tag, count, bank + 1, n)

                ln_sums(f"{T}cln", CC, 2, lambda c: acc[:, c, q_from:L], L - q_from,
                        lambda c: pe.wait_ge(sem(f"{T}tap"), CC * (TAPS - 1) + c + 1))
                pe.wait_ge(sem(f"{T}y"), DC)
                for i in range(2):
                    linear_item(f"{T}wo{i}", lambda k: ycat[:, k, q_from:L], n=L - q_from)
                ln_sums(f"{T}pln", DC, 4, lambda c: zT[:, c, q_from:L], L - q_from,
                        lambda c: pe.wait_ge(sem(f"{T}pln_in"), c + 1))

            pe.wait_ge(sem("h_post"), DC * DEPTH2)
            for t in range(2):
                for half in range(2):
                    g = CHUNK["out"] + 2 * t + half
                    bank_free(g)
                    for c in range(4):
                        last = nc.tensor.transpose(PS[:, g % 2, c * P:(c + 1) * P],
                                                   hT[:, 4 * half + c, META + t * P:META + (t + 1) * P], ident)
                    done(last)

        @block.scalar
        def _(act):
            af = nc.scalar.activation

            at = 0
            for name, n in VEC_LIST:
                v = a[name]
                v = v.rearrange("a b -> (a b)") if len(v.shape) == 2 else v
                act.dma_start(vec_rows[at:at + n, 0, :], v.rearrange("(c p) -> c p", p=P)).then_inc(sem("vec_in"), 16)
                at += n
            for l in range(DEPTH2):
                act.dma_start(vec_rows[0:TAPS * CC, 1 + l, :],
                              a["conv_w_2"][l].rearrange("j (c p) -> (j c) p", p=P)).then_inc(sem("vec_in"), 16)

            def take(g, dst, src, f=ACT.Copy, count=True, **kw):
                act.wait_ge(sem("chunk_done"), g + 1)
                ins = af(dst, src, f, **kw)
                if count:
                    ins.then_inc(sem("chunk_out"), 1)

            def bank(g, rows=P, c0=0, n=L):
                return PS[0:rows, g % 2, c0:c0 + n]

            def squares(tag, c, src, wait, n):
                wait()
                if c >= 2:
                    act.wait_ge(sem(f"sum_{tag}"), c - 1)
                af(sq[:, c % 2, 0:n], src, ACT.Square).then_inc(sem(f"sq_{tag}"), 1)

            def std(tag, sums, bank_, n, dim, eps, dst, guard=None):
                act.wait_ge(sem(f"sum_{tag}"), sums)
                act.wait_ge(sem("small"), 1)
                if guard:
                    act.wait_ge(*guard)
                af(dst, PS[:, bank_, 0:n], ACT.Sqrt, bias=eps, scale=1.0 / dim).then_inc(sem(f"std_{tag}"), 1)

            g = CHUNK["start"]
            for c in range(DC):
                take(g, hT[:, c, :], bank(g))
                g += 1
            for at, n in ((0, N_VEC), (TAP_COL[0], TAPS * CC), (TAP_COL[1], TAPS * CC)):
                take(g, cols[:, at:at + n], bank(g, n=n))
                g += 1
            take(g, keep[:, 0:P], bank(g, n=P))
            meta2 = keep[:, 0:P].rearrange("p (c t) -> p c t", c=DC)
            act.wait_ge(sem("chunk_out"), g + 1)
            af(vec_rows[:, 0, :].rearrange("p (c t) -> p c t", c=DC), meta2, ACT.Copy).then_inc(sem("meta2"), 1)
            for c in range(DC):
                squares("pre", c, hT[:, c, :], lambda: None, L)
            std("pre", DC, 2, L, D, eps_rms, nrm[:, 0, :])
            act.wait_ge(sem("lb_shift"), 2)
            af(lb_e0, lb_e0, ACT.Exp).then_inc(sem("lb_exp"), 1)
            af(lb_e1, lb_e1, ACT.Exp).then_inc(sem("lb_exp"), 1)

            g = CHUNK["c"]
            for i in range(4):
                take(g + i, c_raw[:, i, :], bank(g + i))
            take(CHUNK["kpe"], kpe, bank(CHUNK["kpe"]))
            for tag, first in (("cq", 0), ("ckv", 2)):
                for c in range(2):
                    def ready():
                        act.wait_ge(sem("chunk_out"), CHUNK["c"] + first + c + 1)
                        if tag == "ckv":
                            act.wait_ge(sem("sum_cq"), 2)
                    squares(tag, c, c_raw[:, first + c, :], ready, L)
            std("cq", 2, 2, L, LORA, eps_rms, nrm[:, 0, :], guard=(sem("u_pre"), DC))
            std("ckv", 2, 3, L, LORA, eps_rms, nrm[:, 1, :])
            g = CHUNK["wqb"]
            for h in range(HEADS):
                take(g, qn[:, h, :], bank(g, n=SEQ))
                g += 1
            for i in range(4):
                take(g, qpe[:, i, :], bank(g, n=SEQ))
                g += 1
            for h in range(HEADS):
                take(g, kn[:, h, :], bank(g))
                g += 1
            for x, (t0, n) in enumerate(KEY_CHUNKS):
                for half in range(2):
                    take(g, vM[0:n, x, half * 512:half * 512 + 512], bank(g, rows=n, n=512))
                    g += 1

            def attention(tag, steps, s_buf, p_buf, pt_buf, r_buf, o_of, o_guard=None):
                n = len(steps)
                for i in range(n + 2):
                    if i < n:
                        h, q0, nq, nk = steps[i]
                        act.wait_ge(sem(f"{tag}_masked"), i + 1)
                        if i >= 2:
                            act.wait_ge(sem(f"{tag}_pt"), i - 1)
                        af(p_buf[0:nq, i % 2, 0:nk], s_buf[0:nq, i % 2, 0:nk], ACT.Exp, scale=-1.0,
                           bias=r_buf[0:nq, i % 2, 0:1], accum_out=r_buf[0:nq, i % 2, 1:2])\
                            .then_inc(sem(f"{tag}_exp"), 1)
                    j = i - 1
                    if 0 <= j < n:
                        h, q0, nq, nk = steps[j]
                        act.wait_ge(sem(f"{tag}_pt"), j + 1)
                        if j >= 2:
                            act.wait_ge(sem(f"{tag}_o"), j - 1)
                        whole, rest = nk // P, nk % P
                        if whole:
                            v = pt_buf[:, j % 2, 0:whole * P].rearrange("p (x q) -> p x q", q=P)[:, :, 0:nq]
                            s = PS[:, 4 + j % 2, 0:whole * P].rearrange("p (x q) -> p x q", q=P)[:, :, 0:nq]
                            af(v, s, ACT.Copy)
                        af(pt_buf[0:rest, j % 2, whole * P:whole * P + nq],
                           PS[0:rest, 4 + j % 2, whole * P:whole * P + nq], ACT.Copy).then_inc(sem(f"{tag}_pt_out"), 1)
                    j = i - 2
                    if 0 <= j < n:
                        h, q0, nq, nk = steps[j]
                        act.wait_ge(sem(f"{tag}_o"), j + 1)
                        dst, rows = o_of(h, q0, nq)
                        af(dst, PS[rows, 6 + j % 2, 0:nq], ACT.Copy).then_inc(sem(f"{tag}_o_out"), 1)

            act.wait_ge(sem("meta2"), 1)
            attention("mla", MLA_STEPS, att_s, att_p, att_pt, att_r,
                      lambda h, q0, nq: (o_mla[:, h, q0 - META:q0 - META + nq], slice(0, P)))

            g = CHUNK["hg0"]
            for f, dst in ((ACT.Silu, hq), (ACT.Sigmoid, hf), (ACT.Copy, hi)):
                for h in range(HEADS):
                    take(g, dst[:, h, :], bank(g), f)
                    g += 1
            for h in range(HEADS):
                take(g, hg[:, h, :], bank(g, c0=META, n=SEQ), ACT.Silu)
                g += 1
            act.wait_ge(sem("mla_probs"), len(MLA_STEPS))
            act.wait_ge(sem("mla_o"), len(MLA_STEPS))
            g = CHUNK["gate0"]
            for c in range(2 * DC):
                take(g, gates[:, c, :], bank(g, n=SEQ), ACT.Sigmoid, bias=vec("b_gate", c))
                g += 1
            for h in range(HEADS):
                g = CHUNK["vT"] + h
                take(g, v_tok[:, :, h * P:(h + 1) * P], bank(g, n=2 * P).rearrange("p (t n) -> p t n", t=2), count=False)
                take(g, v_meta[0:META, h * P:(h + 1) * P], bank(g, rows=META, c0=2 * P, n=P))
            for h in range(HEADS):
                g = CHUNK["kT"] + h
                take(g, kT_tok[:, h, :], bank(g, n=P), count=False)
                take(g, kT_meta[0:META, h, :], bank(g, rows=META, c0=P, n=P))
            for h in range(HEADS):
                g = CHUNK["S"] + h
                take(g, S1[:, h, :], bank(g, n=P), count=False)
                take(g, S2[:, h, :], bank(g, c0=P, n=P))
            for h in range(HEADS):
                g = CHUNK["o"] + h
                take(g, o_h[:, h, :], bank(g, n=SEQ))

            for h in range(HEADS):
                squares("hg", h, o_h[:, h, :], lambda: act.wait_ge(sem("chunk_out"), CHUNK["o"] + h + 1), SEQ)
                std("hg", h + 1, 2 + h % 2, SEQ, P, eps_rms, nrm[:, h % 2, 0:SEQ],
                    guard=(sem("y_hg"), h - 1) if h >= 2 else None)
            g = CHUNK["hgo0"]
            act.wait_ge(sem("y_hg"), HEADS)
            for c in range(DC):
                take(g, ya[:, c, :], bank(g, n=SEQ))
                g += 1
            for c in range(DC):
                take(g, yb[:, c, :], bank(g, n=SEQ))
                g += 1
            for c in range(DC):
                take(g, mixed[:, c, :], bank(g, n=SEQ))
                squares("post", c, mixed[:, c, :], lambda: act.wait_ge(sem("chunk_out"), g + 1), SEQ)
                g += 1
            std("post", DC, 2, SEQ, D, eps_rms, nrm[:, 0, 0:SEQ])
            for c in range(DC):
                def ready():
                    act.wait_ge(sem("h_mid"), c + 1)
                    act.wait_ge(sem("sum_post"), DC)
                squares("fpre", c, hT[:, c, META:L], ready, SEQ)
            std("fpre", DC, 3, SEQ, D, eps_rms, nrm[:, 1, 0:SEQ])
            g = CHUNK["ffi0"]
            for j in range(FC):
                take(g, hid[:, j, :], bank(g, n=SEQ), ACT.Silu)
                if j >= 2:
                    act.wait_ge(sem("hidden"), j - 1)
                take(g + 1, up[:, j % 2, :], bank(g + 1, n=SEQ))
                g += 2
            for c in range(DC):
                take(g, ffo[:, c, :], bank(g, n=SEQ))
                squares("fpost", c, ffo[:, c, :], lambda: act.wait_ge(sem("chunk_out"), g + 1), SEQ)
                g += 1
            std("fpost", DC, 2, SEQ, D, eps_rms, nrm[:, 0, 0:SEQ])

            for l in range(DEPTH2):
                T = f"L{l}"
                q_from = 0 if l == 0 else META
                nq_all = L - q_from
                g = CHUNK[f"{T}kw"]
                take(g, kiT, bank(g))
                take(g + 1, idx_w, bank(g + 1, n=16).rearrange("p (t n) -> p t n", t=2), scale=IDX_W_SCALE)
                for i in range(4):
                    take(g + 2 + i, qiT[:, i, :], bank(g + 2 + i))
                for s in range(16):
                    t, h = divmod(s, HEADS)
                    nk = Q_TILES[t][2]
                    act.wait_ge(sem(f"{T}idx"), s + 1)
                    if s >= 2:
                        act.wait_ge(sem(f"{T}score"), s - 1)
                    af(relu[:, s % 2, 0:nk], PS[:, 2 + s % 2, 0:nk], ACT.Relu, scale=IDX_SCALE)\
                        .then_inc(sem(f"{T}relu"), 1)
                g = CHUNK[f"{T}a"]
                for c in range(CC):
                    take(g, upad[:, c, TAPS - 1:TAPS - 1 + L], bank(g))
                    g += 1
                for c in range(CC):
                    take(g, gsig[:, c, :], bank(g), ACT.Sigmoid)
                    g += 1
                for dst in (q2, k2):
                    for i in range(4):
                        take(g, dst[:, i, :], bank(g))
                        g += 1
                for x, (t0, n) in enumerate(KEY_CHUNKS):
                    take(g, v2[0:n, x, :], bank(g, rows=n, n=512))
                    g += 1
                for dst in (szc, sza):
                    for i in range(4):
                        take(g, dst[:, i, :], bank(g), ACT.Silu)
                        g += 1
                attention(f"{T}att", DSA_STEPS[l], at2_s, at2_p, at2_pt, at2_r,
                          lambda h, q0, nq: (ycat[64 * (h % 2):64 * (h % 2) + 64, 4 + h // 2, q0:q0 + nq],
                                             slice(64 * (h % 2), 64 * (h % 2) + 64)))

                def ln_std(tag, count, src, bank_, dim):
                    for c in range(count):
                        squares(tag, c, src(c), lambda: act.wait_ge(sem(f"{tag}_centred"), c + 1), nq_all)
                    std(tag, count, bank_, nq_all, dim, eps_ln, nrm[:, 0, 0:nq_all])

                ln_std(f"{T}cln", CC, lambda c: acc[:, c, q_from:L], 3, CONV_C)
                for c in range(CC):
                    act.wait_ge(sem(f"{T}cln_scaled"), c + 1)
                    af(ycat[:, c, q_from:L], acc[:, c, q_from:L], ACT.Silu, scale=vec("conv_ln_g_2", 4 * l + c),
                       bias=vec("conv_ln_b_2", 4 * l + c)).then_inc(sem(f"{T}silu"), 1)
                g = CHUNK[f"{T}wo0"]
                for c in range(DC):
                    take(g, zT[:, c, q_from:L], bank(g, n=nq_all))
                    g += 1
                ln_std(f"{T}pln", DC, lambda c: zT[:, c, q_from:L], 5, D)
                for c in range(DC):
                    act.wait_ge(sem(f"{T}pln_scaled"), c + 1)
                    af(hT[:, c, q_from:L], zT[:, c, q_from:L], ACT.Identity, scale=vec("post_ln_g_2", 8 * l + c),
                       bias=vec("post_ln_b_2", 8 * l + c)).then_inc(sem("h_post"), 1)
            for t in range(2):
                for half in range(2):
                    g = CHUNK["out"] + 2 * t + half
                    take(g, out_tok[:, t, half * 512:half * 512 + 512], bank(g, n=512))

        @block.vector
        def _(dve):
            v = nc.vector
            order = [0]

            def link(ins):
                order[0] += 1
                ins.then_inc(sem("dve_order"), 1)
                dve.wait_ge(sem("dve_order"), order[0])

            v.memset(ones[:, :], 1.0).then_inc(sem("ones"), 1)
            v.memset(small[:, 0:1], EPS_RMS)
            v.memset(small[:, 1:2], EPS_LN).then_inc(sem("small"), 1)
            dve.wait_ge(sem("chunk_out"), CHUNK["start"] + DC + 1)
            l0 = cols[:, VEC["lb_logits"]:VEC["lb_logits"] + 8]
            l1 = cols[:, VEC["lb_logits"] + 8:VEC["lb_logits"] + 16]
            link(v.tensor_tensor(lb_m, l0, l1, ALU.max))
            v.tensor_tensor(lb_e0, l0, lb_m, ALU.subtract).then_inc(sem("lb_shift"), 1)
            v.tensor_tensor(lb_e1, l1, lb_m, ALU.subtract).then_inc(sem("lb_shift"), 1)

            def rstd(tag, count, buf):
                dve.wait_ge(sem(f"std_{tag}"), count)
                link(v.reciprocal(buf, buf))

            rstd("pre", 1, nrm[:, 0, :])
            for c in range(DC):
                v.scalar_tensor_tensor(out=uT[:, c, :], in0=hT[:, c, :], scalar=vec("mix_pre_g", c), in1=nrm[:, 0, :],
                                       op0=ALU.mult, op1=ALU.mult).then_inc(sem("u_pre"), 1)
            dve.wait_ge(sem("lb_exp"), 2)
            link(v.tensor_tensor(lb_m, lb_e0, lb_e1, ALU.add))
            link(v.reciprocal(lb_m, lb_m))
            link(v.tensor_tensor(lb, lb_e0, lb_m, ALU.mult))
            link(v.tensor_scalar(oml, lb, -1.0, 1.0, ALU.mult, ALU.add))

            for tag, b, first, name in (("cq", 0, 0, "q_a_norm_g"), ("ckv", 1, 2, "kv_a_norm_g")):
                rstd(tag, 1, nrm[:, b, :])
                for c in range(2):
                    v.scalar_tensor_tensor(out=c_nrm[:, first + c, :], in0=c_raw[:, first + c, :],
                                           scalar=vec(name, c), in1=nrm[:, b, :],
                                           op0=ALU.mult, op1=ALU.mult).then_inc(sem("c_nrm"), 1)

            def rope(tag, i, src, dst, t0, n, ta, tb):
                v.tensor_tensor(ta[:, i % 2, 0:n], src, cosT[:, t0:t0 + n], ALU.mult)
                dve.wait_ge(sem(f"{tag}_rope"), i + 1)
                v.tensor_tensor(tb[:, i % 2, 0:n], PS[:, 6 + i % 2, 0:n], sinT[:, t0:t0 + n], ALU.mult)\
                    .then_inc(sem(f"{tag}_rope_out"), 1)
                dve.wait_ge(sem(f"{tag}_rope_out"), i + 1)
                v.tensor_tensor(dst, ta[:, i % 2, 0:n], tb[:, i % 2, 0:n], ALU.add).then_inc(sem(f"{tag}_roped"), 1)

            dve.wait_ge(sem("chunk_out"), CHUNK["wkvb"])
            for i in range(4):
                rope("mla", i, qpe[:, i, :], qpr[:, i, :], META, SEQ, rope_a, rope_b)
            rope("mla", 4, kpe, kpr, 0, L, rope_a, rope_b)

            def attention(tag, steps, scale, mask_of, s_buf, p_buf, r_buf):
                n = len(steps)
                for i in range(n + 1):
                    if i < n:
                        h, q0, nq, nk = steps[i]
                        dve.wait_ge(sem(f"{tag}_scores"), i + 1)
                        if i >= 2:
                            dve.wait_ge(sem(f"{tag}_exp"), i - 1)
                        v.tensor_tensor_reduce(out=s_buf[0:nq, i % 2, 0:nk], in0=PS[0:nq, 2 + i % 2, 0:nk],
                                               in1=mask_of(q0, nq, nk), scale=-scale, scalar=BIG,
                                               op0=ALU.add, op1=ALU.min,
                                               accum_out=r_buf[0:nq, i % 2, 0:1]).then_inc(sem(f"{tag}_masked"), 1)
                    j = i - 1
                    if 0 <= j < n:
                        h, q0, nq, nk = steps[j]
                        dve.wait_ge(sem(f"{tag}_exp"), j + 1)
                        link(v.reciprocal(r_buf[0:nq, j % 2, 1:2], r_buf[0:nq, j % 2, 1:2]))
                        v.tensor_scalar(p_buf[0:nq, j % 2, 0:nk], p_buf[0:nq, j % 2, 0:nk],
                                        r_buf[0:nq, j % 2, 1:2], None, ALU.mult).then_inc(sem(f"{tag}_probs"), 1)

            attention("mla", MLA_STEPS, MLA_SCALE, lambda q0, nq, nk: cst(CAUSAL[q0])[0:nq, :], att_s, att_p, att_r)

            dve.wait_ge(sem("mla_o"), len(MLA_STEPS))
            g = CHUNK["hg0"] + 8
            for h in range(HEADS):
                dve.wait_ge(sem("chunk_out"), g + h + 1)
                v.tensor_scalar(hf[:, h, :], hf[:, h, :], oml[:, h:h + 1], lb[:, h:h + 1], ALU.mult, ALU.add)\
                    .then_inc(sem("f_ready"), 1)
            dve.wait_ge(sem("f_ready"), HEADS)
            for half in range(2):
                s = slice(1088 * half, 1088 * half + 1088)
                v.tensor_scalar(flat["k"][:, s], flat["f"][:, s], -1.0, 1.0, ALU.mult, ALU.add)\
                    .then_inc(sem("level_ready"), 1)
            dve.wait_ge(sem("chunk_out"), CHUNK["vT"] + 8)
            lvl = cst("level").rearrange("p (l n) -> p l n", n=P)
            blocks = [flat["f"]]
            at = 0
            for lv in range(4):
                n = HEADS * L >> (lv + 1)
                blocks.append(tree[:, at:at + n])
                at += n
            t16 = blocks[4].rearrange("p (h b) -> p h b", h=HEADS)
            t32, t64, t128 = (tree[:, at + o:at + o + 8 * n].rearrange("p (h b) -> p h b", h=HEADS)
                              for o, n in ((0, 8), (64, 4), (96, 2)))
            for lv in range(LEVELS + 1):
                for half in range(2):
                    for b in range(2):
                        i = 4 * lv + 2 * half + b
                        dve.wait_ge(sem("level_done"), i + 1)
                        dst = scoresT[:, 8 * half + 4 * b:8 * half + 4 * b + 4, :]
                        src = PS[:, 2 + 2 * half + b, :].rearrange("p (j n) -> p j n", n=P)
                        m = lvl[:, lv:lv + 1, :].to_broadcast([P, 4, P])
                        if lv == 0:
                            v.tensor_tensor(dst, src, m, ALU.mult).then_inc(sem("level_masked"), 1)
                        else:
                            v.copy_predicated(dst, m.bitcast(U32), src).then_inc(sem("level_masked"), 1)
                    hs = slice(4 * half, 4 * half + 4)
                    if lv == 0:
                        v.tensor_tensor(flat["q"][:, 1088 * half:1088 * half + 1088],
                                        flat["q"][:, 1088 * half:1088 * half + 1088],
                                        flat["f"][:, 1088 * half:1088 * half + 1088], ALU.mult)\
                            .then_inc(sem("level_ready"), 1)
                        continue
                    B = 1 << (lv - 1)
                    if B < 16:
                        n = 1088 // (2 * B)
                        view = lambda x: x[:, 1088 * half:1088 * half + 1088].rearrange("p (n u b) -> p n u b", u=2, b=B)
                        qv, kv = view(flat["q"]), view(flat["k"])
                        tot = blocks[lv - 1][:, n * 2 * half:n * 2 * half + 2 * n].rearrange("p (n u) -> p n u", u=2)
                        nxt = blocks[lv][:, n * half:n * half + n]
                        lo = tot[:, :, 0:1].to_broadcast([P, n, B])
                        hi_ = tot[:, :, 1:2].to_broadcast([P, n, B])
                        q_up, k_lo = qv[:, :, 1, :], kv[:, :, 0, :]
                        lo1, hi1 = tot[:, :, 0], tot[:, :, 1]
                    else:
                        n = SEQ // (2 * B)
                        view = lambda x: x[:, hs, META:L].rearrange("p h (n u b) -> p h n u b", u=2, b=B)
                        qv, kv = view(hq), view(hk)
                        tot = {16: t16[:, hs, 1:17], 32: t32[:, hs, :], 64: t64[:, hs, :]}[B]
                        tot = tot.rearrange("p h (n u) -> p h n u", u=2)
                        nxt = {16: t32, 32: t64, 64: t128}[B][:, hs, :]
                        lo = tot[:, :, :, 0:1].to_broadcast([P, 4, n, B])
                        hi_ = tot[:, :, :, 1:2].to_broadcast([P, 4, n, B])
                        q_up, k_lo = qv[:, :, :, 1, :], kv[:, :, :, 0, :]
                        lo1, hi1 = tot[:, :, :, 0], tot[:, :, :, 1]
                    v.tensor_tensor(q_up, q_up, lo, ALU.mult)
                    link(v.tensor_tensor(nxt, lo1, hi1, ALU.mult))
                    v.tensor_tensor(k_lo, k_lo, hi_, ALU.mult).then_inc(sem("level_ready"), 1)
            for h in range(HEADS):
                dve.wait_ge(sem("chunk_out"), CHUNK["S"] + h + 1)
                v.scalar_tensor_tensor(out=S2[:, h, :], in0=S1[:, h, :], scalar=t128[:, h, 0:1], in1=S2[:, h, :],
                                       op0=ALU.mult, op1=ALU.add).then_inc(sem("state"), 1)
            dve.wait_ge(sem("chunk_out"), CHUNK["o"] + HEADS)
            for h in range(HEADS):
                rstd("hg", h + 1, nrm[:, h % 2, 0:SEQ])
                link(v.scalar_tensor_tensor(out=o_h[:, h, :], in0=o_h[:, h, :], scalar=vec("hg_norm_g", 0),
                                            in1=nrm[:, h % 2, 0:SEQ], op0=ALU.mult, op1=ALU.mult))
                v.tensor_tensor(y_hg[:, h, :], o_h[:, h, :], hg[:, h, :], ALU.mult).then_inc(sem("y_hg"), 1)

            for c in range(DC):
                dve.wait_ge(sem("chunk_out"), CHUNK["hgo0"] + c + 1)
                v.tensor_tensor(ya[:, c, :], ya[:, c, :], gates[:, c, :], ALU.mult)
            for c in range(DC):
                dve.wait_ge(sem("chunk_out"), CHUNK["mlo0"] + c + 1)
                link(v.tensor_tensor(yb[:, c, :], yb[:, c, :], gates[:, DC + c, :], ALU.mult))
                v.tensor_tensor(ya[:, c, :], ya[:, c, :], yb[:, c, :], ALU.add).then_inc(sem("mixed"), 1)
            rstd("post", 1, nrm[:, 0, 0:SEQ])
            for c in range(DC):
                link(v.scalar_tensor_tensor(out=mixed[:, c, :], in0=mixed[:, c, :], scalar=vec("mix_post_g", c),
                                            in1=nrm[:, 0, 0:SEQ], op0=ALU.mult, op1=ALU.mult))
                v.tensor_tensor(hT[:, c, META:L], hT[:, c, META:L], mixed[:, c, :], ALU.add).then_inc(sem("h_mid"), 1)
            rstd("fpre", 1, nrm[:, 1, 0:SEQ])
            for c in range(DC):
                v.scalar_tensor_tensor(out=uT[:, c, META:L], in0=hT[:, c, META:L], scalar=vec("ffn_pre_g", c),
                                       in1=nrm[:, 1, 0:SEQ], op0=ALU.mult, op1=ALU.mult).then_inc(sem("u_fpre"), 1)
            for j in range(FC):
                dve.wait_ge(sem("chunk_out"), CHUNK["ffi0"] + 2 * j + 2)
                v.tensor_tensor(hid[:, j, :], hid[:, j, :], up[:, j % 2, :], ALU.mult).then_inc(sem("hidden"), 1)
            rstd("fpost", 1, nrm[:, 0, 0:SEQ])
            v.tensor_copy(hT[:, :, 0:META], vec_rows[:, 0, :].rearrange("p (c t) -> p c t", c=DC))
            for c in range(DC):
                link(v.scalar_tensor_tensor(out=ffo[:, c, :], in0=ffo[:, c, :], scalar=vec("ffn_post_g", c),
                                            in1=nrm[:, 0, 0:SEQ], op0=ALU.mult, op1=ALU.mult))
                v.tensor_tensor(hT[:, c, META:L], hT[:, c, META:L], ffo[:, c, :], ALU.add).then_inc(sem("h_ready"), 1)

            v.memset(upad[:, :, 0:TAPS - 1], 0.0)
            v.memset(top8[:, :, :], NEG)
            for l in range(DEPTH2):
                T = f"L{l}"
                q_from = 0 if l == 0 else META
                n_all = L - q_from
                dve.wait_ge(sem("chunk_out"), CHUNK[f"{T}a"])
                for i in range(4):
                    rope(f"{T}i", i, qiT[:, i, :], qir[:, i, :], 0, L, rope2_a, rope2_b)
                rope(f"{T}i", 4, kiT, kir, 0, L, rope2_a, rope2_b)
                for s in range(16):
                    t, h = divmod(s, HEADS)
                    q0, nq, nk = Q_TILES[t]
                    dve.wait_ge(sem(f"{T}relu"), s + 1)
                    if s:
                        dve.wait_ge(sem(f"{T}score"), s)
                    v.scalar_tensor_tensor(out=score[:, t, 0:nk], in0=relu[:, s % 2, 0:nk], scalar=idx_w[:, t, h:h + 1],
                                           in1=cst(CAUSAL[q0]) if h == 0 else score[:, t, 0:nk],
                                           op0=ALU.mult, op1=ALU.add).then_inc(sem(f"{T}score"), 1)
                dve.wait_ge(sem(f"{T}score"), 16)
                for r in range(ROUNDS):
                    for t in range(2):
                        nk = Q_TILES[t][2]
                        v.max(top8[:, t, :], score[:, t, 0:nk]).then_inc(sem(f"{T}top"), 1)
                    for t in range(2):
                        nk = Q_TILES[t][2]
                        dve.wait_ge(sem(f"{T}top"), 4 * r + 2 if r < ROUNDS - 1 else 4 * r + 2)
                        if r == ROUNDS - 1 and TOPK % 8:
                            link(v.memset(top8[:, t, TOPK % 8:8], NEG))
                        v.match_replace(score[:, t, 0:nk], in_to_replace=top8[:, t, :], in_values=score[:, t, 0:nk],
                                        imm_value=NEG).then_inc(sem(f"{T}top"), 1)
                    dve.wait_ge(sem(f"{T}top"), 4 * r + 4)
                for t in range(2):
                    q0, nq, nk = Q_TILES[t]
                    link(v.tensor_scalar(sel[:, t, 0:nk], score[:, t, 0:nk], NEG, NEG, ALU.not_equal, ALU.mult))
                    link(v.tensor_tensor(sel[:, t, 0:nk], sel[:, t, 0:nk], cst(CAUSAL[q0]), ALU.min))

                for c in range(CC):
                    dve.wait_ge(sem("chunk_out"), CHUNK[f"{T}g"] + c + 1)
                    link(v.tensor_tensor(upad[:, c, TAPS - 1:TAPS - 1 + L], upad[:, c, TAPS - 1:TAPS - 1 + L],
                                         gsig[:, c, :], ALU.mult))
                for j in range(TAPS):
                    for c in range(CC):
                        w = cols[:, TAP_COL[l] + CC * j + c:TAP_COL[l] + CC * j + c + 1]
                        if j == 0:
                            ins = v.tensor_scalar(acc[:, c, :], upad[:, c, 0:L], w, vec("conv_b_2", 4 * l + c),
                                                  ALU.mult, ALU.add)
                        else:
                            dve.wait_ge(sem(f"{T}tap"), CC * (j - 1) + c + 1)
                            ins = v.scalar_tensor_tensor(out=acc[:, c, :], in0=upad[:, c, j:j + L], scalar=w,
                                                         in1=acc[:, c, :], op0=ALU.mult, op1=ALU.add)
                        ins.then_inc(sem(f"{T}tap"), 1)

                for i in range(8):
                    src, dst = (q2, q2r) if i < 4 else (k2, k2r)
                    dve.wait_ge(sem("chunk_out"), CHUNK[f"{T}q"] + i + 1)
                    rope(f"{T}q", i, src[:, i % 4, :], dst[:, i % 4, :], 0, L, rope2_a, rope2_b)
                attention(f"{T}att", DSA_STEPS[l], ATT_SCALE,
                          lambda q0, nq, nk: cst("causal_m")[0:nq, :] if q0 == 0 else sel[:, (q0 - META) // P, 0:nk],
                          at2_s, at2_p, at2_r)

                def centre(tag, count, src, bank_, dim):
                    dve.wait_ge(sem(f"{tag}_mean"), 1)
                    mean = nrm[:, 1, 0:n_all]
                    link(v.tensor_scalar(mean, PS[:, bank_, 0:n_all], 1.0 / dim, None, ALU.mult))
                    for c in range(count):
                        v.tensor_tensor(src(c), src(c), mean, ALU.subtract).then_inc(sem(f"{tag}_centred"), 1)
                    rstd(tag, 1, nrm[:, 0, 0:n_all])
                    dve.wait_ge(sem(f"sq_{tag}"), count)
                    for c in range(count):
                        v.tensor_tensor(src(c), src(c), nrm[:, 0, 0:n_all], ALU.mult).then_inc(sem(f"{tag}_scaled"), 1)

                centre(f"{T}cln", CC, lambda c: acc[:, c, q_from:L], 2, CONV_C)
                for c in range(CC):
                    dve.wait_ge(sem(f"{T}silu"), c + 1)
                    v.tensor_tensor(ycat[:, c, q_from:L], ycat[:, c, q_from:L], szc[:, c, q_from:L], ALU.mult)\
                        .then_inc(sem(f"{T}y"), 1)
                dve.wait_ge(sem(f"{T}att_o_out"), len(DSA_STEPS[l]))
                for c in range(CC):
                    v.tensor_tensor(ycat[:, CC + c, q_from:L], ycat[:, CC + c, q_from:L], sza[:, c, q_from:L],
                                    ALU.mult).then_inc(sem(f"{T}y"), 1)
                for c in range(DC):
                    dve.wait_ge(sem("chunk_out"), CHUNK[f"{T}wo0"] + c + 1)
                    v.scalar_tensor_tensor(out=zT[:, c, q_from:L], in0=hT[:, c, q_from:L], scalar=ALPHA,
                                           in1=zT[:, c, q_from:L], op0=ALU.mult, op1=ALU.add)\
                        .then_inc(sem(f"{T}pln_in"), 1)
                dve.wait_ge(sem(f"{T}pln_in"), DC)
                centre(f"{T}pln", DC, lambda c: zT[:, c, q_from:L], 4, D)


_INS = ["x", "meta_tokens", "w_in", "b_gate", "lb_logits", "hg_norm_g", "w_hg_o", "q_a_norm_g", "w_q_b",
        "kv_a_norm_g", "w_kv_b", "w_mla_o", "w_out", "mix_pre_g", "mix_post_g", "ffn_pre_g", "ffn_post_g",
        "w_ffn_in", "w_ffn_out", "meta_tokens_2", "w_in_2", "conv_w_2", "conv_b_2", "conv_ln_g_2",
        "conv_ln_b_2", "w_out_2", "post_ln_g_2", "post_ln_b_2"]


def kernel(**inputs):
    import numpy as _np
    import concourse.bacc as _bacc
    from concourse import mybir as _mybir
    from concourse.bass_utils import run_bass_kernel_spmd as _run

    nc = _bacc.Bacc("TRN2", target_bir_lowering=False, num_devices=1)
    arrays, args = {}, {}
    for name in _INS + ["constants"]:
        arr = shape_constants() if name == "constants" else _np.ascontiguousarray(inputs[name])
        arrays[f"in_{name}"] = arr
        args[name] = nc.dram_tensor(f"in_{name}", arr.shape, _mybir.dt.from_np(arr.dtype), kind="ExternalInput").ap()
    out = nc.dram_tensor("out", (1, SEQ, D), F32, kind="ExternalOutput").ap()
    bass_blocks(nc, args, out)
    r = _run(nc, [arrays], core_ids=[0])
    return r.results[0]["out"]
```

```python
from contextlib import ExitStack

import numpy as np

import concourse.bass as bass
from concourse import mybir

F32 = mybir.dt.float32
F32R = mybir.dt.float32r
U32 = mybir.dt.uint32
ALU = mybir.AluOpType
ACT = mybir.ActivationFunctionType

P = 128
META = 16
SEQ = 256
L = META + SEQ
D = 1024
DC = D // P
HEADS = 8
EPS_RMS = 1e-6
EPS_LN = 1e-5
NEG = -3.0e38
BIG = 3.0e38

LORA = 256
NOPE, ROPE, VDIM = 128, 64, 128
MLA_SCALE = float(NOPE + ROPE) ** -0.5
FFN = 2816
FC = FFN // P
FFN_ITEMS = FFN // 256
LEVELS = 7
GATE_COL = 4 * D + 2 * LORA + ROPE

DEPTH2 = 2
CONV_C = 512
CC = CONV_C // P
TAPS = 31
HD = 64
TOPK = min(256, L // 4)
ROUNDS = -(-TOPK // 8)
IDX_SCALE = float(HD) ** -0.5
IDX_W_SCALE = float(HEADS) ** -0.5
ATT_SCALE = float(HD) ** -0.5
ALPHA = (2.0 * DEPTH2) ** 0.25
COL2 = dict(a=0, g=512, zc=1024, q=1536, k=2048, v=2560, za=3072, qi=3584, ki=4096)

KEY_CHUNKS = [(0, 128), (128, 128), (256, 16)]

CONST = {}
_at = 0
for _name, _n in (("ident", P), ("rot", P), ("cos", L), ("sin", L), ("level", (LEVELS + 1) * P),
                  ("causal_m", META), ("causal_0", META + P), ("causal_1", L)):
    CONST[_name] = (_at, _n)
    _at += _n
N_CONST = _at


def shape_constants():
    c = np.zeros((P, N_CONST), np.float32)

    def put(name, a):
        at, n = CONST[name]
        c[:a.shape[0], at:at + n] = a

    put("ident", np.eye(P, dtype=np.float32))
    rot = np.zeros((P, P), np.float32)
    for m in range(P):
        if m % 64 < 32:
            rot[m + 32, m] = -1.0
        else:
            rot[m - 32, m] = 1.0
    put("rot", rot)
    inv = (1.0 / (np.float32(10000.0) ** (np.arange(0, 64, 2, dtype=np.float32) / np.float32(64)))).astype(np.float32)
    ang = np.arange(L, dtype=np.float32)[None, :] * inv[np.arange(P) % 32][:, None]
    put("cos", np.cos(ang).astype(np.float32))
    put("sin", np.sin(ang).astype(np.float32))
    s, t = np.arange(P)[:, None], np.arange(P)[None, :]
    masks = [s == t]
    for lv in range(LEVELS):
        b = 1 << lv
        masks.append((s // (2 * b) == t // (2 * b)) & (s // b % 2 == 0) & (t // b % 2 == 1))
    put("level", np.concatenate(masks, 1).astype(np.float32))
    for name, first, rows in (("causal_m", 0, META), ("causal_0", META, P), ("causal_1", META + P, P)):
        n = CONST[name][1]
        put(name, np.where(np.arange(n)[None, :] <= first + np.arange(rows)[:, None], 0.0, NEG).astype(np.float32))
    return c


VEC_LIST = [("mix_pre_g", 8), ("mix_post_g", 8), ("ffn_pre_g", 8), ("ffn_post_g", 8), ("b_gate", 16),
            ("lb_logits", 16), ("hg_norm_g", 1), ("q_a_norm_g", 2), ("kv_a_norm_g", 2),
            ("conv_b_2", 8), ("conv_ln_g_2", 8), ("conv_ln_b_2", 8), ("post_ln_g_2", 16), ("post_ln_b_2", 16)]
VEC = {}
_at = 0
for _name, _n in VEC_LIST:
    VEC[_name] = _at
    _at += _n
N_VEC = _at
TAP_COL = [N_VEC, N_VEC + TAPS * CC]
N_COLS = N_VEC + 2 * TAPS * CC

SLOTS = 3
ITEM_N = 2048


def items(name, n):
    return [(f"{name}{i}", 1) for i in range(n)]


STREAM = (items("c", 2) + [("kpe", 2)] + items("hg", 2) + items("wqb", 2) + items("wkvb", 2) + items("hg", 16)[2:]
          + items("gate", 8) + items("mlo", 4) + items("hgo", 4) + items("mix", 4)
          + items("ffi", 2 * FFN_ITEMS) + items("ffo", 2 * DC))
for _l in range(DEPTH2):
    STREAM += [(f"L{_l}kw", 2)]
    for _n, _k in (("qi", 2), ("a", 2), ("g", 2), ("q", 2), ("k", 2), ("v", 2), ("zc", 2), ("za", 2), ("wo", 4)):
        STREAM += items(f"L{_l}{_n}", _k)
SPLIT = {n: i for i, n in enumerate(n for n, _ in STREAM if not n.startswith(("wqb", "wkvb")))}
SPLIT_ORDER = list(SPLIT)

MLA_N = 2 * HEADS
DSA_N = [3 * HEADS, 2 * HEADS]


def part(name, c):
    return f"{name}{c // 2}", c % 2


def ffi_chunk(j, up):
    return f"ffi{j // 2 * 2 + up}", j % 2


def z_chunks(l, s):
    n = DSA_N[l] + 2
    return [("zc" if z < 4 else "za", z % 4) for z in range(s * 8 // n, (s + 1) * 8 // n)]


ORDER = [("start", i) for i in range(12)]
ORDER += [(n, i) for n, k in (("c0", 2), ("c1", 2), ("kpe", 1), ("wqb", 12), ("wkvb", 14)) for i in range(k)]
ORDER += [part("hg", c) for c in range(32)]
for _h in range(HEADS):
    ORDER += [("vT", _h)] + ([part("gate", _h // 2)] if _h % 2 else [])
ORDER += [part("gate", c) for c in range(4, 16)]
for _h in range(HEADS):
    ORDER += [("kT", _h)] + ([part("mlo", _h // 2)] if _h % 2 else [])
for _h in range(HEADS):
    ORDER += [("S", _h)] + ([part("mlo", 4 + _h // 2)] if _h % 2 else [])
ORDER += [("o", h) for h in range(HEADS)]
ORDER += [part(n, c) for n in ("hgo", "mix") for c in range(DC)]
ORDER += [part("ffi", c) for c in range(4 * FFN_ITEMS)] + [("ffo", c) for c in range(DC)]
for _l in range(DEPTH2):
    ORDER += [(f"L{_l}kw", 0), (f"L{_l}kw", 1)]
    ORDER += [part(f"L{_l}{n}", i) for n in ("qi", "a", "g", "q", "k", "v") for i in range(4)]
    ORDER += [(f"L{_l}vt", i) for i in range(3)]
    ORDER += [part(f"L{_l}{n}", i) for s in range(DSA_N[_l] + 2) for n, i in z_chunks(_l, s)]
    ORDER += [part(f"L{_l}wo", c) for c in range(DC)]
ORDER += [("out", i) for i in range(4)]
CHUNK = {c: i for i, c in enumerate(ORDER)}
SLOT, USE, PREV = {}, {}, {}
_uses, _last = [0] * SLOTS, [None] * SLOTS
for _i, (_it, _dmas) in enumerate(STREAM):
    _s = _i % SLOTS
    SLOT[_it] = _s
    _uses[_s] += 16 * _dmas
    USE[_it] = _uses[_s]
    PREV[_it] = _last[_s]
    _last[_s] = _it
LAST_CHUNK = {}
for (_n, _m), _g in CHUNK.items():
    if _n in SPLIT:
        LAST_CHUNK[_n] = max(_g, LAST_CHUNK.get(_n, 0))
ENDS = {g: n for n, g in LAST_CHUNK.items()}


def bass_blocks(nc, a, out):
    ctx = ExitStack()
    with ctx:
        def sb(name, shape, dt=F32):
            return ctx.enter_context(nc.sbuf_tensor(name, shape, dt))

        sems = {}

        def sem(name):
            if name not in sems:
                sems[name] = ctx.enter_context(nc.semaphore(name))
            return sems[name]

        ring = sb("ring", [P, SLOTS, ITEM_N])
        w_hi, w_lo = sb("w_hi", [P, 2, ITEM_N], F32R), sb("w_lo", [P, 2, ITEM_N], F32R)
        x_hi, x_lo = sb("x_hi", [P, DC, L], F32R), sb("x_lo", [P, DC, L], F32R)
        u_t = sb("u_t", [P, 4, L])
        const = sb("const", [P, N_CONST])
        ones = sb("ones", [P, P])
        vec_rows = sb("vec_rows", [P, 3, P])
        cols = sb("cols", [P, N_COLS])
        small = sb("small", [P, 64])
        hT = sb("hT", [P, DC, L])
        keep = sb("keep", [P, 2048])
        ZONE_A, ZONE_B = 10752, 13440
        zone_at = nc.sbuf_base
        zoneA = sb("zoneA", [P, ZONE_A])
        zoneB = sb("zoneB", [P, ZONE_B])
        assert nc.sbuf_base == zone_at + 4 * (ZONE_A + ZONE_B)

        def in_zone(name, at, *shape):
            return nc.alloc_sbuf_tensor_at(name, [P, *shape], F32R, offset=zone_at + 4 * at)

        sq = sb("sq", [P, 2, L])
        nrm = sb("nrm", [P, 2, L])

        class Zone:
            def __init__(self, t, at=0):
                self.t, self.at = t, at

            def __call__(self, *shape):
                n = int(np.prod(shape))
                v = self.t[:, self.at:self.at + n]
                self.at += n
                if len(shape) == 2:
                    v = v.rearrange("p (a b) -> p a b", b=shape[1])
                if len(shape) == 3:
                    v = v.rearrange("p (a b c) -> p a b c", b=shape[1], c=shape[2])
                return v

        PS = ctx.enter_context(nc.psum_tensor("PS", [P, 8, 512], F32))

        def cst(name, rows=P):
            at, n = CONST[name]
            return const[0:rows, at:at + n]

        ident, rotm, cosT, sinT = cst("ident"), cst("rot"), cst("cos"), cst("sin")

        def vec(name, c):
            return cols[:, VEC[name] + c:VEC[name] + c + 1]

        eps_rms, eps_ln = small[:, 0:1], small[:, 1:2]
        lb, oml = small[:, 8:16], small[:, 16:24]
        lb_e0, lb_e1, lb_m = small[:, 24:32], small[:, 32:40], small[:, 40:48]

        z = Zone(zoneA)
        hq, hk, hf, hi = z(HEADS, L), z(HEADS, L), z(HEADS, L), z(HEADS, L)
        hg = z(HEADS, SEQ)
        scoresT = Zone(zoneA, 3 * HEADS * L)(HEADS * 2, P)
        flat = {n: v.rearrange("p h t -> p (h t)") for n, v in (("q", hq), ("k", hk), ("f", hf))}
        z = Zone(zoneB)
        c_raw, c_nrm = z(4, L), z(4, L)
        qn, qpe, qpr = z(HEADS, SEQ), z(4, SEQ), z(4, SEQ)
        kn, kpe, kpr = z(HEADS, L), z(L), z(L)
        vM = z(3, HEADS * VDIM)
        att_s, att_p, att_r = z(2, L), z(2, L), z(2, 2)
        rope_a, rope_b = att_s, att_p
        att_pt = Zone(zoneB)(2, 3 * P)
        assert z.at <= 13440
        z = Zone(zoneB)
        tree = z(HEADS * L)
        v_tok, v_meta = z(2, HEADS * P), z(HEADS * P)
        S1, S2 = z(HEADS, P), z(HEADS, P)
        kT_tok, kT_meta = z(HEADS, P), z(HEADS, P)
        o_h = Zone(zoneB, z.at - 2 * HEADS * P)(HEADS, SEQ)
        gates = z(2 * DC, SEQ)
        assert z.at <= 13440
        o_mla = keep[:, :].rearrange("p (h t) -> p h t", h=HEADS)
        z = Zone(zoneA)
        ya, mixed = z(DC, SEQ), z(DC, SEQ)
        y_mla = Zone(zoneA, 2 * HEADS * L)(DC, SEQ)
        y_hg = Zone(zoneA, 3 * HEADS * L)(HEADS, SEQ)
        mix_hi, mix_lo = in_zone("mix_hi", ZONE_A, DC, SEQ), in_zone("mix_lo", ZONE_A + DC * SEQ, DC, SEQ)
        hid_hi, hid_lo = in_zone("hid_hi", 0, FC, SEQ), in_zone("hid_lo", ZONE_A, FC, SEQ)
        z = Zone(zoneB, FC * SEQ)
        hid, up = z(4, SEQ), z(2, SEQ)
        ffo = z(DC, SEQ)
        z = Zone(zoneA)
        kiT, kir, qiT, qir = z(L), z(L), z(4, L), z(4, L)
        idx_w = z(2, 8)
        upad, gsig = z(CC, TAPS - 1 + L), z(CC, L)
        acc = z(CC, L)
        zT = Zone(zoneA, z.at)(DC, L)
        q2, k2 = z(4, L), z(4, L)
        assert z.at <= 10752
        z = Zone(zoneB)
        q2r, k2r = z(4, L), z(4, L)
        v2 = z(3, HEADS * HD)
        szc, sza = z(CC, L), z(CC, L)
        relu = z(2, L)
        score = z(2, L)
        sel = z(2, L)
        top8 = z(2, 8)
        at2_s, at2_p, at2_pt, at2_r = z(2, L), z(2, L), z(2, 3 * P), z(2, 2)
        rope2_a, rope2_b = z(2, L), z(2, L)
        ycat = z(DC, L)
        vT2 = keep[:, 0:4 * L].rearrange("p (c t) -> p c t", c=4)
        assert z.at <= 13440, z.at
        assert z.at <= 13440, z.at
        out_tok = zoneA[:, 0:2 * D].rearrange("p (t d) -> p t d", t=2)
        x_tok = zoneA[:, 0:2 * D].rearrange("p (t d) -> p t d", t=2)
        m_tok = zoneA[:, 2 * D:4 * D].rearrange("p (t d) -> p t d", t=2)

        def slot(name):
            return ring[:, SLOT[name], :]

        def w_ready(eng, name):
            eng.wait_ge(sem(f"slot{SLOT[name]}_full"), USE[name])

        def split_size(name):
            return {"kpe": DC * 2 * ROPE, "kw": DC * (2 * HD + HEADS)}.get(
                name[2:] if name[0] == "L" else name, 11 * P if name.startswith("ffo") else ITEM_N)

        def out_of_psum(eng, name, m=0):
            eng.wait_ge(sem("chunk_out"), CHUNK[name, m] + 1)

        Q_TILES = [(META, P, META + P), (META + P, P, L)]
        MLA_STEPS = [(h, *t) for h in range(HEADS) for t in Q_TILES]
        DSA_STEPS = [[(h, *t) for h in range(HEADS) for t in ([(0, META, META)] if l == 0 else []) + Q_TILES]
                     for l in range(DEPTH2)]
        CAUSAL = {0: "causal_m", META: "causal_0", META + P: "causal_1"}

        block = ctx.enter_context(nc.Block())

        @block.sync
        def _(sp):
            x2 = a["x"][0].rearrange("(t p) d -> p t d", p=P)
            sp.dma_start(x_tok, x2).then_inc(sem("x_in"), 16)
            sp.dma_start(m_tok[0:META, 0, :], a["meta_tokens"]).then_inc(sem("x_in"), 16)
            sp.dma_start(m_tok[0:META, 1, :], a["meta_tokens_2"]).then_inc(sem("x_in"), 16)
            sp.dma_start(const[:, 0:2 * P], a["constants"][:, 0:2 * P]).then_inc(sem("const_in"), 16)

            def free(name):
                before = PREV[name]
                if before in SPLIT:
                    sp.wait_ge(sem("w_lo"), SPLIT[before] + 1)
                elif before is not None:
                    sp.wait_ge(sem("chunk_done"), CHUNK[before[:-1], {"wqb0": 9, "wqb1": 11, "wkvb0": 13, "wkvb1": 13}[before]] + 1)

            def full(name, ins):
                ins.then_inc(sem(f"slot{SLOT[name]}_full"), 16)

            def kview(w):
                return w.rearrange("(k p) n -> p k n", p=P)

            def load(name, w, n):
                k = w.shape[1]
                free(name)
                full(name, sp.dma_start(slot(name)[:, 0:k * n].rearrange("p (k n) -> p k n", k=k), w))

            w_in = kview(a["w_in"][0])

            def load_cols(name, w, count, c0=0, first=0):
                for i in range(first, count):
                    load(f"{name}{i}", w[:, :, c0 + i * 256:c0 + (i + 1) * 256], 256)

            load_cols("c", w_in, 2, 4 * D)
            sp.dma_start(const[:, 2 * P:N_CONST], a["constants"][:, 2 * P:N_CONST]).then_inc(sem("tables_in"), 16)

            def load_twice(name, w, n, cols_):
                free(name)
                dst = slot(name)[:, 0:DC * (n + 64)].rearrange("p (k n) -> p k n", k=DC)
                full(name, sp.dma_start(dst[:, :, 0:64], w[:, :, cols_:cols_ + 64]))
                full(name, sp.dma_start(dst[:, :, 64:64 + n], w[:, :, cols_:cols_ + n]))

            load_twice("kpe", w_in, ROPE, 4 * D + 512)
            load_cols("hg", w_in, 2)
            for i in range(2):
                load(f"wqb{i}", kview(a["w_q_b"][0])[:, :, i * 768:(i + 1) * 768], 768)
            for i in range(2):
                load(f"wkvb{i}", kview(a["w_kv_b"][0])[:, :, i * 1024:(i + 1) * 1024], 1024)
            load_cols("hg", w_in, 16, first=2)
            load_cols("gate", w_in, 8, GATE_COL)
            for n, w in (("mlo", "w_mla_o"), ("hgo", "w_hg_o"), ("mix", "w_out")):
                load_cols(n, kview(a[w][0]), 4)
            w_fi = kview(a["w_ffn_in"][0])
            for i in range(2 * FFN_ITEMS):
                c0 = i % 2 * FFN + i // 2 * 256
                load(f"ffi{i}", w_fi[:, :, c0:c0 + 256], 256)
            w_fo = kview(a["w_ffn_out"][0])
            for i in range(2 * DC):
                load(f"ffo{i}", w_fo[:, i % 2 * 11:i % 2 * 11 + 11, i // 2 * P:(i // 2 + 1) * P], P)
            for l in range(DEPTH2):
                w2 = kview(a["w_in_2"][l])
                load_twice(f"L{l}kw", w2, HD + HEADS, COL2["ki"])
                for n in ("qi", "a", "g", "q", "k", "v", "zc", "za"):
                    load_cols(f"L{l}{n}", w2, 2, COL2[n])
                load_cols(f"L{l}wo", kview(a["w_out_2"][l]), 4)
            for t in range(2):
                out_of_psum(sp, "out", 2 * t + 1)
                sp.dma_start(out[0, t * P:(t + 1) * P, :], out_tok[:, t, :]).then_inc(sem("stored"), 16)
            sp.wait_ge(sem("stored"), 32)

        @block.tensor
        def _(pe):
            mm = nc.tensor.matmul

            def bank_free(g):
                if g >= 2:
                    pe.wait_ge(sem("chunk_out"), g - 1)

            def done(ins):
                ins.then_inc(sem("chunk_done"), 1)

            def linear(g, lhs, rhs, n, k=DC, rows=P, ready=None):
                bank_free(g)
                for i in range(k):
                    if ready:
                        ready(i)
                    last = mm(PS[0:rows, g % 2, 0:n], lhs(i), rhs(i), start=(i == 0), stop=(i == k - 1))
                done(last)

            def split_ready(name):
                pe.wait_ge(sem("w_lo"), SPLIT[name] + 1)

            def pair(name, k, n):
                return (w[:, SPLIT[name] % 2, 0:k * n].rearrange("p (k n) -> p k n", k=k) for w in (w_hi, w_lo))

            def three(out_, hi_w, lo_w, hi_x, lo_x, start, stop):
                mm(out_, hi_w, hi_x, start=start, stop=False)
                mm(out_, hi_w, lo_x, start=False, stop=False)
                return mm(out_, lo_w, hi_x, start=False, stop=stop)

            def chunk(name, m, x, t0=0, ready=None, width=256):
                g = CHUNK[name, m]
                if m == 0:
                    split_ready(name)
                bank_free(g)
                hi_w, lo_w = pair(name, DC, width)
                hi_x, lo_x = x
                n = hi_x.shape[2] - t0
                for i in range(DC):
                    if ready:
                        ready(i)
                    last = three(PS[:, g % 2, 0:n], hi_w[:, i, m * P:(m + 1) * P], lo_w[:, i, m * P:(m + 1) * P],
                                 hi_x[:, i, t0:], lo_x[:, i, t0:], i == 0, i == DC - 1)
                done(last)

            def x_ready(tag):
                return lambda i: pe.wait_ge(sem(f"lo_{tag}"), i + 1)

            def norm_step(tag, c, count, bank, n, first=0):
                pe.wait_ge(sem(f"sq_{tag}"), first + c + 1)
                mm(PS[:, bank, 0:n], ones[:, :], sq[:, (first + c) % 2, 0:n], start=(c == 0),
                   stop=(c == count - 1)).then_inc(sem(f"sum_{tag}"), 1)

            def norm_sum(tag, count, bank, n, first=0):
                for c in range(count):
                    norm_step(tag, c, count, bank, n, first)

            def linear_norm(tag, chunks, n):
                for c, chunk in enumerate(chunks):
                    chunk()
                    if c:
                        norm_step(tag, c - 1, len(chunks), 2, n)
                norm_step(tag, len(chunks) - 1, len(chunks), 2, n)

            X = (x_hi, x_lo)

            pe.wait_ge(sem("const_in"), 16)
            pe.wait_ge(sem("x_in"), 48)
            for c in range(DC):
                g = CHUNK["start", c]
                bank_free(g)
                b = PS[:, g % 2, :]
                nc.tensor.transpose(b[:, 0:META], m_tok[0:META, 0, c * P:(c + 1) * P], ident[0:META, 0:META])
                for t in range(2):
                    last = nc.tensor.transpose(b[:, META + t * P:META + (t + 1) * P],
                                               x_tok[:, t, c * P:(c + 1) * P], ident)
                done(last)
            pe.wait_ge(sem("vec_in"), 16 * (len(VEC_LIST) + 2))
            for j, n in enumerate((N_VEC, TAPS * CC, TAPS * CC)):
                g = CHUNK["start", DC + j]
                bank_free(g)
                done(nc.tensor.transpose(PS[:, g % 2, 0:n], vec_rows[0:n, j, :], ident[0:n, 0:n]))
            g = CHUNK["start", DC + 3]
            bank_free(g)
            for c in range(DC):
                last = nc.tensor.transpose(PS[:, g % 2, c * META:(c + 1) * META],
                                           m_tok[0:META, 1, c * P:(c + 1) * P], ident[0:META, 0:META])
            done(last)

            pe.wait_ge(sem("ones"), 1)
            norm_sum("pre", DC, 2, L)

            for c in range(4):
                chunk(*part("c", c), X, ready=x_ready("pre") if c == 0 else None)
            chunk("kpe", 0, X, width=2 * ROPE)
            norm_sum("cq", 2, 2, L)
            norm_sum("ckv", 2, 3, L)
            wq = [slot(f"wqb{i}")[:, 0:2 * 768].rearrange("p (k h c) -> p k h c", k=2, h=4) for i in range(2)]
            for h in range(HEADS):
                if h % 4 == 0:
                    w_ready(pe, f"wqb{h // 4}")
                linear(CHUNK["wqb", h], lambda i: wq[h // 4][:, i, h % 4, 0:NOPE], lambda i: c_nrm[:, i, META:L], SEQ,
                       k=2, ready=lambda i: pe.wait_ge(sem("c_nrm"), i + 1))
            for hp in range(HEADS // 2):
                g = CHUNK["wqb", HEADS + hp]
                bank_free(g)
                for half in range(2):
                    h = 2 * hp + half
                    for i in range(2):
                        last = mm(PS[half * 64:half * 64 + 64, g % 2, 0:SEQ], wq[h // 4][:, i, h % 4, NOPE:NOPE + ROPE],
                                  c_nrm[:, i, META:L], start=(i == 0), stop=(i == 1))
                done(last)
            wkv = [slot(f"wkvb{i}").rearrange("p (k h c) -> p k h c", k=2, h=4) for i in range(2)]
            for h in range(HEADS):
                if h % 4 == 0:
                    w_ready(pe, f"wkvb{h // 4}")
                linear(CHUNK["wkvb", h], lambda i: wkv[h // 4][:, i, h % 4, 0:NOPE], lambda i: c_nrm[:, 2 + i, :], L,
                       k=2, ready=lambda i: pe.wait_ge(sem("c_nrm"), 2 + i + 1))
            for x, (t0, n) in enumerate(KEY_CHUNKS):
                for half in range(2):
                    linear(CHUNK["wkvb", HEADS + 2 * x + half], lambda i: c_nrm[:, 2 + i, t0:t0 + n],
                           lambda i: wkv[half][:, i, :, NOPE:NOPE + VDIM], 4 * VDIM, k=2, rows=n)

            def rope(tag, i, src):
                if i >= 2:
                    pe.wait_ge(sem(f"{tag}_rope_out"), i - 1)
                mm(PS[:, 6 + i % 2, 0:src.shape[1]], rotm, src, start=True, stop=True)\
                    .then_inc(sem(f"{tag}_rope"), 1)

            out_of_psum(pe, "wqb", 11)
            for i in range(5):
                rope("mla", i, qpe[:, i, :] if i < 4 else kpe[:, :])

            def attention_step(i, tag, steps, s_mm, v_of, p_buf, pt_buf, o_rows):
                n = len(steps)
                if i < n:
                    if i >= 2:
                        pe.wait_ge(sem(f"{tag}_masked"), i - 1)
                    s_mm(steps[i], PS[:, 2 + i % 2, :]).then_inc(sem(f"{tag}_scores"), 1)
                j = i - 1
                if 0 <= j < n:
                    h, q0, nq, nk = steps[j]
                    pe.wait_ge(sem(f"{tag}_probs"), j + 1)
                    if j >= 2:
                        pe.wait_ge(sem(f"{tag}_pt_out"), j - 1)
                    for x, (k0, kn_) in enumerate(KEY_CHUNKS):
                        m = min(kn_, nk - k0)
                        if m > 0:
                            last = nc.tensor.transpose(PS[0:m, 4 + j % 2, x * P:x * P + nq],
                                                       p_buf[0:nq, j % 2, k0:k0 + m], ident[0:nq, 0:nq])
                    last.then_inc(sem(f"{tag}_pt"), 1)
                j = i - 2
                if 0 <= j < n:
                    h, q0, nq, nk = steps[j]
                    pe.wait_ge(sem(f"{tag}_pt_out"), j + 1)
                    if j >= 2:
                        pe.wait_ge(sem(f"{tag}_o_out"), j - 1)
                    rows = o_rows(h)
                    used = [(x, min(kn_, nk - k0)) for x, (k0, kn_) in enumerate(KEY_CHUNKS) if nk > k0]
                    for x, m in used:
                        last = mm(PS[rows, 6 + j % 2, 0:nq], v_of(h, x, m), pt_buf[0:m, j % 2, x * P:x * P + nq],
                                  start=(x == 0), stop=(x == used[-1][0]))
                    last.then_inc(sem(f"{tag}_o"), 1)

            def mla_scores(step, b):
                h, q0, nq, nk = step
                r = slice(64 * (h % 2), 64 * (h % 2) + 64)
                mm(b[:, 0:nk], qn[:, h, q0 - META:q0 - META + nq], kn[:, h, 0:nk], start=True, stop=False)
                return mm(b[:, 0:nk], qpr[r, h // 2, q0 - META:q0 - META + nq], kpr[r, 0:nk], start=False, stop=True)

            pe.wait_ge(sem("mla_roped"), 5)
            out_of_psum(pe, "wkvb", 13)
            for s in range(MLA_N + 2):
                attention_step(s, "mla", MLA_STEPS, mla_scores, lambda h, x, m: vM[0:m, x, h * VDIM:(h + 1) * VDIM],
                               att_p, att_pt, lambda h: slice(0, P))
                if s < MLA_N:
                    for c in (2 * s, 2 * s + 1):
                        chunk(*part("hg", c), X)

            for h in range(HEADS):
                g = CHUNK["vT", h]
                bank_free(g)
                b = PS[:, g % 2, :]
                for t in range(2):
                    nc.tensor.transpose(b[:, t * P:(t + 1) * P], hi[:, h, META + t * P:META + (t + 1) * P], ident)
                done(nc.tensor.transpose(b[0:META, 2 * P:3 * P], hi[:, h, 0:META], ident))
                if h % 2:
                    chunk(*part("gate", h // 2), X, META)
            for lv in range(LEVELS + 1):
                for half in range(2):
                    pe.wait_ge(sem("level_ready"), 2 * lv + half + 1)
                    for b in range(2):
                        if lv:
                            pe.wait_ge(sem("level_masked"), 4 * (lv - 1) + 2 * half + b + 1)
                        for j in range(4):
                            h, t = divmod(8 * half + 4 * b + j, 2)
                            tok = slice(META + t * P, META + (t + 1) * P)
                            last = mm(PS[:, 2 + 2 * half + b, j * P:(j + 1) * P], hk[:, h, tok], hq[:, h, tok],
                                      start=True, stop=True)
                        last.then_inc(sem("level_done"), 1)
                    if 2 * lv + half < 12:
                        chunk(*part("gate", 4 + 2 * lv + half), X, META)
            pe.wait_ge(sem("level_ready"), 2 * LEVELS + 4)
            for h in range(HEADS):
                g = CHUNK["kT", h]
                bank_free(g)
                nc.tensor.transpose(PS[:, g % 2, 0:P], hk[:, h, META:META + P], ident)
                done(nc.tensor.transpose(PS[0:META, g % 2, P:2 * P], hk[:, h, 0:META], ident))
                if h % 2:
                    chunk(*part("mlo", h // 2), X, META, ready=x_ready("mla") if h == 1 else None)
            for h in range(HEADS):
                g = CHUNK["S", h]
                bank_free(g)
                out_of_psum(pe, "kT", h)
                mm(PS[:, g % 2, 0:P], kT_meta[0:META, h, :], v_meta[0:META, h * P:(h + 1) * P], start=True, stop=True)
                done(mm(PS[:, g % 2, P:2 * P], kT_tok[:, h, :], v_tok[:, 0, h * P:(h + 1) * P], start=True, stop=True))
                if h % 2:
                    chunk(*part("mlo", 4 + h // 2), X, META)
            for h in range(HEADS):
                g = CHUNK["o", h]
                bank_free(g)
                pe.wait_ge(sem("state"), h + 1)
                for t in range(2):
                    b = PS[:, g % 2, t * P:(t + 1) * P]
                    mm(b, v_tok[:, t, h * P:(h + 1) * P], scoresT[:, 2 * h + t, :], start=True, stop=False)
                    last = mm(b, (S1, S2)[t][:, h, :], hq[:, h, META + t * P:META + (t + 1) * P], start=False, stop=True)
                done(last)
            for h in range(HEADS):
                if h >= 2:
                    pe.wait_ge(sem("std_hg"), h - 1)
                norm_sum("hg", 1, 2 + h % 2, SEQ, first=h)

            for c in range(DC):
                chunk(*part("hgo", c), X, META, ready=x_ready("hg") if c == 0 else None)
            linear_norm("post", [lambda c=c: chunk(*part("mix", c), (mix_hi, mix_lo),
                                                   ready=x_ready("mix") if c == 0 else None)
                                 for c in range(DC)], SEQ)
            norm_sum("fpre", DC, 3, SEQ)

            for c in range(4 * FFN_ITEMS):
                chunk(*part("ffi", c), X, META, ready=x_ready("fpre") if c == 0 else None)

            def ffo_chunk(c):
                g = CHUNK["ffo", c]
                bank_free(g)
                for half in range(2):
                    split_ready(f"ffo{2 * c + half}")
                    hi_w, lo_w = pair(f"ffo{2 * c + half}", 11, P)
                    for i in range(11):
                        k = 11 * half + i
                        if c == 0:
                            x_ready("hid")(k)
                        last = three(PS[:, g % 2, 0:SEQ], hi_w[:, i, :], lo_w[:, i, :], hid_hi[:, k, :], hid_lo[:, k, :],
                                     k == 0, k == FC - 1)
                    if half == 0:
                        last.then_inc(sem("half_done"), 1)
                done(last)

            linear_norm("fpost", [lambda c=c: ffo_chunk(c) for c in range(DC)], SEQ)

            for l in range(DEPTH2):
                T = f"L{l}"
                q_from = 0 if l == 0 else META
                n_q = L - q_from
                chunk(f"{T}kw", 0, X, ready=x_ready(f"{T}h"), width=2 * HD + HEADS)
                hi_w, lo_w = pair(f"{T}kw", DC, 2 * HD + HEADS)
                g = CHUNK[f"{T}kw", 1]
                bank_free(g)
                for t in range(2):
                    tok = slice(META + t * P, META + (t + 1) * P)
                    for i in range(DC):
                        last = three(PS[:, g % 2, 8 * t:8 * t + 8], x_hi[:, i, tok], x_lo[:, i, tok],
                                     hi_w[:, i, 2 * HD:], lo_w[:, i, 2 * HD:], i == 0, i == DC - 1)
                done(last)
                for m in range(4):
                    chunk(*part(f"{T}qi", m), X, q_from)
                out_of_psum(pe, *part(f"{T}qi", 3))
                for i in range(5):
                    rope(f"{T}i", i, qiT[:, i, q_from:L] if i < 4 else kiT[:, :])
                pe.wait_ge(sem(f"{T}i_roped"), 5)
                for s in range(16):
                    t, h = divmod(s, HEADS)
                    q0, nq, nk = Q_TILES[t]
                    r = slice(64 * (h % 2), 64 * (h % 2) + 64)
                    if s >= 2:
                        pe.wait_ge(sem(f"{T}relu"), s - 1)
                    mm(PS[:, 2 + s % 2, 0:nk], qir[r, h // 2, q0:q0 + nq], kir[r, 0:nk], start=True, stop=True)\
                        .then_inc(sem(f"{T}idx"), 1)
                    if s % 4 == 3:
                        chunk(*part(f"{T}a", s // 4), X)
                for n, t0 in (("g", 0), ("q", q_from), ("k", 0), ("v", 0)):
                    for m in range(4):
                        chunk(*part(f"{T}{n}", m), X, t0)
                out_of_psum(pe, *part(f"{T}v", 3))
                for x, (t0, n) in enumerate(KEY_CHUNKS):
                    g = CHUNK[f"{T}vt", x]
                    bank_free(g)
                    for c in range(4):
                        last = nc.tensor.transpose(PS[0:n, g % 2, c * P:(c + 1) * P], vT2[:, c, t0:t0 + n], ident)
                    done(last)
                for i in range(8):
                    rope(f"{T}q", i, q2[:, i, q_from:L] if i < 4 else k2[:, i - 4, :])

                def dsa_scores(step, b):
                    h, q0, nq, nk = step
                    r = slice(64 * (h % 2), 64 * (h % 2) + 64)
                    return mm(b[0:nq, 0:nk], q2r[r, h // 2, q0:q0 + nq], k2r[r, h // 2, 0:nk], start=True, stop=True)

                pe.wait_ge(sem(f"{T}q_roped"), 8)
                out_of_psum(pe, f"{T}vt", 2)
                for s in range(DSA_N[l] + 2):
                    attention_step(s, f"{T}att", DSA_STEPS[l], dsa_scores,
                                   lambda h, x, m: v2[0:m, x, h * HD:(h + 1) * HD],
                                   at2_p, at2_pt, lambda h: slice(64 * (h % 2), 64 * (h % 2) + 64))
                    for n, m in z_chunks(l, s):
                        chunk(*part(f"{T}{n}", m), X, q_from)

                def ln_sums(tag, count, bank, src, n, ready):
                    for c in range(count):
                        ready(c)
                        last = mm(PS[:, bank, 0:n], ones[:, :], src(c), start=(c == 0), stop=(c == count - 1))
                    last.then_inc(sem(f"{tag}_mean"), 1)
                    norm_sum(tag, count, bank + 1, n)

                ln_sums(f"{T}cln", CC, 2, lambda c: acc[:, c, q_from:L], L - q_from,
                        lambda c: pe.wait_ge(sem(f"{T}tap"), CC * (TAPS - 1) + c + 1))
                for c in range(DC):
                    chunk(*part(f"{T}wo", c), X, q_from, ready=x_ready(f"{T}y") if c == 0 else None)
                ln_sums(f"{T}pln", DC, 4, lambda c: zT[:, c, q_from:L], L - q_from,
                        lambda c: pe.wait_ge(sem(f"{T}pln_in"), c + 1))

            pe.wait_ge(sem("h_post"), DC * DEPTH2)
            for t in range(2):
                for half in range(2):
                    g = CHUNK["out", 2 * t + half]
                    bank_free(g)
                    for c in range(4):
                        last = nc.tensor.transpose(PS[:, g % 2, c * P:(c + 1) * P],
                                                   hT[:, 4 * half + c, META + t * P:META + (t + 1) * P], ident)
                    done(last)

        @block.gpsimd
        def _(pool):
            sub = nc.gpsimd.tensor_tensor

            def lo_items(first, last):
                for i in range(SPLIT[first], SPLIT[last] + 1):
                    n = SPLIT_ORDER[i]
                    size = split_size(n)
                    pool.wait_ge(sem("w_hi"), i + 1)
                    sub(w_lo[:, i % 2, 0:size], slot(n)[:, 0:size], w_hi[:, i % 2, 0:size], ALU.subtract)\
                        .then_inc(sem("w_lo"), 1)

            def lo_x(tag, c, dst, src, hi_):
                pool.wait_ge(sem(f"hi_{tag}"), c + 1)
                sub(dst, src, hi_, ALU.subtract).then_inc(sem(f"lo_{tag}"), 1)

            lo_items("c0", "c1")
            for c in range(DC):
                lo_x("pre", c, x_lo[:, c, :], u_t[:, c % 4, :], x_hi[:, c, :])
            lo_items("kpe", "mlo1")
            for h in range(HEADS):
                lo_x("mla", h, x_lo[:, h, META:L], o_mla[:, h, :], x_hi[:, h, META:L])
            lo_items("mlo2", "hgo1")
            for h in range(HEADS):
                lo_x("hg", h, x_lo[:, h, META:L], y_hg[:, h, :], x_hi[:, h, META:L])
            lo_items("hgo2", "hgo3")
            for c in range(DC):
                if c == 6:
                    lo_items("mix0", "mix0")
                lo_x("mix", c, mix_lo[:, c, :], ya[:, c, :], mix_hi[:, c, :])
            lo_items("mix1", "ffi1")
            for c in range(DC):
                lo_x("fpre", c, x_lo[:, c, META:L], u_t[:, c % 4, 0:SEQ], x_hi[:, c, META:L])
            for j in range(0, FC, 2):
                if j + 3 < FC:
                    lo_items(f"ffi{j + 2}", f"ffi{j + 3}")
                else:
                    lo_items("ffo0", "ffo1")
                for i in (j, j + 1):
                    lo_x("hid", i, hid_lo[:, i, :], hid[:, i % 4, :], hid_hi[:, i, :])
            lo_items("ffo2", "L0qi0")
            for l in range(DEPTH2):
                T = f"L{l}"
                q_from = 0 if l == 0 else META
                for c in range(DC):
                    lo_x(f"{T}h", c, x_lo[:, c, :], hT[:, c, :], x_hi[:, c, :])
                lo_items(f"{T}qi1", f"{T}wo1")
                for c in range(DC):
                    lo_x(f"{T}y", c, x_lo[:, c, q_from:L], ycat[:, c, q_from:L], x_hi[:, c, q_from:L])
                lo_items(f"{T}wo2", f"L{l + 1}qi0" if l + 1 < DEPTH2 else f"{T}wo3")

        @block.scalar
        def _(act):
            af = nc.scalar.activation

            at = 0
            for name, n in VEC_LIST:
                v = a[name]
                v = v.rearrange("a b -> (a b)") if len(v.shape) == 2 else v
                act.dma_start(vec_rows[at:at + n, 0, :], v.rearrange("(c p) -> c p", p=P)).then_inc(sem("vec_in"), 16)
                at += n
            for l in range(DEPTH2):
                act.dma_start(vec_rows[0:TAPS * CC, 1 + l, :],
                              a["conv_w_2"][l].rearrange("j (c p) -> (j c) p", p=P)).then_inc(sem("vec_in"), 16)

            def take(name, m, dst, f=ACT.Copy, rows=P, c0=0, n=L, view=None, count=True, **kw):
                g = CHUNK[name, m]
                act.wait_ge(sem("chunk_done"), g + 1)
                src = PS[0:rows, g % 2, c0:c0 + n]
                ins = af(dst, view(src) if view else src, f, **kw)
                if count:
                    ins.then_inc(sem("chunk_out"), 1)
                    if g in ENDS:
                        round_item(SPLIT[ENDS[g]] + 2)

            def round_item(i):
                if i < len(SPLIT):
                    n = SPLIT_ORDER[i]
                    w_ready(act, n)
                    af(w_hi[:, i % 2, 0:split_size(n)], slot(n)[:, 0:split_size(n)], ACT.Copy).then_inc(sem("w_hi"), 1)

            def squares(tag, c, src, wait, n):
                wait()
                if c >= 2:
                    act.wait_ge(sem(f"sum_{tag}"), c - 1)
                af(sq[:, c % 2, 0:n], src, ACT.Square).then_inc(sem(f"sq_{tag}"), 1)

            def std(tag, sums, bank_, n, dim, eps, dst, guard=None):
                act.wait_ge(sem(f"sum_{tag}"), sums)
                act.wait_ge(sem("small"), 1)
                if guard:
                    act.wait_ge(*guard)
                af(dst, PS[:, bank_, 0:n], ACT.Sqrt, bias=eps, scale=1.0 / dim).then_inc(sem(f"std_{tag}"), 1)

            round_item(0)
            round_item(1)
            for c in range(DC):
                take("start", c, hT[:, c, :])
            for j, (at, n) in enumerate(((0, N_VEC), (TAP_COL[0], TAPS * CC), (TAP_COL[1], TAPS * CC))):
                take("start", DC + j, cols[:, at:at + n], n=n)
            take("start", DC + 3, vec_rows[:, 0, :], n=P)
            for c in range(DC):
                squares("pre", c, hT[:, c, :], lambda: None, L)
            std("pre", DC, 2, L, D, eps_rms, nrm[:, 0, :])
            act.wait_ge(sem("lb_shift"), 2)
            af(lb_e0, lb_e0, ACT.Exp).then_inc(sem("lb_exp"), 1)
            af(lb_e1, lb_e1, ACT.Exp).then_inc(sem("lb_exp"), 1)

            for i in range(4):
                take(*part("c", i), c_raw[:, i, :])
            take("kpe", 0, kpe)
            for tag, first in (("cq", 0), ("ckv", 2)):
                for c in range(2):
                    def ready():
                        out_of_psum(act, *part("c", first + c))
                        if tag == "ckv":
                            act.wait_ge(sem("sum_cq"), 2)
                    squares(tag, c, c_raw[:, first + c, :], ready, L)
            std("cq", 2, 2, L, LORA, eps_rms, nrm[:, 0, :], guard=(sem("hi_pre"), DC))
            std("ckv", 2, 3, L, LORA, eps_rms, nrm[:, 1, :])
            for h in range(HEADS):
                take("wqb", h, qn[:, h, :], n=SEQ)
            for i in range(4):
                take("wqb", HEADS + i, qpe[:, i, :], n=SEQ)
            for h in range(HEADS):
                take("wkvb", h, kn[:, h, :])
            for x, (t0, n) in enumerate(KEY_CHUNKS):
                for half in range(2):
                    take("wkvb", HEADS + 2 * x + half, vM[0:n, x, half * 512:half * 512 + 512], rows=n, n=512)

            def attention_step(i, tag, steps, s_buf, p_buf, pt_buf, r_buf, o_of):
                n = len(steps)
                if i < n:
                    h, q0, nq, nk = steps[i]
                    act.wait_ge(sem(f"{tag}_masked"), i + 1)
                    if i >= 2:
                        act.wait_ge(sem(f"{tag}_pt"), i - 1)
                    af(p_buf[0:nq, i % 2, 0:nk], s_buf[0:nq, i % 2, 0:nk], ACT.Exp, scale=-1.0,
                       bias=r_buf[0:nq, i % 2, 0:1], accum_out=r_buf[0:nq, i % 2, 1:2])\
                        .then_inc(sem(f"{tag}_exp"), 1)
                j = i - 1
                if 0 <= j < n:
                    h, q0, nq, nk = steps[j]
                    act.wait_ge(sem(f"{tag}_pt"), j + 1)
                    if j >= 2:
                        act.wait_ge(sem(f"{tag}_o"), j - 1)
                    whole, rest = nk // P, nk % P
                    if whole:
                        v = pt_buf[:, j % 2, 0:whole * P].rearrange("p (x q) -> p x q", q=P)[:, :, 0:nq]
                        s = PS[:, 4 + j % 2, 0:whole * P].rearrange("p (x q) -> p x q", q=P)[:, :, 0:nq]
                        af(v, s, ACT.Copy)
                    af(pt_buf[0:rest, j % 2, whole * P:whole * P + nq],
                       PS[0:rest, 4 + j % 2, whole * P:whole * P + nq], ACT.Copy).then_inc(sem(f"{tag}_pt_out"), 1)
                j = i - 2
                if 0 <= j < n:
                    h, q0, nq, nk = steps[j]
                    act.wait_ge(sem(f"{tag}_o"), j + 1)
                    dst, rows = o_of(h, q0, nq)
                    af(dst, PS[rows, 6 + j % 2, 0:nq], ACT.Copy).then_inc(sem(f"{tag}_o_out"), 1)
                if i < n:
                    h, q0, nq, nk = steps[i]
                    act.wait_ge(sem(f"{tag}_inv"), i + 1)
                    af(p_buf[0:nq, i % 2, 0:nk], p_buf[0:nq, i % 2, 0:nk], ACT.Copy,
                       scale=r_buf[0:nq, i % 2, 1:2]).then_inc(sem(f"{tag}_probs"), 1)

            hg_out = [(hq, ACT.Silu), (hf, ACT.Sigmoid), (hi, ACT.Copy), (hg, ACT.Silu)]
            for s in range(MLA_N + 2):
                attention_step(s, "mla", MLA_STEPS, att_s, att_p, att_pt, att_r,
                               lambda h, q0, nq: (o_mla[:, h, q0 - META:q0 - META + nq], slice(0, P)))
                if s < MLA_N:
                    for c in (2 * s, 2 * s + 1):
                        dst, f = hg_out[c // HEADS]
                        off = META if dst is hg else 0
                        take(*part("hg", c), dst[:, c % HEADS, :], f, c0=off, n=L - off)

            def take_gate(c):
                take(*part("gate", c), gates[:, c, :], ACT.Sigmoid, n=SEQ, bias=vec("b_gate", c))

            act.wait_ge(sem("mla_probs"), MLA_N)
            act.wait_ge(sem("mla_o"), MLA_N)
            for h in range(HEADS):
                take("vT", h, v_tok[:, :, h * P:(h + 1) * P], n=2 * P,
                     view=lambda s: s.rearrange("p (t n) -> p t n", t=2), count=False)
                take("vT", h, v_meta[0:META, h * P:(h + 1) * P], rows=META, c0=2 * P, n=P)
                if h % 2:
                    take_gate(h // 2)
            for c in range(4, 16):
                take_gate(c)
            for h in range(HEADS):
                take("kT", h, kT_tok[:, h, :], n=P, count=False)
                take("kT", h, kT_meta[0:META, h, :], rows=META, c0=P, n=P)
                if h % 2:
                    take(*part("mlo", h // 2), y_mla[:, h // 2, :], n=SEQ)
            for h in range(HEADS):
                take("S", h, S1[:, h, :], n=P, count=False)
                take("S", h, S2[:, h, :], c0=P, n=P)
                if h % 2:
                    take(*part("mlo", 4 + h // 2), y_mla[:, 4 + h // 2, :], n=SEQ)
            for h in range(HEADS):
                take("o", h, o_h[:, h, :], n=SEQ)

            for h in range(HEADS):
                squares("hg", h, o_h[:, h, :], lambda: out_of_psum(act, "o", h), SEQ)
                std("hg", h + 1, 2 + h % 2, SEQ, P, eps_rms, nrm[:, h % 2, 0:SEQ],
                    guard=(sem("y_hg"), h - 1) if h >= 2 else None)
            act.wait_ge(sem("y_hg"), HEADS)
            for c in range(DC):
                take(*part("hgo", c), ya[:, c, :], n=SEQ)
            for c in range(DC):
                take(*part("mix", c), mixed[:, c, :], n=SEQ)
                squares("post", c, mixed[:, c, :], lambda: out_of_psum(act, *part("mix", c)), SEQ)
            std("post", DC, 2, SEQ, D, eps_rms, nrm[:, 0, 0:SEQ])
            for c in range(DC):
                def ready():
                    act.wait_ge(sem("h_mid"), c + 1)
                    act.wait_ge(sem("sum_post"), DC)
                squares("fpre", c, hT[:, c, META:L], ready, SEQ)
            std("fpre", DC, 3, SEQ, D, eps_rms, nrm[:, 1, 0:SEQ])
            for j in range(FC):
                if j >= 4:
                    act.wait_ge(sem("lo_hid"), j - 3)
                take(*ffi_chunk(j, 0), hid[:, j % 4, :], ACT.Silu, n=SEQ)
                if j % 2:
                    for i in (j - 1, j):
                        if i >= 2:
                            act.wait_ge(sem("hi_hid"), i - 1)
                        take(*ffi_chunk(i, 1), up[:, i % 2, :], n=SEQ)
            for c in range(DC):
                act.wait_ge(sem("half_done"), c + 1)
                round_item(SPLIT[f"ffo{2 * c}"] + 2)
                take("ffo", c, ffo[:, c, :], n=SEQ)
                round_item(SPLIT[f"ffo{2 * c + 1}"] + 2)
                squares("fpost", c, ffo[:, c, :], lambda: out_of_psum(act, "ffo", c), SEQ)
            std("fpost", DC, 2, SEQ, D, eps_rms, nrm[:, 0, 0:SEQ])

            for l in range(DEPTH2):
                T = f"L{l}"
                q_from = 0 if l == 0 else META
                n_q = L - q_from
                take(f"{T}kw", 0, kiT)
                take(f"{T}kw", 1, idx_w, n=16, view=lambda s: s.rearrange("p (t n) -> p t n", t=2), scale=IDX_W_SCALE)
                for i in range(4):
                    take(*part(f"{T}qi", i), qiT[:, i, q_from:L], n=n_q)
                for s in range(16):
                    t, h = divmod(s, HEADS)
                    nk = Q_TILES[t][2]
                    act.wait_ge(sem(f"{T}idx"), s + 1)
                    if s >= 2:
                        act.wait_ge(sem(f"{T}score"), s - 1)
                    af(relu[:, s % 2, 0:nk], PS[:, 2 + s % 2, 0:nk], ACT.Relu, scale=IDX_SCALE)\
                        .then_inc(sem(f"{T}relu"), 1)
                    if s % 4 == 3:
                        take(*part(f"{T}a", s // 4), upad[:, s // 4, TAPS - 1:TAPS - 1 + L])
                for c in range(CC):
                    take(*part(f"{T}g", c), gsig[:, c, :], ACT.Sigmoid)
                for i in range(4):
                    take(*part(f"{T}q", i), q2[:, i, q_from:L], n=n_q)
                for i in range(4):
                    take(*part(f"{T}k", i), k2[:, i, :])
                for i in range(4):
                    take(*part(f"{T}v", i), vT2[:, i, :])
                for x, (t0, n) in enumerate(KEY_CHUNKS):
                    take(f"{T}vt", x, v2[0:n, x, :], rows=n, n=512)
                for s in range(DSA_N[l] + 2):
                    attention_step(s, f"{T}att", DSA_STEPS[l], at2_s, at2_p, at2_pt, at2_r,
                                   lambda h, q0, nq: (ycat[64 * (h % 2):64 * (h % 2) + 64, 4 + h // 2, q0:q0 + nq],
                                                      slice(64 * (h % 2), 64 * (h % 2) + 64)))
                    for n, m in z_chunks(l, s):
                        take(*part(f"{T}{n}", m), (szc if n == "zc" else sza)[:, m, q_from:L], ACT.Silu, n=n_q)

                def ln_std(tag, count, src, bank_, dim):
                    for c in range(count):
                        squares(tag, c, src(c), lambda: act.wait_ge(sem(f"{tag}_centred"), c + 1), n_q)
                    std(tag, count, bank_, n_q, dim, eps_ln, nrm[:, 0, 0:n_q])

                ln_std(f"{T}cln", CC, lambda c: acc[:, c, q_from:L], 3, CONV_C)
                for c in range(CC):
                    act.wait_ge(sem(f"{T}cln_scaled"), c + 1)
                    af(ycat[:, c, q_from:L], acc[:, c, q_from:L], ACT.Silu, scale=vec("conv_ln_g_2", 4 * l + c),
                       bias=vec("conv_ln_b_2", 4 * l + c)).then_inc(sem(f"{T}silu"), 1)
                for c in range(DC):
                    take(*part(f"{T}wo", c), zT[:, c, q_from:L], n=n_q)
                ln_std(f"{T}pln", DC, lambda c: zT[:, c, q_from:L], 5, D)
                for c in range(DC):
                    act.wait_ge(sem(f"{T}pln_scaled"), c + 1)
                    af(hT[:, c, q_from:L], zT[:, c, q_from:L], ACT.Identity, scale=vec("post_ln_g_2", 8 * l + c),
                       bias=vec("post_ln_b_2", 8 * l + c)).then_inc(sem("h_post"), 1)
            for t in range(2):
                for half in range(2):
                    take("out", 2 * t + half, out_tok[:, t, half * 512:half * 512 + 512], n=512)

        @block.vector
        def _(dve):
            v = nc.vector
            order = [0]

            def link(ins):
                order[0] += 1
                ins.then_inc(sem("dve_order"), 1)
                dve.wait_ge(sem("dve_order"), order[0])

            v.memset(ones[:, :], 1.0).then_inc(sem("ones"), 1)
            v.memset(small[:, 0:1], EPS_RMS)
            v.memset(small[:, 1:2], EPS_LN).then_inc(sem("small"), 1)
            out_of_psum(dve, "start", DC)
            l0 = cols[:, VEC["lb_logits"]:VEC["lb_logits"] + 8]
            l1 = cols[:, VEC["lb_logits"] + 8:VEC["lb_logits"] + 16]
            link(v.tensor_tensor(lb_m, l0, l1, ALU.max))
            v.tensor_tensor(lb_e0, l0, lb_m, ALU.subtract).then_inc(sem("lb_shift"), 1)
            v.tensor_tensor(lb_e1, l1, lb_m, ALU.subtract).then_inc(sem("lb_shift"), 1)

            def rstd(tag, count, buf):
                dve.wait_ge(sem(f"std_{tag}"), count)
                link(v.reciprocal(buf, buf))

            def split(tag, dst, src):
                v.tensor_copy(dst, src).then_inc(sem(f"hi_{tag}"), 1)

            def norm_split(tag, name, src, rs, n, t0):
                for c in range(DC):
                    if c >= 4:
                        dve.wait_ge(sem(f"lo_{tag}"), c - 3)
                    link(v.scalar_tensor_tensor(out=u_t[:, c % 4, 0:n], in0=src(c), scalar=vec(name, c), in1=rs,
                                                op0=ALU.mult, op1=ALU.mult))
                    split(tag, x_hi[:, c, t0:t0 + n], u_t[:, c % 4, 0:n])

            rstd("pre", 1, nrm[:, 0, :])
            norm_split("pre", "mix_pre_g", lambda c: hT[:, c, :], nrm[:, 0, :], L, 0)
            dve.wait_ge(sem("lb_exp"), 2)
            link(v.tensor_tensor(lb_m, lb_e0, lb_e1, ALU.add))
            link(v.reciprocal(lb_m, lb_m))
            link(v.tensor_tensor(lb, lb_e0, lb_m, ALU.mult))
            link(v.tensor_scalar(oml, lb, -1.0, 1.0, ALU.mult, ALU.add))

            for tag, b, first, name in (("cq", 0, 0, "q_a_norm_g"), ("ckv", 1, 2, "kv_a_norm_g")):
                rstd(tag, 1, nrm[:, b, :])
                for c in range(2):
                    v.scalar_tensor_tensor(out=c_nrm[:, first + c, :], in0=c_raw[:, first + c, :],
                                           scalar=vec(name, c), in1=nrm[:, b, :],
                                           op0=ALU.mult, op1=ALU.mult).then_inc(sem("c_nrm"), 1)

            def rope(tag, i, src, dst, t0, n, ta, tb):
                v.tensor_tensor(ta[:, i % 2, 0:n], src, cosT[:, t0:t0 + n], ALU.mult)
                dve.wait_ge(sem(f"{tag}_rope"), i + 1)
                v.tensor_tensor(tb[:, i % 2, 0:n], PS[:, 6 + i % 2, 0:n], sinT[:, t0:t0 + n], ALU.mult)\
                    .then_inc(sem(f"{tag}_rope_out"), 1)
                dve.wait_ge(sem(f"{tag}_rope_out"), i + 1)
                v.tensor_tensor(dst, ta[:, i % 2, 0:n], tb[:, i % 2, 0:n], ALU.add).then_inc(sem(f"{tag}_roped"), 1)

            dve.wait_ge(sem("tables_in"), 16)
            out_of_psum(dve, "wqb", 11)
            for i in range(4):
                rope("mla", i, qpe[:, i, :], qpr[:, i, :], META, SEQ, rope_a, rope_b)
            rope("mla", 4, kpe, kpr, 0, L, rope_a, rope_b)

            def attention_step(i, tag, steps, scale, mask_of, s_buf, r_buf):
                if i < len(steps):
                    h, q0, nq, nk = steps[i]
                    dve.wait_ge(sem(f"{tag}_scores"), i + 1)
                    if i >= 2:
                        dve.wait_ge(sem(f"{tag}_exp"), i - 1)
                        dve.wait_ge(sem(f"{tag}_probs"), i - 1)
                    v.tensor_tensor_reduce(out=s_buf[0:nq, i % 2, 0:nk], in0=PS[0:nq, 2 + i % 2, 0:nk],
                                           in1=mask_of(q0, nq, nk), scale=-scale, scalar=BIG,
                                           op0=ALU.add, op1=ALU.min,
                                           accum_out=r_buf[0:nq, i % 2, 0:1]).then_inc(sem(f"{tag}_masked"), 1)
                    dve.wait_ge(sem(f"{tag}_exp"), i + 1)
                    v.reciprocal(r_buf[0:nq, i % 2, 1:2], r_buf[0:nq, i % 2, 1:2]).then_inc(sem(f"{tag}_inv"), 1)

            def forget(h):
                out_of_psum(dve, *part("hg", HEADS + h))
                v.tensor_scalar(hf[:, h, :], hf[:, h, :], oml[:, h:h + 1], lb[:, h:h + 1], ALU.mult, ALU.add)\
                    .then_inc(sem("f_ready"), 1)

            for s in range(MLA_N):
                attention_step(s, "mla", MLA_STEPS, MLA_SCALE, lambda q0, nq, nk: cst(CAUSAL[q0])[0:nq, :], att_s, att_r)
                if 8 <= s < 8 + HEADS:
                    forget(s - 8)

            dve.wait_ge(sem("mla_o"), MLA_N)
            dve.wait_ge(sem("f_ready"), HEADS)
            for half in range(2):
                s = slice(1088 * half, 1088 * half + 1088)
                v.tensor_scalar(flat["k"][:, s], flat["f"][:, s], -1.0, 1.0, ALU.mult, ALU.add)\
                    .then_inc(sem("level_ready"), 1)
            out_of_psum(dve, "vT", HEADS - 1)
            lvl = cst("level").rearrange("p (l n) -> p l n", n=P)
            blocks = [flat["f"]]
            at = 0
            for lv in range(4):
                n = HEADS * L >> (lv + 1)
                blocks.append(tree[:, at:at + n])
                at += n
            t16 = blocks[4].rearrange("p (h b) -> p h b", h=HEADS)
            t32, t64, t128 = (tree[:, at + o:at + o + 8 * n].rearrange("p (h b) -> p h b", h=HEADS)
                              for o, n in ((0, 8), (64, 4), (96, 2)))
            for lv in range(LEVELS + 1):
                for half in range(2):
                    if 2 * lv + half >= 12:
                        if 2 * lv + half == 12:
                            dve.wait_ge(sem("chunk_done"), CHUNK["gate7", 1] + 1)
                        for h in range(2 * (2 * lv + half - 12), 2 * (2 * lv + half - 12) + 2):
                            split("mla", x_hi[:, h, META:L], o_mla[:, h, :])
                    for b in range(2):
                        i = 4 * lv + 2 * half + b
                        dve.wait_ge(sem("level_done"), i + 1)
                        dst = scoresT[:, 8 * half + 4 * b:8 * half + 4 * b + 4, :]
                        src = PS[:, 2 + 2 * half + b, :].rearrange("p (j n) -> p j n", n=P)
                        m = lvl[:, lv:lv + 1, :].to_broadcast([P, 4, P])
                        if lv == 0:
                            v.tensor_tensor(dst, src, m, ALU.mult).then_inc(sem("level_masked"), 1)
                        else:
                            v.copy_predicated(dst, m.bitcast(U32), src).then_inc(sem("level_masked"), 1)
                    hs = slice(4 * half, 4 * half + 4)
                    if lv == 0:
                        v.tensor_tensor(flat["q"][:, 1088 * half:1088 * half + 1088],
                                        flat["q"][:, 1088 * half:1088 * half + 1088],
                                        flat["f"][:, 1088 * half:1088 * half + 1088], ALU.mult)\
                            .then_inc(sem("level_ready"), 1)
                        continue
                    B = 1 << (lv - 1)
                    if B < 16:
                        n = 1088 // (2 * B)
                        view = lambda x: x[:, 1088 * half:1088 * half + 1088].rearrange("p (n u b) -> p n u b", u=2, b=B)
                        qv, kv = view(flat["q"]), view(flat["k"])
                        tot = blocks[lv - 1][:, n * 2 * half:n * 2 * half + 2 * n].rearrange("p (n u) -> p n u", u=2)
                        nxt = blocks[lv][:, n * half:n * half + n]
                        lo = tot[:, :, 0:1].to_broadcast([P, n, B])
                        hi_ = tot[:, :, 1:2].to_broadcast([P, n, B])
                        q_up, k_lo = qv[:, :, 1, :], kv[:, :, 0, :]
                        lo1, hi1 = tot[:, :, 0], tot[:, :, 1]
                    else:
                        n = SEQ // (2 * B)
                        view = lambda x: x[:, hs, META:L].rearrange("p h (n u b) -> p h n u b", u=2, b=B)
                        qv, kv = view(hq), view(hk)
                        tot = {16: t16[:, hs, 1:17], 32: t32[:, hs, :], 64: t64[:, hs, :]}[B]
                        tot = tot.rearrange("p h (n u) -> p h n u", u=2)
                        nxt = {16: t32, 32: t64, 64: t128}[B][:, hs, :]
                        lo = tot[:, :, :, 0:1].to_broadcast([P, 4, n, B])
                        hi_ = tot[:, :, :, 1:2].to_broadcast([P, 4, n, B])
                        q_up, k_lo = qv[:, :, :, 1, :], kv[:, :, :, 0, :]
                        lo1, hi1 = tot[:, :, :, 0], tot[:, :, :, 1]
                    v.tensor_tensor(q_up, q_up, lo, ALU.mult)
                    link(v.tensor_tensor(nxt, lo1, hi1, ALU.mult))
                    v.tensor_tensor(k_lo, k_lo, hi_, ALU.mult).then_inc(sem("level_ready"), 1)
            for h in range(HEADS):
                out_of_psum(dve, "S", h)
                v.scalar_tensor_tensor(out=S2[:, h, :], in0=S1[:, h, :], scalar=t128[:, h, 0:1], in1=S2[:, h, :],
                                       op0=ALU.mult, op1=ALU.add).then_inc(sem("state"), 1)
            for c in range(DC):
                out_of_psum(dve, *part("mlo", c))
                v.tensor_tensor(y_mla[:, c, :], y_mla[:, c, :], gates[:, DC + c, :], ALU.mult)\
                    .then_inc(sem("b_gated"), 1)
            out_of_psum(dve, "o", HEADS - 1)
            dve.wait_ge(sem("chunk_done"), CHUNK["mlo3", 1] + 1)
            for h in range(HEADS):
                rstd("hg", h + 1, nrm[:, h % 2, 0:SEQ])
                link(v.scalar_tensor_tensor(out=o_h[:, h, :], in0=o_h[:, h, :], scalar=vec("hg_norm_g", 0),
                                            in1=nrm[:, h % 2, 0:SEQ], op0=ALU.mult, op1=ALU.mult))
                v.tensor_tensor(y_hg[:, h, :], o_h[:, h, :], hg[:, h, :], ALU.mult).then_inc(sem("y_hg"), 1)
                dve.wait_ge(sem("y_hg"), h + 1)
                split("hg", x_hi[:, h, META:L], y_hg[:, h, :])

            dve.wait_ge(sem("b_gated"), DC)
            for c in range(DC):
                out_of_psum(dve, *part("hgo", c))
                link(v.tensor_tensor(ya[:, c, :], ya[:, c, :], gates[:, c, :], ALU.mult))
                link(v.tensor_tensor(ya[:, c, :], ya[:, c, :], y_mla[:, c, :], ALU.add))
                split("mix", mix_hi[:, c, :], ya[:, c, :])
            rstd("post", 1, nrm[:, 0, 0:SEQ])
            for c in range(DC):
                link(v.scalar_tensor_tensor(out=mixed[:, c, :], in0=mixed[:, c, :], scalar=vec("mix_post_g", c),
                                            in1=nrm[:, 0, 0:SEQ], op0=ALU.mult, op1=ALU.mult))
                v.tensor_tensor(hT[:, c, META:L], hT[:, c, META:L], mixed[:, c, :], ALU.add).then_inc(sem("h_mid"), 1)
            rstd("fpre", 1, nrm[:, 1, 0:SEQ])
            norm_split("fpre", "ffn_pre_g", lambda c: hT[:, c, META:L], nrm[:, 1, 0:SEQ], SEQ, META)
            for j in range(FC):
                out_of_psum(dve, *ffi_chunk(j, 1))
                link(v.tensor_tensor(hid[:, j % 4, :], hid[:, j % 4, :], up[:, j % 2, :], ALU.mult))
                split("hid", hid_hi[:, j, :], hid[:, j % 4, :])
            rstd("fpost", 1, nrm[:, 0, 0:SEQ])
            link(v.tensor_copy(hT[:, :, 0:META], vec_rows[:, 0, :].rearrange("p (c t) -> p c t", c=DC)))
            for c in range(DC):
                link(v.scalar_tensor_tensor(out=ffo[:, c, :], in0=ffo[:, c, :], scalar=vec("ffn_post_g", c),
                                            in1=nrm[:, 0, 0:SEQ], op0=ALU.mult, op1=ALU.mult))
                v.tensor_tensor(hT[:, c, META:L], hT[:, c, META:L], ffo[:, c, :], ALU.add).then_inc(sem("h_ready"), 1)
                dve.wait_ge(sem("h_ready"), c + 1)
                split("L0h", x_hi[:, c, :], hT[:, c, :])

            v.memset(upad[:, :, 0:TAPS - 1], 0.0)
            v.memset(top8[:, :, :], NEG)
            for l in range(DEPTH2):
                T = f"L{l}"
                q_from = 0 if l == 0 else META
                n_all = L - q_from
                if l:
                    for c in range(DC):
                        dve.wait_ge(sem("h_post"), c + 1)
                        split(f"{T}h", x_hi[:, c, :], hT[:, c, :])
                out_of_psum(dve, *part(f"{T}qi", 3))
                for i in range(4):
                    rope(f"{T}i", i, qiT[:, i, q_from:L], qir[:, i, q_from:L], q_from, n_all, rope2_a, rope2_b)
                rope(f"{T}i", 4, kiT, kir, 0, L, rope2_a, rope2_b)
                for s in range(16):
                    t, h = divmod(s, HEADS)
                    q0, nq, nk = Q_TILES[t]
                    dve.wait_ge(sem(f"{T}relu"), s + 1)
                    if s:
                        dve.wait_ge(sem(f"{T}score"), s)
                    v.scalar_tensor_tensor(out=score[:, t, 0:nk], in0=relu[:, s % 2, 0:nk], scalar=idx_w[:, t, h:h + 1],
                                           in1=cst(CAUSAL[q0]) if h == 0 else score[:, t, 0:nk],
                                           op0=ALU.mult, op1=ALU.add).then_inc(sem(f"{T}score"), 1)
                dve.wait_ge(sem(f"{T}score"), 16)
                for r in range(ROUNDS):
                    for t in range(2):
                        nk = Q_TILES[t][2]
                        v.max(top8[:, t, :], score[:, t, 0:nk]).then_inc(sem(f"{T}top"), 1)
                    for t in range(2):
                        nk = Q_TILES[t][2]
                        dve.wait_ge(sem(f"{T}top"), 4 * r + 2 if r < ROUNDS - 1 else 4 * r + 2)
                        if r == ROUNDS - 1 and TOPK % 8:
                            link(v.memset(top8[:, t, TOPK % 8:8], NEG))
                        v.match_replace(score[:, t, 0:nk], in_to_replace=top8[:, t, :], in_values=score[:, t, 0:nk],
                                        imm_value=NEG).then_inc(sem(f"{T}top"), 1)
                    dve.wait_ge(sem(f"{T}top"), 4 * r + 4)
                for t in range(2):
                    q0, nq, nk = Q_TILES[t]
                    link(v.tensor_scalar(sel[:, t, 0:nk], score[:, t, 0:nk], NEG, NEG, ALU.not_equal, ALU.mult))
                    link(v.tensor_tensor(sel[:, t, 0:nk], sel[:, t, 0:nk], cst(CAUSAL[q0]), ALU.min))

                for c in range(CC):
                    out_of_psum(dve, *part(f"{T}g", c))
                    link(v.tensor_tensor(upad[:, c, TAPS - 1:TAPS - 1 + L], upad[:, c, TAPS - 1:TAPS - 1 + L],
                                         gsig[:, c, :], ALU.mult))

                def tap(j):
                    for c in range(CC):
                        w = cols[:, TAP_COL[l] + CC * j + c:TAP_COL[l] + CC * j + c + 1]
                        if j == 0:
                            ins = v.tensor_scalar(acc[:, c, :], upad[:, c, 0:L], w, vec("conv_b_2", 4 * l + c),
                                                  ALU.mult, ALU.add)
                        else:
                            dve.wait_ge(sem(f"{T}tap"), CC * (j - 1) + c + 1)
                            ins = v.scalar_tensor_tensor(out=acc[:, c, :], in0=upad[:, c, j:j + L], scalar=w,
                                                         in1=acc[:, c, :], op0=ALU.mult, op1=ALU.add)
                        ins.then_inc(sem(f"{T}tap"), 1)

                first_taps = TAPS - 24
                for j in range(first_taps):
                    tap(j)
                for i in range(8):
                    src, dst = (q2, q2r) if i < 4 else (k2, k2r)
                    t0 = q_from if i < 4 else 0
                    out_of_psum(dve, *part(f"{T}{'q' if i < 4 else 'k'}", i % 4))
                    rope(f"{T}q", i, src[:, i % 4, t0:L], dst[:, i % 4, t0:L], t0, L - t0, rope2_a, rope2_b)
                for s in range(DSA_N[l]):
                    attention_step(s, f"{T}att", DSA_STEPS[l], ATT_SCALE,
                                   lambda q0, nq, nk: cst("causal_m")[0:nq, :] if q0 == 0
                                   else sel[:, (q0 - META) // P, 0:nk], at2_s, at2_r)
                    for j in range(s * 24 // DSA_N[l], (s + 1) * 24 // DSA_N[l]):
                        tap(first_taps + j)

                def centre(tag, count, src, bank_, dim):
                    dve.wait_ge(sem(f"{tag}_mean"), 1)
                    mean = nrm[:, 1, 0:n_all]
                    link(v.tensor_scalar(mean, PS[:, bank_, 0:n_all], 1.0 / dim, None, ALU.mult))
                    for c in range(count):
                        v.tensor_tensor(src(c), src(c), mean, ALU.subtract).then_inc(sem(f"{tag}_centred"), 1)
                    rstd(tag, 1, nrm[:, 0, 0:n_all])
                    dve.wait_ge(sem(f"sq_{tag}"), count)
                    for c in range(count):
                        v.tensor_tensor(src(c), src(c), nrm[:, 0, 0:n_all], ALU.mult).then_inc(sem(f"{tag}_scaled"), 1)

                dve.wait_ge(sem("chunk_done"), CHUNK[f"{T}za1", 1] + 1)
                centre(f"{T}cln", CC, lambda c: acc[:, c, q_from:L], 2, CONV_C)
                for c in range(CC):
                    dve.wait_ge(sem(f"{T}silu"), c + 1)
                    link(v.tensor_tensor(ycat[:, c, q_from:L], ycat[:, c, q_from:L], szc[:, c, q_from:L], ALU.mult))
                    split(f"{T}y", x_hi[:, c, q_from:L], ycat[:, c, q_from:L])
                dve.wait_ge(sem(f"{T}att_o_out"), len(DSA_STEPS[l]))
                for c in range(CC):
                    link(v.tensor_tensor(ycat[:, CC + c, q_from:L], ycat[:, CC + c, q_from:L], sza[:, c, q_from:L],
                                         ALU.mult))
                    split(f"{T}y", x_hi[:, CC + c, q_from:L], ycat[:, CC + c, q_from:L])
                for c in range(DC):
                    out_of_psum(dve, *part(f"{T}wo", c))
                    v.scalar_tensor_tensor(out=zT[:, c, q_from:L], in0=hT[:, c, q_from:L], scalar=ALPHA,
                                           in1=zT[:, c, q_from:L], op0=ALU.mult, op1=ALU.add)\
                        .then_inc(sem(f"{T}pln_in"), 1)
                dve.wait_ge(sem(f"{T}pln_in"), DC)
                centre(f"{T}pln", DC, lambda c: zT[:, c, q_from:L], 4, D)


_INS = ["x", "meta_tokens", "w_in", "b_gate", "lb_logits", "hg_norm_g", "w_hg_o", "q_a_norm_g", "w_q_b",
        "kv_a_norm_g", "w_kv_b", "w_mla_o", "w_out", "mix_pre_g", "mix_post_g", "ffn_pre_g", "ffn_post_g",
        "w_ffn_in", "w_ffn_out", "meta_tokens_2", "w_in_2", "conv_w_2", "conv_b_2", "conv_ln_g_2",
        "conv_ln_b_2", "w_out_2", "post_ln_g_2", "post_ln_b_2"]


def kernel(**inputs):
    import numpy as _np
    import concourse.bacc as _bacc
    from concourse import mybir as _mybir
    from concourse.bass_utils import run_bass_kernel_spmd as _run

    nc = _bacc.Bacc("TRN2", target_bir_lowering=False, num_devices=1)
    arrays, args = {}, {}
    for name in _INS + ["constants"]:
        arr = shape_constants() if name == "constants" else _np.ascontiguousarray(inputs[name])
        arrays[f"in_{name}"] = arr
        args[name] = nc.dram_tensor(f"in_{name}", arr.shape, _mybir.dt.from_np(arr.dtype), kind="ExternalInput").ap()
    out = nc.dram_tensor("out", (1, SEQ, D), F32, kind="ExternalOutput").ap()
    bass_blocks(nc, args, out)
    r = _run(nc, [arrays], core_ids=[0])
    return r.results[0]["out"]
```

```python
from contextlib import ExitStack

import numpy as np

import concourse.bass as bass
from concourse import mybir

F32 = mybir.dt.float32
F32R = mybir.dt.float32r
U32 = mybir.dt.uint32
ALU = mybir.AluOpType
ACT = mybir.ActivationFunctionType

P = 128
META = 16
SEQ = 256
L = META + SEQ
D = 1024
DC = D // P
HEADS = 8
EPS_RMS = 1e-6
EPS_LN = 1e-5
NEG = -3.0e38
BIG = 3.0e38

LORA = 256
NOPE, ROPE, VDIM = 128, 64, 128
MLA_SCALE = float(NOPE + ROPE) ** -0.5
FFN = 2816
FC = FFN // P
FFN_ITEMS = FFN // 256
LEVELS = 7
GATE_COL = 4 * D + 2 * LORA + ROPE

DEPTH2 = 2
CONV_C = 512
CC = CONV_C // P
TAPS = 31
HD = 64
TOPK = min(256, L // 4)
ROUNDS = -(-TOPK // 8)
IDX_SCALE = float(HD) ** -0.5
IDX_W_SCALE = float(HEADS) ** -0.5
ATT_SCALE = float(HD) ** -0.5
ALPHA = (2.0 * DEPTH2) ** 0.25
COL2 = dict(a=0, g=512, zc=1024, q=1536, k=2048, v=2560, za=3072, qi=3584, ki=4096)

KEY_CHUNKS = [(0, 128), (128, 128), (256, 16)]

CONST = {}
_at = 0
for _name, _n in (("ident", P), ("rot", P), ("cos", L), ("sin", L), ("level", (LEVELS + 1) * P),
                  ("causal_m", META), ("causal_0", META + P), ("causal_1", L)):
    CONST[_name] = (_at, _n)
    _at += _n
N_CONST = _at


def shape_constants():
    c = np.zeros((P, N_CONST), np.float32)

    def put(name, a):
        at, n = CONST[name]
        c[:a.shape[0], at:at + n] = a

    put("ident", np.eye(P, dtype=np.float32))
    rot = np.zeros((P, P), np.float32)
    for m in range(P):
        if m % 64 < 32:
            rot[m + 32, m] = -1.0
        else:
            rot[m - 32, m] = 1.0
    put("rot", rot)
    inv = (1.0 / (np.float32(10000.0) ** (np.arange(0, 64, 2, dtype=np.float32) / np.float32(64)))).astype(np.float32)
    ang = np.arange(L, dtype=np.float32)[None, :] * inv[np.arange(P) % 32][:, None]
    put("cos", np.cos(ang).astype(np.float32))
    put("sin", np.sin(ang).astype(np.float32))
    s, t = np.arange(P)[:, None], np.arange(P)[None, :]
    masks = [s == t]
    for lv in range(LEVELS):
        b = 1 << lv
        masks.append((s // (2 * b) == t // (2 * b)) & (s // b % 2 == 0) & (t // b % 2 == 1))
    put("level", np.concatenate(masks, 1).astype(np.float32))
    for name, first, rows in (("causal_m", 0, META), ("causal_0", META, P), ("causal_1", META + P, P)):
        n = CONST[name][1]
        put(name, np.where(np.arange(n)[None, :] <= first + np.arange(rows)[:, None], 0.0, NEG).astype(np.float32))
    return c


VEC_LIST = [("mix_pre_g", 8), ("mix_post_g", 8), ("ffn_pre_g", 8), ("ffn_post_g", 8), ("b_gate", 16),
            ("lb_logits", 16), ("hg_norm_g", 1), ("q_a_norm_g", 2), ("kv_a_norm_g", 2),
            ("conv_b_2", 8), ("conv_ln_g_2", 8), ("conv_ln_b_2", 8), ("post_ln_g_2", 16), ("post_ln_b_2", 16)]
VEC = {}
_at = 0
for _name, _n in VEC_LIST:
    VEC[_name] = _at
    _at += _n
N_VEC = _at
TAP_COL = [N_VEC, N_VEC + TAPS * CC]
N_COLS = N_VEC + 2 * TAPS * CC

SLOTS = 3
ITEM_N = 2048


def items(name, n):
    return [(f"{name}{i}", 1) for i in range(n)]


STREAM = (items("c", 2) + [("kpe", 2)] + items("hg", 2) + items("wqb", 2) + items("wkvb", 2) + items("hg", 16)[2:]
          + items("gate", 8) + items("mlo", 4) + items("hgo", 4) + items("mix", 4)
          + items("ffi", 2 * FFN_ITEMS) + items("ffo", 2 * DC))
for _l in range(DEPTH2):
    STREAM += [(f"L{_l}kw", 2)]
    for _n, _k in (("qi", 2), ("a", 2), ("g", 2), ("q", 2), ("k", 2), ("v", 2), ("zc", 2), ("za", 2), ("wo", 4)):
        STREAM += items(f"L{_l}{_n}", _k)


def pieces(item):
    if item.startswith("ffo"):
        return [(P, 0, 0, 6, P), (P, 6, 0, 5, P)]
    if item == "kpe":
        return [(2 * ROPE, 0, 0, DC, 2 * ROPE)]
    if item[2:] == "kw":
        return [(2 * HD + HEADS, 0, 0, DC, 2 * HD), (2 * HD + HEADS, 0, 2 * HD, DC, HEADS)]
    return [(2 * P, 0, 0, DC, P), (2 * P, 0, P, DC, P)]


PAIRS, PIECE_N = 4, DC * P
PIECES = [(n, m) for n, _ in STREAM if not n.startswith(("wqb", "wkvb")) for m in range(len(pieces(n)))]
SPLIT = {x: i for i, x in enumerate(PIECES)}

MLA_N = 2 * HEADS
DSA_N = [3 * HEADS, 2 * HEADS]
DSA_LAG = 2
CLN_STEP = [DSA_N[0] - 6, DSA_N[1] - 4]


def part(name, c):
    return f"{name}{c // 2}", c % 2


def ffi_chunk(j, up):
    return f"ffi{j // 2 * 2 + up}", j % 2


def z_chunks(l, s):
    n = DSA_N[l] + DSA_LAG + 1
    return [("zc" if z < 4 else "za", z % 4) for z in range(s * 8 // n, (s + 1) * 8 // n)]


ORDER = [("start", i) for i in range(12)]
ORDER += [(n, i) for n, k in (("c0", 2), ("c1", 2), ("kpe", 1), ("wqb", 12), ("wkvb", 14)) for i in range(k)]
ORDER += [part("hg", c) for c in range(32)]
for _h in range(HEADS):
    ORDER += [("vT", _h)] + ([part("gate", _h // 2)] if _h % 2 else [])
ORDER += [part("gate", c) for c in range(4, 16)]
for _h in range(HEADS):
    ORDER += [("kT", _h)] + ([part("mlo", _h // 2)] if _h % 2 else [])
ORDER += [("S", h) for h in range(HEADS)] + [("o", h) for h in range(HEADS)]
ORDER += [part("mlo", c) for c in range(4, DC)]
ORDER += [part(n, c) for n in ("hgo", "mix") for c in range(DC)]
ORDER += [part("ffi", c) for c in range(4 * FFN_ITEMS)] + [("ffo", c) for c in range(DC)]
for _l in range(DEPTH2):
    ORDER += [(f"L{_l}kw", 0), (f"L{_l}kw", 1)]
    ORDER += [part(f"L{_l}{n}", i) for n in ("qi", "a", "g", "q", "k", "v") for i in range(4)]
    ORDER += [(f"L{_l}vt", i) for i in range(3)]
    ORDER += [part(f"L{_l}{n}", i) for s in range(DSA_N[_l] + DSA_LAG + 1) for n, i in z_chunks(_l, s)]
    ORDER += [part(f"L{_l}wo", c) for c in range(DC)]
ORDER += [("out", i) for i in range(4)]
CHUNK = {c: i for i, c in enumerate(ORDER)}
SLOT, USE, PREV = {}, {}, {}
_uses, _last = [0] * SLOTS, [None] * SLOTS
for _i, (_it, _dmas) in enumerate(STREAM):
    _s = _i % SLOTS
    SLOT[_it] = _s
    _uses[_s] += 16 * _dmas
    USE[_it] = _uses[_s]
    PREV[_it] = _last[_s]
    _last[_s] = _it
ENDS = {g: SPLIT[x] for x, g in CHUNK.items() if x in SPLIT}
MLA_USED = dict(wqb0=("wqb", 9), wqb1=("wqb", 11), wkvb0=("wkvb", 12), wkvb1=("wkvb", 13))


def bass_blocks(nc, a, out):
    ctx = ExitStack()
    with ctx:
        def sb(name, shape, dt=F32):
            return ctx.enter_context(nc.sbuf_tensor(name, shape, dt))

        sems = {}

        def sem(name):
            if name not in sems:
                sems[name] = ctx.enter_context(nc.semaphore(name))
            return sems[name]

        ring = sb("ring", [P, SLOTS, ITEM_N])
        w_hi, w_lo = sb("w_hi", [P, PAIRS, PIECE_N], F32R), sb("w_lo", [P, PAIRS, PIECE_N], F32R)
        x_hi, x_lo = sb("x_hi", [P, DC, L], F32R), sb("x_lo", [P, DC, L], F32R)
        u_t = sb("u_t", [P, 4, L])
        const = sb("const", [P, N_CONST])
        MEANS = (D, LORA, P, CONV_C)
        means = sb("means", [P, len(MEANS), P])
        vec_rows = sb("vec_rows", [P, 3, P])
        cols = sb("cols", [P, N_COLS])
        small = sb("small", [P, 64])
        hT = sb("hT", [P, DC, L])
        keep = sb("keep", [P, 2048])
        ZONE_A, ZONE_B = 10752, 13440
        zone_at = nc.sbuf_base
        zoneA = sb("zoneA", [P, ZONE_A])
        zoneB = sb("zoneB", [P, ZONE_B])
        assert nc.sbuf_base == zone_at + 4 * (ZONE_A + ZONE_B)

        def in_zone(name, at, *shape):
            return nc.alloc_sbuf_tensor_at(name, [P, *shape], F32R, offset=zone_at + 4 * at)

        sq = sb("sq", [P, 2, L])
        nrm = sb("nrm", [P, 2, L])
        hg_rs = u_t[:, :, :].rearrange("p a b -> p (a b)")[:, 0:4 * SEQ].rearrange("p (a b) -> p a b", a=2)

        class Zone:
            def __init__(self, t, at=0):
                self.t, self.at = t, at

            def __call__(self, *shape):
                n = int(np.prod(shape))
                v = self.t[:, self.at:self.at + n]
                self.at += n
                if len(shape) == 2:
                    v = v.rearrange("p (a b) -> p a b", b=shape[1])
                if len(shape) == 3:
                    v = v.rearrange("p (a b c) -> p a b c", b=shape[1], c=shape[2])
                return v

        PS = ctx.enter_context(nc.psum_tensor("PS", [P, 8, 512], F32))

        def cst(name, rows=P):
            at, n = CONST[name]
            return const[0:rows, at:at + n]

        ident, rotm, cosT, sinT = cst("ident"), cst("rot"), cst("cos"), cst("sin")

        def vec(name, c):
            return cols[:, VEC[name] + c:VEC[name] + c + 1]

        eps_rms, eps_ln = small[:, 0:1], small[:, 1:2]
        lb, oml = small[:, 8:16], small[:, 16:24]
        lb_e0, lb_e1, lb_m = small[:, 24:32], small[:, 32:40], small[:, 40:48]

        z = Zone(zoneA)
        hq, hk, hf, hi = z(HEADS, L), z(HEADS, L), z(HEADS, L), z(HEADS, L)
        hg = z(HEADS, SEQ)
        scoresT = Zone(zoneA, 3 * HEADS * L)(HEADS * 2, P)
        flat = {n: v.rearrange("p h t -> p (h t)") for n, v in (("q", hq), ("k", hk), ("f", hf))}
        z = Zone(zoneB)
        c_raw, c_nrm = z(4, L), z(4, L)
        qn, qpe, qpr = z(HEADS, SEQ), z(4, SEQ), z(4, SEQ)
        kn, kpe, kpr = z(HEADS, L), z(L), z(L)
        vM = z(3, HEADS * VDIM)
        att_s, att_p, att_r = z(2, L), z(2, L), z(8, 2)
        rope_a, rope_b = att_s, att_p
        att_pt = Zone(zoneB)(2, 3 * P)
        assert z.at <= 13440
        z = Zone(zoneB)
        tree = z(HEADS * L)
        v_tok, v_meta = z(2, HEADS * P), z(HEADS * P)
        S1, S2 = z(HEADS, P), z(HEADS, P)
        kT_tok, kT_meta = z(HEADS, P), z(HEADS, P)
        o_h = Zone(zoneB, z.at - 2 * HEADS * P)(HEADS, SEQ)
        gates = z(2 * DC, SEQ)
        assert z.at <= 13440
        o_mla = keep[:, :].rearrange("p (h t) -> p h t", h=HEADS)
        z = Zone(zoneA)
        ya, mixed = z(DC, SEQ), z(DC, SEQ)
        y_mla = Zone(zoneA, 2 * HEADS * L)(DC, SEQ)
        y_hg = Zone(zoneA, 3 * HEADS * L)(HEADS, SEQ)
        y_hi, y_lo = in_zone("y_hi", ZONE_A, DC, SEQ), in_zone("y_lo", ZONE_A + DC * SEQ, DC, SEQ)
        hid_hi, hid_lo = in_zone("hid_hi", 0, FC, SEQ), in_zone("hid_lo", ZONE_A, FC, SEQ)
        z = Zone(zoneB, FC * SEQ)
        hid, up = z(4, SEQ), z(2, SEQ)
        ffo = z(DC, SEQ)
        z = Zone(zoneA)
        kiT, kir, qiT, qir = z(L), z(L), z(4, L), z(4, L)
        idx_w = z(2, 8)
        upad, gsig = z(CC, TAPS - 1 + L), z(CC, L)
        acc = z(CC, L)
        cln_sq = gsig
        zT = Zone(zoneA, z.at)(DC, L)
        q2, k2 = z(4, L), z(4, L)
        assert z.at <= 10752
        z = Zone(zoneB)
        q2r, k2r = z(4, L), z(4, L)
        v2 = z(3, HEADS * HD)
        szc, sza = z(CC, L), z(CC, L)
        o_tok = Zone(zoneB, z.at)(3, HEADS * HD)
        relu = z(2, L)
        score = z(2, L)
        rope2_a, rope2_b = z(2, L), z(2, L)
        sel = z(2, L)
        top8 = z(2, 8)
        at2_s, at2_p, at2_pt, at2_r = z(2, L), z(DSA_LAG + 1, L), z(2, 3 * P), z(8, 2)
        ycat = z(DC, L)
        vT2 = keep[:, 0:4 * L].rearrange("p (c t) -> p c t", c=4)
        assert z.at <= 13440, z.at
        out_tok = zoneA[:, 0:2 * D].rearrange("p (t d) -> p t d", t=2)
        x_tok = zoneA[:, 0:2 * D].rearrange("p (t d) -> p t d", t=2)
        m_tok = zoneA[:, 2 * D:4 * D].rearrange("p (t d) -> p t d", t=2)

        def slot(name):
            return ring[:, SLOT[name], :]

        def w_ready(eng, name):
            eng.wait_ge(sem(f"slot{SLOT[name]}_full"), USE[name])

        def piece_views(i):
            name, m = PIECES[i]
            width, row, col, rows, n = pieces(name)[m]
            src = slot(name)[:, row * width:(row + rows) * width].rearrange("p (k n) -> p k n", n=width)[:, :, col:col + n]
            return (src,) + tuple(w[:, i % PAIRS, 0:n * rows].rearrange("p (k n) -> p k n", n=n) for w in (w_hi, w_lo))

        def out_of_psum(eng, name, m=0):
            eng.wait_ge(sem("chunk_out"), CHUNK[name, m] + 1)

        def tap_weight(l, j, c):
            return cols[:, TAP_COL[l] + CC * j + c:TAP_COL[l] + CC * j + c + 1]

        Q_TILES = [(META, P, META + P), (META + P, P, L)]
        MLA_STEPS = [(h, *t) for h in range(HEADS) for t in Q_TILES]
        O_TILES = [[(0, META, META)] + Q_TILES, Q_TILES]
        TURN_BANKS = (6, 7, 2, 3)
        O_AT = {META: 0, META + P: 1, 0: 2}
        DSA_STEPS = [[(h, *t) for h in range(HEADS) for t in O_TILES[l]] for l in range(DEPTH2)]
        CAUSAL = {0: "causal_m", META: "causal_0", META + P: "causal_1"}

        block = ctx.enter_context(nc.Block())

        @block.sync
        def _(sp):
            x2 = a["x"][0].rearrange("(t p) d -> p t d", p=P)
            sp.dma_start(x_tok, x2).then_inc(sem("x_in"), 16)
            sp.dma_start(m_tok[0:META, 0, :], a["meta_tokens"]).then_inc(sem("x_in"), 16)
            sp.dma_start(m_tok[0:META, 1, :], a["meta_tokens_2"]).then_inc(sem("x_in"), 16)
            sp.dma_start(const[:, 0:2 * P], a["constants"][:, 0:2 * P]).then_inc(sem("const_in"), 16)

            def free(name):
                before = PREV[name]
                if before in MLA_USED:
                    sp.wait_ge(sem("chunk_done"), CHUNK[MLA_USED[before]] + 1)
                elif before is not None:
                    sp.wait_ge(sem("w_lo"), SPLIT[before, len(pieces(before)) - 1] + 1)

            def full(name, ins):
                ins.then_inc(sem(f"slot{SLOT[name]}_full"), 16)

            def kview(w):
                return w.rearrange("(k p) n -> p k n", p=P)

            def load(name, w, n):
                k = w.shape[1]
                free(name)
                full(name, sp.dma_start(slot(name)[:, 0:k * n].rearrange("p (k n) -> p k n", k=k), w))

            w_in = kview(a["w_in"][0])

            def load_cols(name, w, count, c0=0, first=0):
                for i in range(first, count):
                    load(f"{name}{i}", w[:, :, c0 + i * 256:c0 + (i + 1) * 256], 256)

            load_cols("c", w_in, 2, 4 * D)
            at = 0
            for name, n in VEC_LIST:
                v = a[name]
                v = v.rearrange("a b -> (a b)") if len(v.shape) == 2 else v
                sp.dma_start(vec_rows[at:at + n, 0, :], v.rearrange("(c p) -> c p", p=P)).then_inc(sem("vec_in"), 16)
                at += n
            for l in range(DEPTH2):
                sp.dma_start(vec_rows[0:TAPS * CC, 1 + l, :],
                              a["conv_w_2"][l].rearrange("j (c p) -> (j c) p", p=P)).then_inc(sem("vec_in"), 16)

            sp.dma_start(const[:, 2 * P:N_CONST], a["constants"][:, 2 * P:N_CONST]).then_inc(sem("tables_in"), 16)

            def load_twice(name, w, n, cols_):
                free(name)
                dst = slot(name)[:, 0:DC * (n + 64)].rearrange("p (k n) -> p k n", k=DC)
                full(name, sp.dma_start(dst[:, :, 0:64], w[:, :, cols_:cols_ + 64]))
                full(name, sp.dma_start(dst[:, :, 64:64 + n], w[:, :, cols_:cols_ + n]))

            load_twice("kpe", w_in, ROPE, 4 * D + 512)
            load_cols("hg", w_in, 2)
            for i in range(2):
                load(f"wqb{i}", kview(a["w_q_b"][0])[:, :, i * 768:(i + 1) * 768], 768)
            for i in range(2):
                load(f"wkvb{i}", kview(a["w_kv_b"][0])[:, :, i * 1024:(i + 1) * 1024], 1024)
            load_cols("hg", w_in, 16, first=2)
            load_cols("gate", w_in, 8, GATE_COL)
            for n, w in (("mlo", "w_mla_o"), ("hgo", "w_hg_o"), ("mix", "w_out")):
                load_cols(n, kview(a[w][0]), 4)
            w_fi = kview(a["w_ffn_in"][0])
            for i in range(2 * FFN_ITEMS):
                c0 = i % 2 * FFN + i // 2 * 256
                load(f"ffi{i}", w_fi[:, :, c0:c0 + 256], 256)
            w_fo = kview(a["w_ffn_out"][0])
            for i in range(2 * DC):
                load(f"ffo{i}", w_fo[:, i % 2 * 11:i % 2 * 11 + 11, i // 2 * P:(i // 2 + 1) * P], P)
            for l in range(DEPTH2):
                w2 = kview(a["w_in_2"][l])
                load_twice(f"L{l}kw", w2, HD + HEADS, COL2["ki"])
                for n in ("qi", "a", "g", "q", "k", "v", "zc", "za"):
                    load_cols(f"L{l}{n}", w2, 2, COL2[n])
                load_cols(f"L{l}wo", kview(a["w_out_2"][l]), 4)
            for half in range(2):
                for t in range(2):
                    out_of_psum(sp, "out", 2 * half + t)
                    cols_ = slice(half * 512, half * 512 + 512)
                    sp.dma_start(out[0, t * P:(t + 1) * P, cols_], out_tok[:, t, cols_]).then_inc(sem("stored"), 16)
            sp.wait_ge(sem("stored"), 4 * 16)

        @block.tensor
        def _(pe):
            mm = nc.tensor.matmul

            def bank_free(g):
                if g >= 2:
                    pe.wait_ge(sem("chunk_out"), g - 1)

            def done(ins):
                ins.then_inc(sem("chunk_done"), 1)

            def linear(g, lhs, rhs, n, k=DC, rows=P, ready=None):
                bank_free(g)
                for i in range(k):
                    if ready:
                        ready(i)
                    last = mm(PS[0:rows, g % 2, 0:n], lhs(i), rhs(i), start=(i == 0), stop=(i == k - 1))
                done(last)

            def split_ready(i):
                pe.wait_ge(sem("w_lo"), i + 1)

            def three(out_, hi_w, lo_w, hi_x, lo_x, start, stop):
                mm(out_, hi_w, hi_x, start=start, stop=False)
                mm(out_, hi_w, lo_x, start=False, stop=False)
                return mm(out_, lo_w, hi_x, start=False, stop=stop)

            def chunk(name, m, x, t0=0, ready=None):
                g = CHUNK[name, m]
                split_ready(SPLIT[name, m])
                bank_free(g)
                _, hi_w, lo_w = piece_views(SPLIT[name, m])
                hi_x, lo_x = x
                n = hi_x.shape[2] - t0
                for i in range(DC):
                    if ready:
                        ready(i)
                    last = three(PS[:, g % 2, 0:n], hi_w[:, i, 0:P], lo_w[:, i, 0:P],
                                 hi_x[:, i, t0:], lo_x[:, i, t0:], i == 0, i == DC - 1)
                done(last)

            def x_ready(tag):
                return lambda i: pe.wait_ge(sem(f"lo_{tag}"), i + 1)

            def mean_of(dim):
                return means[:, MEANS.index(dim), :]

            def norm_step(tag, c, count, bank, n, dim=D, first=0):
                pe.wait_ge(sem(f"sq_{tag}"), first + c + 1)
                mm(PS[:, bank, 0:n], mean_of(dim), sq[:, (first + c) % 2, 0:n], start=(c == 0),
                   stop=(c == count - 1)).then_inc(sem(f"sum_{tag}"), 1)

            def norm_sum(tag, count, bank, n, dim=D):
                for c in range(count):
                    norm_step(tag, c, count, bank, n, dim)

            def linear_norm(tag, chunks, n):
                for c, chunk in enumerate(chunks):
                    chunk()
                    if c:
                        norm_step(tag, c - 1, len(chunks), 2, n)
                norm_step(tag, len(chunks) - 1, len(chunks), 2, n)

            X = (x_hi, x_lo)

            pe.wait_ge(sem("const_in"), 16)
            pe.wait_ge(sem("x_in"), 48)
            pe.wait_ge(sem("means"), len(MEANS))
            for c in range(DC):
                g = CHUNK["start", c]
                bank_free(g)
                b = PS[:, g % 2, :]
                nc.tensor.transpose(b[:, 0:META], m_tok[0:META, 0, c * P:(c + 1) * P], ident[0:META, 0:META])
                for t in range(2):
                    last = nc.tensor.transpose(b[:, META + t * P:META + (t + 1) * P],
                                               x_tok[:, t, c * P:(c + 1) * P], ident)
                done(last)
                if c >= 2:
                    norm_step("pre", c - 2, DC, 2, L)
            for c in (DC - 2, DC - 1):
                norm_step("pre", c, DC, 2, L)
            pe.wait_ge(sem("vec_in"), 16 * (len(VEC_LIST) + 2))
            for j, n in enumerate((N_VEC, TAPS * CC, TAPS * CC)):
                g = CHUNK["start", DC + j]
                bank_free(g)
                done(nc.tensor.transpose(PS[:, g % 2, 0:n], vec_rows[0:n, j, :], ident[0:n, 0:n]))
            g = CHUNK["start", DC + 3]
            bank_free(g)
            for c in range(DC):
                last = nc.tensor.transpose(PS[:, g % 2, c * META:(c + 1) * META],
                                           m_tok[0:META, 1, c * P:(c + 1) * P], ident[0:META, 0:META])
            done(last)

            for c in range(4):
                chunk(*part("c", c), X, ready=x_ready("pre") if c == 0 else None)
            chunk("kpe", 0, X)
            norm_sum("cq", 2, 2, L, LORA)
            norm_sum("ckv", 2, 3, L, LORA)
            wq = [slot(f"wqb{i}")[:, 0:2 * 768].rearrange("p (k h c) -> p k h c", k=2, h=4) for i in range(2)]
            for h in range(HEADS):
                if h % 4 == 0:
                    w_ready(pe, f"wqb{h // 4}")
                linear(CHUNK["wqb", h], lambda i: wq[h // 4][:, i, h % 4, 0:NOPE], lambda i: c_nrm[:, i, META:L], SEQ,
                       k=2, ready=lambda i: pe.wait_ge(sem("c_nrm"), i + 1))
            for hp in range(HEADS // 2):
                g = CHUNK["wqb", HEADS + hp]
                bank_free(g)
                for half in range(2):
                    h = 2 * hp + half
                    for i in range(2):
                        last = mm(PS[half * 64:half * 64 + 64, g % 2, 0:SEQ], wq[h // 4][:, i, h % 4, NOPE:NOPE + ROPE],
                                  c_nrm[:, i, META:L], start=(i == 0), stop=(i == 1))
                done(last)
            wkv = [slot(f"wkvb{i}").rearrange("p (k h c) -> p k h c", k=2, h=4) for i in range(2)]
            for h in range(HEADS):
                if h % 4 == 0:
                    w_ready(pe, f"wkvb{h // 4}")
                linear(CHUNK["wkvb", h], lambda i: wkv[h // 4][:, i, h % 4, 0:NOPE], lambda i: c_nrm[:, 2 + i, :], L,
                       k=2, ready=lambda i: pe.wait_ge(sem("c_nrm"), 2 + i + 1))
            for x, (t0, n) in enumerate(KEY_CHUNKS):
                for half in range(2):
                    linear(CHUNK["wkvb", HEADS + 2 * x + half], lambda i: c_nrm[:, 2 + i, t0:t0 + n],
                           lambda i: wkv[half][:, i, :, NOPE:NOPE + VDIM], 4 * VDIM, k=2, rows=n)

            def rope(tag, i, src):
                if i >= 2:
                    pe.wait_ge(sem(f"{tag}_rope_out"), i - 1)
                mm(PS[:, 6 + i % 2, 0:src.shape[1]], rotm, src, start=True, stop=True)\
                    .then_inc(sem(f"{tag}_rope"), 1)

            out_of_psum(pe, "wqb", 11)
            for i in range(5):
                rope("mla", i, qpe[:, i, :] if i < 4 else kpe[:, :])

            def attention_step(i, tag, steps, s_mm, o_mm, p_buf, pt_buf, probs, lag, o_banks):
                n = len(steps)
                if i < n:
                    if i >= 2:
                        pe.wait_ge(sem(f"{tag}_masked"), i - 1)
                    s_mm(steps[i], PS[:, 2 + i % 2, :]).then_inc(sem(f"{tag}_scores"), 1)
                j = i - lag
                if 0 <= j < n:
                    h, q0, nq, nk = steps[j]
                    pe.wait_ge(sem(f"{tag}_{probs}"), j + 1)
                    if j >= 2:
                        pe.wait_ge(sem(f"{tag}_pt_out"), j - 1)
                    for x, (k0, kn_) in enumerate(KEY_CHUNKS):
                        m = min(kn_, nk - k0)
                        if m > 0:
                            last = nc.tensor.transpose(PS[0:m, 4 + j % 2, x * P:x * P + nq],
                                                       p_buf[0:nq, j % (lag + 1), k0:k0 + m], ident[0:nq, 0:nq])
                    last.then_inc(sem(f"{tag}_pt"), 1)
                j = i - lag - 1
                if 0 <= j < n:
                    h, q0, nq, nk = steps[j]
                    pe.wait_ge(sem(f"{tag}_pt_out"), j + 1)
                    if j >= len(o_banks):
                        pe.wait_ge(sem(f"{tag}_o_out"), j + 1 - len(o_banks))
                    used = [(x, min(kn_, nk - k0)) for x, (k0, kn_) in enumerate(KEY_CHUNKS) if nk > k0]
                    for x, m in used:
                        last = o_mm(h, x, m, nq, PS[:, o_banks[j % len(o_banks)], :], pt_buf[0:m, j % 2, x * P:x * P + nq],
                                    dict(start=(x == 0), stop=(x == used[-1][0])))
                    last.then_inc(sem(f"{tag}_o"), 1)

            def mla_scores(step, b):
                h, q0, nq, nk = step
                r = slice(64 * (h % 2), 64 * (h % 2) + 64)
                mm(b[:, 0:nk], qn[:, h, q0 - META:q0 - META + nq], kn[:, h, 0:nk], start=True, stop=False)
                return mm(b[:, 0:nk], qpr[r, h // 2, q0 - META:q0 - META + nq], kpr[r, 0:nk], start=False, stop=True)

            def mla_out(h, x, m, nq, b, p_t, ends):
                return mm(b[:, 0:nq], vM[0:m, x, h * VDIM:(h + 1) * VDIM], p_t, **ends)

            pe.wait_ge(sem("mla_roped"), 5)
            out_of_psum(pe, "wkvb", 13)
            for s in range(MLA_N + 2):
                attention_step(s, "mla", MLA_STEPS, mla_scores, mla_out, att_p, att_pt, "probs", 1, (6, 7))
                if s < MLA_N:
                    for c in (2 * s, 2 * s + 1):
                        chunk(*part("hg", c), X)

            for h in range(HEADS):
                g = CHUNK["vT", h]
                bank_free(g)
                b = PS[:, g % 2, :]
                for t in range(2):
                    nc.tensor.transpose(b[:, t * P:(t + 1) * P], hi[:, h, META + t * P:META + (t + 1) * P], ident)
                done(nc.tensor.transpose(b[0:META, 2 * P:3 * P], hi[:, h, 0:META], ident))
                if h % 2:
                    chunk(*part("gate", h // 2), X, META)
            for lv in range(LEVELS + 1):
                for half in range(2):
                    pe.wait_ge(sem("level_ready"), 2 * lv + half + 1)
                    for b in range(2):
                        if lv:
                            pe.wait_ge(sem("level_masked"), 4 * (lv - 1) + 2 * half + b + 1)
                        for j in range(4):
                            h, t = divmod(8 * half + 4 * b + j, 2)
                            tok = slice(META + t * P, META + (t + 1) * P)
                            last = mm(PS[:, 2 + 2 * half + b, j * P:(j + 1) * P], hk[:, h, tok], hq[:, h, tok],
                                      start=True, stop=True)
                        last.then_inc(sem("level_done"), 1)
                    if 2 * lv + half < 12:
                        chunk(*part("gate", 4 + 2 * lv + half), X, META)
            pe.wait_ge(sem("level_ready"), 2 * LEVELS + 4)
            for h in range(HEADS):
                g = CHUNK["kT", h]
                bank_free(g)
                nc.tensor.transpose(PS[:, g % 2, 0:P], hk[:, h, META:META + P], ident)
                done(nc.tensor.transpose(PS[0:META, g % 2, P:2 * P], hk[:, h, 0:META], ident))
                if h % 2:
                    chunk(*part("mlo", h // 2), X, META, ready=x_ready("mla") if h == 1 else None)
            for h in range(HEADS):
                g = CHUNK["S", h]
                bank_free(g)
                out_of_psum(pe, "kT", h)
                mm(PS[:, g % 2, 0:P], kT_meta[0:META, h, :], v_meta[0:META, h * P:(h + 1) * P], start=True, stop=True)
                done(mm(PS[:, g % 2, P:2 * P], kT_tok[:, h, :], v_tok[:, 0, h * P:(h + 1) * P], start=True, stop=True))
            for h in range(HEADS):
                g = CHUNK["o", h]
                bank_free(g)
                pe.wait_ge(sem("state"), h + 1)
                for t in range(2):
                    b = PS[:, g % 2, t * P:(t + 1) * P]
                    mm(b, v_tok[:, t, h * P:(h + 1) * P], scoresT[:, 2 * h + t, :], start=True, stop=False)
                    last = mm(b, (S1, S2)[t][:, h, :], hq[:, h, META + t * P:META + (t + 1) * P], start=False, stop=True)
                done(last)
            for h in range(HEADS):
                pe.wait_ge(sem("sq_hg"), h + 1)
                mm(PS[:, 2 + h // 2, h % 2 * SEQ:h % 2 * SEQ + SEQ], mean_of(P), sq[:, h % 2, 0:SEQ], start=True, stop=True)\
                    .then_inc(sem("sum_hg"), 1)
                if h % 2:
                    chunk(*part("mlo", 4 + h // 2), X, META)

            for c in range(DC):
                chunk(*part("hgo", c), (y_hi, y_lo), ready=x_ready("hg") if c == 0 else None)
            linear_norm("post", [lambda c=c: chunk(*part("mix", c), X, META,
                                                   ready=x_ready("mix") if c == 0 else None)
                                 for c in range(DC)], SEQ)
            norm_sum("fpre", DC, 3, SEQ)

            for c in range(4 * FFN_ITEMS):
                chunk(*part("ffi", c), X, META, ready=x_ready("fpre") if c == 0 else None)

            def ffo_chunk(c):
                g = CHUNK["ffo", c]
                bank_free(g)
                for q in range(4):
                    i0 = SPLIT[f"ffo{2 * c + q // 2}", q % 2]
                    split_ready(i0)
                    _, hi_w, lo_w = piece_views(i0)
                    for i in range(hi_w.shape[1]):
                        k = 11 * (q // 2) + 6 * (q % 2) + i
                        if c == 0:
                            x_ready("hid")(k)
                        last = three(PS[:, g % 2, 0:SEQ], hi_w[:, i, :], lo_w[:, i, :], hid_hi[:, k, :], hid_lo[:, k, :],
                                     k == 0, k == FC - 1)
                    if q < 3:
                        last.then_inc(sem("piece_done"), 1)
                done(last)

            linear_norm("fpost", [lambda c=c: ffo_chunk(c) for c in range(DC)], SEQ)

            for l in range(DEPTH2):
                T = f"L{l}"
                q_from = 0 if l == 0 else META
                n_q = L - q_from
                chunk(f"{T}kw", 0, X, ready=x_ready(f"{T}h"))
                split_ready(SPLIT[f"{T}kw", 1])
                _, hi_w, lo_w = piece_views(SPLIT[f"{T}kw", 1])
                g = CHUNK[f"{T}kw", 1]
                bank_free(g)
                for t in range(2):
                    tok = slice(META + t * P, META + (t + 1) * P)
                    for i in range(DC):
                        last = three(PS[:, g % 2, 8 * t:8 * t + 8], x_hi[:, i, tok], x_lo[:, i, tok],
                                     hi_w[:, i, :], lo_w[:, i, :], i == 0, i == DC - 1)
                done(last)
                for m in range(5):
                    chunk(*part(f"{T}qi", m) if m < 4 else part(f"{T}a", 0), X, q_from if m < 4 else 0)
                    out_of_psum(pe, *part(f"{T}qi", m - 1) if m else (f"{T}kw", 0))
                    rope("i", 5 * l + m, qiT[:, m - 1, q_from:L] if m else kiT[:, :])
                pe.wait_ge(sem("i_roped"), 5 * (l + 1))
                for s in range(16):
                    t, h = divmod(s, HEADS)
                    q0, nq, nk = Q_TILES[t]
                    r = slice(64 * (h % 2), 64 * (h % 2) + 64)
                    if s >= 2:
                        pe.wait_ge(sem("relu"), 16 * l + s - 1)
                    mm(PS[:, 2 + s % 2, 0:nk], qir[r, h // 2, q0:q0 + nq], kir[r, 0:nk], start=True, stop=True)\
                        .then_inc(sem("idx"), 1)
                    if s in (3, 7, 11):
                        chunk(*part(f"{T}a", 1 + s // 4), X)
                for n, t0 in (("g", 0), ("q", q_from), ("k", 0), ("v", 0)):
                    for m in range(4):
                        chunk(*part(f"{T}{n}", m), X, t0)
                        if n == "k":
                            out_of_psum(pe, *part(f"{T}q", m))
                            rope("q", 8 * l + m, q2[:, m, q_from:L])
                        if n == "v":
                            out_of_psum(pe, *part(f"{T}k", m))
                            rope("q", 8 * l + 4 + m, k2[:, m, :])
                out_of_psum(pe, *part(f"{T}v", 3))
                for x, (t0, n) in enumerate(KEY_CHUNKS):
                    g = CHUNK[f"{T}vt", x]
                    bank_free(g)
                    for c in range(4):
                        last = nc.tensor.transpose(PS[0:n, g % 2, c * P:(c + 1) * P], vT2[:, c, t0:t0 + n], ident)
                    done(last)

                def dsa_scores(step, b):
                    h, q0, nq, nk = step
                    r = slice(64 * (h % 2), 64 * (h % 2) + 64)
                    return mm(b[0:nq, 0:nk], q2r[r, h // 2, q0:q0 + nq], k2r[r, h // 2, 0:nk], start=True, stop=True)

                def dsa_out(h, x, m, nq, b, p_t, ends):
                    return mm(b[0:nq, 0:HD], p_t, v2[0:m, x, h * HD:(h + 1) * HD], **ends)

                pe.wait_ge(sem("q_roped"), 8 * (l + 1))
                out_of_psum(pe, f"{T}vt", 2)
                for s in range(DSA_N[l] + DSA_LAG + 1):
                    attention_step(s, f"{T}att", DSA_STEPS[l], dsa_scores, dsa_out, at2_p, at2_pt, "exp", DSA_LAG, (6,))
                    if s == CLN_STEP[l]:
                        pe.wait_ge(sem(f"{T}tap"), CC * TAPS)
                        for c in range(CC):
                            last = mm(PS[:, 7, 0:n_q], mean_of(CONV_C), acc[:, c, q_from:L], start=(c == 0),
                                      stop=(c == CC - 1))
                        last.then_inc(sem(f"{T}cln_mean"), 1)
                    if s == CLN_STEP[l] + 3:
                        for c in range(CC):
                            pe.wait_ge(sem(f"sq_{T}cln"), c + 1)
                            last = mm(PS[:, 7, 0:n_q], mean_of(CONV_C), cln_sq[:, c, 0:n_q], start=(c == 0),
                                      stop=(c == CC - 1))
                        last.then_inc(sem(f"sum_{T}cln"), 1)
                    for n, m in z_chunks(l, s):
                        chunk(*part(f"{T}{n}", m), X, q_from)

                pe.wait_ge(sem(f"{T}att_o_out"), len(DSA_STEPS[l]))
                for c in range(4):
                    for q0, nq, _ in O_TILES[l]:
                        last = nc.tensor.transpose(PS[:, TURN_BANKS[c], q0:q0 + nq],
                                                   o_tok[0:nq, O_AT[q0], c * P:(c + 1) * P], ident[0:nq, 0:nq])
                    last.then_inc(sem(f"{T}o_turned"), 1)
                for c in range(DC + 2):
                    if c < DC:
                        chunk(*part(f"{T}wo", c), X, q_from, ready=x_ready(f"{T}y") if c == 0 else None)
                    if c >= 2:
                        pe.wait_ge(sem(f"{T}pln_in"), c - 1)
                        last = mm(PS[:, 4, 0:L - q_from], mean_of(D), zT[:, c - 2, q_from:L], start=(c == 2),
                                  stop=(c == DC + 1))
                last.then_inc(sem(f"{T}pln_mean"), 1)
                norm_sum(f"{T}pln", DC, 5, L - q_from)

            for half in range(2):
                pe.wait_ge(sem("h_post"), DC * (DEPTH2 - 1) + 4 * half + 4)
                for t in range(2):
                    g = CHUNK["out", 2 * half + t]
                    bank_free(g)
                    for c in range(4):
                        last = nc.tensor.transpose(PS[:, g % 2, c * P:(c + 1) * P],
                                                   hT[:, 4 * half + c, META + t * P:META + (t + 1) * P], ident)
                    done(last)

        @block.gpsimd
        def _(pool):
            sub = nc.gpsimd.tensor_tensor

            def lo_items(first, last):
                for i in range(SPLIT[first, 0], SPLIT[last, len(pieces(last)) - 1] + 1):
                    src, hi_w, lo_w = piece_views(i)
                    if i < PAIRS:
                        pool.wait_ge(sem("first_w_hi"), i + 1)
                    else:
                        pool.wait_ge(sem("w_hi"), i - PAIRS + 1)
                    sub(lo_w, src, hi_w, ALU.subtract).then_inc(sem("w_lo"), 1)

            def lo_x(tag, c, dst, src, hi_):
                pool.wait_ge(sem(f"hi_{tag}"), c + 1)
                sub(dst, src, hi_, ALU.subtract).then_inc(sem(f"lo_{tag}"), 1)

            lo_items("c0", "c1")
            for c in range(DC):
                lo_x("pre", c, x_lo[:, c, :], u_t[:, c % 4, :], x_hi[:, c, :])
            lo_items("kpe", "mlo1")
            for h in range(HEADS):
                lo_x("mla", h, x_lo[:, h, META:L], o_mla[:, h, :], x_hi[:, h, META:L])
            lo_items("mlo2", "hgo1")
            for h in range(HEADS):
                lo_x("hg", h, y_lo[:, h, :], y_hg[:, h, :], y_hi[:, h, :])
            lo_items("hgo2", "hgo3")
            for c in range(DC):
                if c == 6:
                    lo_items("mix0", "mix0")
                lo_x("mix", c, x_lo[:, c, META:L], ya[:, c, :], x_hi[:, c, META:L])
            lo_items("mix1", "ffi1")
            for c in range(DC):
                lo_x("fpre", c, x_lo[:, c, META:L], u_t[:, c % 4, 0:SEQ], x_hi[:, c, META:L])
            for j in range(0, FC, 2):
                if j + 3 < FC:
                    lo_items(f"ffi{j + 2}", f"ffi{j + 3}")
                else:
                    lo_items("ffo0", "ffo1")
                for i in (j, j + 1):
                    lo_x("hid", i, hid_lo[:, i, :], hid[:, i % 4, :], hid_hi[:, i, :])
            lo_items("ffo2", "L0qi0")
            for l in range(DEPTH2):
                T = f"L{l}"
                q_from = 0 if l == 0 else META
                for c in range(DC):
                    lo_x(f"{T}h", c, x_lo[:, c, :], hT[:, c, :], x_hi[:, c, :])
                lo_items(f"{T}qi1", f"{T}wo1")
                for c in range(DC):
                    lo_x(f"{T}y", c, x_lo[:, c, q_from:L], ycat[:, c, q_from:L], x_hi[:, c, q_from:L])
                lo_items(f"{T}wo2", f"L{l + 1}qi0" if l + 1 < DEPTH2 else f"{T}wo3")

        @block.scalar
        def _(act):
            af = nc.scalar.activation

            def take(name, m, dst, f=ACT.Copy, rows=P, c0=0, n=L, view=None, count=True, **kw):
                g = CHUNK[name, m]
                act.wait_ge(sem("chunk_done"), g + 1)
                src = PS[0:rows, g % 2, c0:c0 + n]
                ins = af(dst, view(src) if view else src, f, **kw)
                if count:
                    ins.then_inc(sem("chunk_out"), 1)
                    if g in ENDS:
                        round_piece(ENDS[g] + PAIRS)

            def round_piece(i):
                if i < len(PIECES):
                    src, hi_w, _ = piece_views(i)
                    w_ready(act, PIECES[i][0])
                    af(hi_w, src, ACT.Copy).then_inc(sem("w_hi"), 1)

            def warm(f):
                act.wait_ge(sem("small"), 1)
                af(small[:, 4:5], small[:, 0:1], f)

            def split(tag, c, dst, src, ready):
                act.wait_ge(*ready)
                af(dst, src, ACT.Copy).then_inc(sem(f"hi_{tag}"), 1)

            def squares(tag, c, src, wait, n):
                wait()
                if c >= 2:
                    act.wait_ge(sem(f"sum_{tag}"), c - 1)
                af(sq[:, c % 2, 0:n], src, ACT.Square).then_inc(sem(f"sq_{tag}"), 1)

            def std(tag, sums, bank, eps, dst, guard=None):
                act.wait_ge(sem(f"sum_{tag}"), sums)
                act.wait_ge(sem("small"), 1)
                if guard:
                    act.wait_ge(*guard)
                af(dst, PS[:, bank, 0:dst.shape[1]], ACT.Sqrt, bias=eps).then_inc(sem(f"std_{tag}"), 1)

            for c in range(DC):
                take("start", c, hT[:, c, :])
                if c:
                    squares("pre", c - 1, hT[:, c - 1, :], lambda: out_of_psum(act, "start", c - 1), L)
            squares("pre", DC - 1, hT[:, DC - 1, :], lambda: out_of_psum(act, "start", DC - 1), L)
            std("pre", DC, 2, eps_rms, nrm[:, 0, :])
            for j, (at, n) in enumerate(((0, N_VEC), (TAP_COL[0], TAPS * CC), (TAP_COL[1], TAPS * CC))):
                take("start", DC + j, cols[:, at:at + n], n=n)
            take("start", DC + 3, vec_rows[:, 0, :], n=P)
            for c in range(DC):
                split("pre", c, x_hi[:, c, :], u_t[:, c % 4, :], (sem("u"), c + 1))
            act.wait_ge(sem("lb_shift"), 2)
            af(lb_e0, lb_e0, ACT.Exp).then_inc(sem("lb_exp"), 1)
            af(lb_e1, lb_e1, ACT.Exp).then_inc(sem("lb_exp"), 1)

            warm(ACT.Sqrt)
            for i in range(4):
                take(*part("c", i), c_raw[:, i, :])
            take("kpe", 0, kpe)
            for tag, first in (("cq", 0), ("ckv", 2)):
                for c in range(2):
                    def ready():
                        out_of_psum(act, *part("c", first + c))
                        if tag == "ckv":
                            act.wait_ge(sem("sum_cq"), 2)
                    squares(tag, c, c_raw[:, first + c, :], ready, L)
                std(tag, 2, 2 + first // 2, eps_rms, nrm[:, first // 2, :],
                    guard=(sem("hi_pre"), DC) if first == 0 else None)
            for h in range(HEADS):
                take("wqb", h, qn[:, h, :], n=SEQ)
            for i in range(4):
                take("wqb", HEADS + i, qpe[:, i, :], n=SEQ)
            for h in range(HEADS):
                take("wkvb", h, kn[:, h, :])
            for x, (t0, n) in enumerate(KEY_CHUNKS):
                for half in range(2):
                    take("wkvb", HEADS + 2 * x + half, vM[0:n, x, half * 512:half * 512 + 512], rows=n, n=512)

            def attention_step(i, tag, steps, s_buf, p_buf, pt_buf, r_buf, o_of, lag, late):
                n = len(steps)

                def exp():
                    h, q0, nq, nk = steps[i]
                    act.wait_ge(sem(f"{tag}_masked"), i + 1)
                    if i > lag:
                        act.wait_ge(sem(f"{tag}_pt"), i - lag)
                    af(p_buf[0:nq, i % (lag + 1), 0:nk], s_buf[0:nq, i % 2, 0:nk], ACT.Exp, scale=-1.0,
                       bias=r_buf[0:nq, i % 8, 0:1], accum_out=r_buf[0:nq, i % 8, 1:2])\
                        .then_inc(sem(f"{tag}_exp"), 1)

                if i < n and not late:
                    exp()
                j = i - lag
                if 0 <= j < n:
                    h, q0, nq, nk = steps[j]
                    act.wait_ge(sem(f"{tag}_pt"), j + 1)
                    if j >= 2:
                        act.wait_ge(sem(f"{tag}_o"), j - 1)
                    whole, rest = nk // P, nk % P
                    if whole:
                        v = pt_buf[:, j % 2, 0:whole * P].rearrange("p (x q) -> p x q", q=P)[:, :, 0:nq]
                        s = PS[:, 4 + j % 2, 0:whole * P].rearrange("p (x q) -> p x q", q=P)[:, :, 0:nq]
                        af(v, s, ACT.Copy)
                    af(pt_buf[0:rest, j % 2, whole * P:whole * P + nq],
                       PS[0:rest, 4 + j % 2, whole * P:whole * P + nq], ACT.Copy).then_inc(sem(f"{tag}_pt_out"), 1)
                j = i - lag - 1
                if 0 <= j < n:
                    h, q0, nq, nk = steps[j]
                    act.wait_ge(sem(f"{tag}_o"), j + 1)
                    dst = o_of(h, q0, nq)
                    if late:
                        act.wait_ge(sem(f"{tag}_inv"), j + 1)
                        af(dst, PS[0:nq, 6, 0:HD], ACT.Copy, scale=r_buf[0:nq, j % 8, 1:2])\
                            .then_inc(sem(f"{tag}_o_out"), 1)
                    else:
                        af(dst, PS[:, 6 + j % 2, 0:nq], ACT.Copy).then_inc(sem(f"{tag}_o_out"), 1)
                if i < n and late:
                    exp()
                if i < n and not late:
                    h, q0, nq, nk = steps[i]
                    act.wait_ge(sem(f"{tag}_inv"), i + 1)
                    af(p_buf[0:nq, i % (lag + 1), 0:nk], p_buf[0:nq, i % (lag + 1), 0:nk], ACT.Copy,
                       scale=r_buf[0:nq, i % 8, 1:2]).then_inc(sem(f"{tag}_probs"), 1)

            hg_out = [(hq, ACT.Silu), (hf, ACT.Sigmoid), (hi, ACT.Copy), (hg, ACT.Silu)]
            for s in range(MLA_N + 2):
                attention_step(s, "mla", MLA_STEPS, att_s, att_p, att_pt, att_r,
                               lambda h, q0, nq: o_mla[:, h, q0 - META:q0 - META + nq], lag=1, late=False)
                if s < MLA_N:
                    for c in (2 * s, 2 * s + 1):
                        dst, f = hg_out[c // HEADS]
                        off = META if dst is hg else 0
                        take(*part("hg", c), dst[:, c % HEADS, :], f, c0=off, n=L - off)

            def take_gate(c):
                take(*part("gate", c), gates[:, c, :], ACT.Sigmoid, n=SEQ, bias=vec("b_gate", c))

            act.wait_ge(sem("mla_probs"), MLA_N)
            act.wait_ge(sem("mla_o"), MLA_N)
            for h in range(HEADS):
                take("vT", h, v_tok[:, :, h * P:(h + 1) * P], n=2 * P,
                     view=lambda s: s.rearrange("p (t n) -> p t n", t=2), count=False)
                take("vT", h, v_meta[0:META, h * P:(h + 1) * P], rows=META, c0=2 * P, n=P)
                if h % 2:
                    take_gate(h // 2)
            for c in range(4, 16):
                take_gate(c)
            for h in range(HEADS):
                act.wait_ge(sem("mla_o_out"), 2 * h + 2)
                af(x_hi[:, h, META:L], o_mla[:, h, :], ACT.Copy).then_inc(sem("hi_mla"), 1)
            for h in range(HEADS):
                take("kT", h, kT_tok[:, h, :], n=P, count=False)
                take("kT", h, kT_meta[0:META, h, :], rows=META, c0=P, n=P)
                if h % 2:
                    take(*part("mlo", h // 2), y_mla[:, h // 2, :], n=SEQ)
            for h in range(HEADS):
                take("S", h, S1[:, h, :], n=P, count=False)
                take("S", h, S2[:, h, :], c0=P, n=P)
            warm(ACT.Sqrt)
            for h in range(HEADS):
                take("o", h, o_h[:, h, :], n=SEQ)

            for h in range(HEADS):
                squares("hg", h, o_h[:, h, :], lambda: out_of_psum(act, "o", h), SEQ)
                if h % 2:
                    std("hg", h + 1, 2 + h // 2, eps_rms, hg_rs[:, h // 2 % 2, :],
                        guard=(sem("y_hg"), h - 3) if h > 3 else (sem("lo_pre"), DC))
                    for i in range(max(h - 3, 0), h - 1):
                        split("hg", i, y_hi[:, i, :], y_hg[:, i, :], (sem("y_hg"), i + 1))
                    take(*part("mlo", 4 + h // 2), y_mla[:, 4 + h // 2, :], n=SEQ)
            for h in range(HEADS - 2, HEADS):
                split("hg", h, y_hi[:, h, :], y_hg[:, h, :], (sem("y_hg"), h + 1))
            for c in range(DC):
                take(*part("hgo", c), ya[:, c, :], n=SEQ)
            for c in range(DC):
                take(*part("mix", c), mixed[:, c, :], n=SEQ)
                squares("post", c, mixed[:, c, :], lambda: out_of_psum(act, *part("mix", c)), SEQ)
            std("post", DC, 2, eps_rms, nrm[:, 0, 0:SEQ])
            for c in range(DC):
                def ready():
                    act.wait_ge(sem("h_mid"), c + 1)
                    act.wait_ge(sem("sum_post"), DC)
                squares("fpre", c, hT[:, c, META:L], ready, SEQ)
            std("fpre", DC, 3, eps_rms, nrm[:, 1, 0:SEQ])
            warm(ACT.Silu)
            for c in range(DC):
                split("fpre", c, x_hi[:, c, META:L], u_t[:, c % 4, 0:SEQ], (sem("u"), DC + c + 1))
            for j in range(FC):
                if j >= 4:
                    act.wait_ge(sem("lo_hid"), j - 3)
                take(*ffi_chunk(j, 0), hid[:, j % 4, :], ACT.Silu, n=SEQ)
                if j % 2:
                    for i in (j - 1, j):
                        if i >= 2:
                            act.wait_ge(sem("hi_hid"), i - 1)
                        take(*ffi_chunk(i, 1), up[:, i % 2, :], n=SEQ)
            warm(ACT.Sqrt)
            for c in range(DC):
                for q in range(3):
                    act.wait_ge(sem("piece_done"), 3 * c + q + 1)
                    round_piece(SPLIT[f"ffo{2 * c + q // 2}", q % 2] + PAIRS)
                take("ffo", c, ffo[:, c, :], n=SEQ)
                round_piece(SPLIT[f"ffo{2 * c + 1}", 1] + PAIRS)
                squares("fpost", c, ffo[:, c, :], lambda: out_of_psum(act, "ffo", c), SEQ)
            std("fpost", DC, 2, eps_rms, nrm[:, 0, 0:SEQ])
            for c in range(DC):
                split("L0h", c, x_hi[:, c, :], hT[:, c, :], (sem("h_ready"), c + 1))

            for l in range(DEPTH2):
                T = f"L{l}"
                q_from = 0 if l == 0 else META
                n_q = L - q_from
                take(f"{T}kw", 0, kiT)
                take(f"{T}kw", 1, idx_w, n=16, view=lambda s: s.rearrange("p (t n) -> p t n", t=2), scale=IDX_W_SCALE)
                for i in range(4):
                    take(*part(f"{T}qi", i), qiT[:, i, q_from:L], n=n_q)
                take(*part(f"{T}a", 0), upad[:, 0, TAPS - 1:TAPS - 1 + L])
                for s in range(16):
                    t, h = divmod(s, HEADS)
                    nk = Q_TILES[t][2]
                    act.wait_ge(sem("idx"), 16 * l + s + 1)
                    if s >= 2:
                        act.wait_ge(sem("score"), 16 * l + s - 1)
                    af(relu[:, s % 2, 0:nk], PS[:, 2 + s % 2, 0:nk], ACT.Relu, scale=IDX_SCALE)\
                        .then_inc(sem("relu"), 1)
                    if s in (3, 7, 11):
                        take(*part(f"{T}a", 1 + s // 4), upad[:, 1 + s // 4, TAPS - 1:TAPS - 1 + L])
                for c in range(CC):
                    take(*part(f"{T}g", c), gsig[:, c, :], ACT.Sigmoid)
                for i in range(4):
                    take(*part(f"{T}q", i), q2[:, i, q_from:L], n=n_q)
                for i in range(4):
                    take(*part(f"{T}k", i), k2[:, i, :])
                for i in range(4):
                    take(*part(f"{T}v", i), vT2[:, i, :])
                for x, (t0, n) in enumerate(KEY_CHUNKS):
                    take(f"{T}vt", x, v2[0:n, x, :], rows=n, n=512)
                for s in range(DSA_N[l] + DSA_LAG + 1):
                    attention_step(s, f"{T}att", DSA_STEPS[l], at2_s, at2_p, at2_pt, at2_r,
                                   lambda h, q0, nq: o_tok[0:nq, O_AT[q0], h * HD:(h + 1) * HD], lag=DSA_LAG, late=True)
                    if s == DSA_N[l] + DSA_LAG:
                        out_of_psum(act, *part(f"{T}za", 2))
                        af(szc[:, :, q_from:L], szc[:, :, q_from:L], ACT.Silu).then_inc(sem(f"{T}gates"), 1)
                        for c in range(CC):
                            act.wait_ge(sem(f"{T}cln_scaled"), c + 1)
                            af(ycat[:, c, q_from:L], acc[:, c, q_from:L], ACT.Silu, scale=vec("conv_ln_g_2", 4 * l + c),
                               bias=vec("conv_ln_b_2", 4 * l + c)).then_inc(sem(f"{T}silu"), 1)
                        af(sza[:, 0:3, q_from:L], sza[:, 0:3, q_from:L], ACT.Silu).then_inc(sem(f"{T}gates"), 1)
                    for n, m in z_chunks(l, s):
                        last = (n, m) == ("za", 3)
                        take(*part(f"{T}{n}", m), (szc if n == "zc" else sza)[:, m, q_from:L],
                             ACT.Silu if last else ACT.Copy, n=n_q)
                    if s == CLN_STEP[l] + 2:
                        for c in range(CC):
                            act.wait_ge(sem(f"{T}cln_centred"), c + 1)
                            af(cln_sq[:, c, 0:n_q], acc[:, c, q_from:L], ACT.Square).then_inc(sem(f"sq_{T}cln"), 1)
                    if s == CLN_STEP[l] + 4:
                        std(f"{T}cln", 1, 7, eps_ln, nrm[:, 0, 0:n_q])

                act.wait_ge(sem("chunk_done"), CHUNK[f"{T}za1", 1] + 1)
                for c in range(DC):
                    split(f"{T}y", c, x_hi[:, c, q_from:L], ycat[:, c, q_from:L], (sem("y"), DC * l + c + 1))
                warm(ACT.Sqrt)
                for c in range(DC):
                    take(*part(f"{T}wo", c), zT[:, c, q_from:L], n=n_q)
                for c in range(DC):
                    squares(f"{T}pln", c, zT[:, c, q_from:L], lambda: act.wait_ge(sem(f"{T}pln_centred"), c + 1), n_q)
                std(f"{T}pln", DC, 5, eps_ln, nrm[:, 0, 0:n_q])
                for c in range(DC):
                    act.wait_ge(sem(f"{T}pln_scaled"), c + 1)
                    af(hT[:, c, q_from:L], zT[:, c, q_from:L], ACT.Identity, scale=vec("post_ln_g_2", 8 * l + c),
                       bias=vec("post_ln_b_2", 8 * l + c)).then_inc(sem("h_post"), 1)
            for half in range(2):
                for t in range(2):
                    take("out", 2 * half + t, out_tok[:, t, half * 512:half * 512 + 512], n=512)

        @block.vector
        def _(dve):
            v = nc.vector
            order = [0]

            def link(ins):
                order[0] += 1
                ins.then_inc(sem("dve_order"), 1)
                dve.wait_ge(sem("dve_order"), order[0])

            for i, dim in enumerate(MEANS):
                v.memset(means[:, i, :], 1.0 / dim).then_inc(sem("means"), 1)
            v.memset(small[:, 0:1], EPS_RMS)
            v.memset(small[:, 1:2], EPS_LN).then_inc(sem("small"), 1)
            for i in range(PAIRS):
                src, hi_w, _ = piece_views(i)
                w_ready(dve, PIECES[i][0])
                v.tensor_copy(hi_w, src).then_inc(sem("first_w_hi"), 1)
            out_of_psum(dve, "start", DC)
            l0 = cols[:, VEC["lb_logits"]:VEC["lb_logits"] + 8]
            l1 = cols[:, VEC["lb_logits"] + 8:VEC["lb_logits"] + 16]
            link(v.tensor_tensor(lb_m, l0, l1, ALU.max))
            v.tensor_tensor(lb_e0, l0, lb_m, ALU.subtract).then_inc(sem("lb_shift"), 1)
            v.tensor_tensor(lb_e1, l1, lb_m, ALU.subtract).then_inc(sem("lb_shift"), 1)

            def rstd(tag, count, buf):
                dve.wait_ge(sem(f"std_{tag}"), count)
                link(v.reciprocal(buf, buf))

            def split(tag, dst, src):
                v.tensor_copy(dst, src).then_inc(sem(f"hi_{tag}"), 1)

            def norm(tag, name, src, rs, n):
                for c in range(DC):
                    if c >= 4:
                        dve.wait_ge(sem(f"lo_{tag}"), c - 3)
                    v.scalar_tensor_tensor(out=u_t[:, c % 4, 0:n], in0=src(c), scalar=vec(name, c), in1=rs,
                                           op0=ALU.mult, op1=ALU.mult).then_inc(sem("u"), 1)

            rstd("pre", 1, nrm[:, 0, :])
            norm("pre", "mix_pre_g", lambda c: hT[:, c, :], nrm[:, 0, :], L)
            dve.wait_ge(sem("lb_exp"), 2)
            link(v.tensor_tensor(lb_m, lb_e0, lb_e1, ALU.add))
            link(v.reciprocal(lb_m, lb_m))
            link(v.tensor_tensor(lb, lb_e0, lb_m, ALU.mult))
            link(v.tensor_scalar(oml, lb, -1.0, 1.0, ALU.mult, ALU.add))

            for tag, b, first, name in (("cq", 0, 0, "q_a_norm_g"), ("ckv", 1, 2, "kv_a_norm_g")):
                rstd(tag, 1, nrm[:, b, :])
                for c in range(2):
                    v.scalar_tensor_tensor(out=c_nrm[:, first + c, :], in0=c_raw[:, first + c, :],
                                           scalar=vec(name, c), in1=nrm[:, b, :],
                                           op0=ALU.mult, op1=ALU.mult).then_inc(sem("c_nrm"), 1)

            def rope(tag, i, src, dst, t0, n, ta, tb):
                v.tensor_tensor(ta[:, i % 2, 0:n], src, cosT[:, t0:t0 + n], ALU.mult)
                dve.wait_ge(sem(f"{tag}_rope"), i + 1)
                v.tensor_tensor(tb[:, i % 2, 0:n], PS[:, 6 + i % 2, 0:n], sinT[:, t0:t0 + n], ALU.mult)\
                    .then_inc(sem(f"{tag}_rope_out"), 1)
                dve.wait_ge(sem(f"{tag}_rope_out"), i + 1)
                v.tensor_tensor(dst, ta[:, i % 2, 0:n], tb[:, i % 2, 0:n], ALU.add).then_inc(sem(f"{tag}_roped"), 1)

            dve.wait_ge(sem("tables_in"), 16)
            out_of_psum(dve, "wqb", 11)
            for i in range(4):
                rope("mla", i, qpe[:, i, :], qpr[:, i, :], META, SEQ, rope_a, rope_b)
            rope("mla", 4, kpe, kpr, 0, L, rope_a, rope_b)

            def attention_step(i, tag, steps, scale, mask_of, s_buf, r_buf, lag):
                if i < len(steps):
                    h, q0, nq, nk = steps[i]
                    dve.wait_ge(sem(f"{tag}_scores"), i + 1)
                    if i >= 2:
                        dve.wait_ge(sem(f"{tag}_exp"), i - 1)
                    v.tensor_tensor_reduce(out=s_buf[0:nq, i % 2, 0:nk], in0=PS[0:nq, 2 + i % 2, 0:nk],
                                           in1=mask_of(q0, nq, nk), scale=-scale, scalar=BIG,
                                           op0=ALU.add, op1=ALU.min,
                                           accum_out=r_buf[0:nq, i % 8, 0:1]).then_inc(sem(f"{tag}_masked"), 1)
                j = i - lag
                if 0 <= j < len(steps):
                    nq = steps[j][2]
                    dve.wait_ge(sem(f"{tag}_exp"), j + 1)
                    v.reciprocal(r_buf[0:nq, j % 8, 1:2], r_buf[0:nq, j % 8, 1:2]).then_inc(sem(f"{tag}_inv"), 1)

            def forget(h):
                out_of_psum(dve, *part("hg", HEADS + h))
                v.tensor_scalar(hf[:, h, :], hf[:, h, :], oml[:, h:h + 1], lb[:, h:h + 1], ALU.mult, ALU.add)\
                    .then_inc(sem("f_ready"), 1)

            for s in range(MLA_N):
                attention_step(s, "mla", MLA_STEPS, MLA_SCALE, lambda q0, nq, nk: cst(CAUSAL[q0])[0:nq, :], att_s, att_r, 0)
                if 8 <= s < 8 + HEADS:
                    forget(s - 8)

            dve.wait_ge(sem("mla_o"), MLA_N)
            dve.wait_ge(sem("f_ready"), HEADS)
            for half in range(2):
                s = slice(1088 * half, 1088 * half + 1088)
                v.tensor_scalar(flat["k"][:, s], flat["f"][:, s], -1.0, 1.0, ALU.mult, ALU.add)\
                    .then_inc(sem("level_ready"), 1)
            out_of_psum(dve, "vT", HEADS - 1)
            lvl = cst("level").rearrange("p (l n) -> p l n", n=P)
            blocks = [flat["f"]]
            at = 0
            for lv in range(4):
                n = HEADS * L >> (lv + 1)
                blocks.append(tree[:, at:at + n])
                at += n
            t16 = blocks[4].rearrange("p (h b) -> p h b", h=HEADS)
            t32, t64, t128 = (tree[:, at + o:at + o + 8 * n].rearrange("p (h b) -> p h b", h=HEADS)
                              for o, n in ((0, 8), (64, 4), (96, 2)))
            for lv in range(LEVELS + 1):
                for half in range(2):
                    for b in range(2):
                        i = 4 * lv + 2 * half + b
                        dve.wait_ge(sem("level_done"), i + 1)
                        dst = scoresT[:, 8 * half + 4 * b:8 * half + 4 * b + 4, :]
                        src = PS[:, 2 + 2 * half + b, :].rearrange("p (j n) -> p j n", n=P)
                        m = lvl[:, lv:lv + 1, :].to_broadcast([P, 4, P])
                        if lv == 0:
                            v.tensor_tensor(dst, src, m, ALU.mult).then_inc(sem("level_masked"), 1)
                        else:
                            v.copy_predicated(dst, m.bitcast(U32), src).then_inc(sem("level_masked"), 1)
                    hs = slice(4 * half, 4 * half + 4)
                    if lv == 0:
                        v.tensor_tensor(flat["q"][:, 1088 * half:1088 * half + 1088],
                                        flat["q"][:, 1088 * half:1088 * half + 1088],
                                        flat["f"][:, 1088 * half:1088 * half + 1088], ALU.mult)\
                            .then_inc(sem("level_ready"), 1)
                        continue
                    B = 1 << (lv - 1)
                    if B < 16:
                        n = 1088 // (2 * B)
                        view = lambda x: x[:, 1088 * half:1088 * half + 1088].rearrange("p (n u b) -> p n u b", u=2, b=B)
                        qv, kv = view(flat["q"]), view(flat["k"])
                        tot = blocks[lv - 1][:, n * 2 * half:n * 2 * half + 2 * n].rearrange("p (n u) -> p n u", u=2)
                        nxt = blocks[lv][:, n * half:n * half + n]
                        lo = tot[:, :, 0:1].to_broadcast([P, n, B])
                        hi_ = tot[:, :, 1:2].to_broadcast([P, n, B])
                        q_up, k_lo = qv[:, :, 1, :], kv[:, :, 0, :]
                        lo1, hi1 = tot[:, :, 0], tot[:, :, 1]
                    else:
                        n = SEQ // (2 * B)
                        view = lambda x: x[:, hs, META:L].rearrange("p h (n u b) -> p h n u b", u=2, b=B)
                        qv, kv = view(hq), view(hk)
                        tot = {16: t16[:, hs, 1:17], 32: t32[:, hs, :], 64: t64[:, hs, :]}[B]
                        tot = tot.rearrange("p h (n u) -> p h n u", u=2)
                        nxt = {16: t32, 32: t64, 64: t128}[B][:, hs, :]
                        lo = tot[:, :, :, 0:1].to_broadcast([P, 4, n, B])
                        hi_ = tot[:, :, :, 1:2].to_broadcast([P, 4, n, B])
                        q_up, k_lo = qv[:, :, :, 1, :], kv[:, :, :, 0, :]
                        lo1, hi1 = tot[:, :, :, 0], tot[:, :, :, 1]
                    v.tensor_tensor(q_up, q_up, lo, ALU.mult)
                    link(v.tensor_tensor(nxt, lo1, hi1, ALU.mult))
                    v.tensor_tensor(k_lo, k_lo, hi_, ALU.mult).then_inc(sem("level_ready"), 1)
            for h in range(HEADS):
                out_of_psum(dve, "S", h)
                v.scalar_tensor_tensor(out=S2[:, h, :], in0=S1[:, h, :], scalar=t128[:, h, 0:1], in1=S2[:, h, :],
                                       op0=ALU.mult, op1=ALU.add).then_inc(sem("state"), 1)

            def gate_mla(c):
                out_of_psum(dve, *part("mlo", c))
                v.tensor_tensor(y_mla[:, c, :], y_mla[:, c, :], gates[:, DC + c, :], ALU.mult)\
                    .then_inc(sem("b_gated"), 1)

            for c in range(4):
                gate_mla(c)
            dve.wait_ge(sem("chunk_done"), CHUNK["o", HEADS - 1] + 1)
            for h in range(HEADS):
                if h % 2 == 0:
                    rstd("hg", h // 2 + 1, hg_rs[:, h // 2 % 2, :])
                link(v.scalar_tensor_tensor(out=o_h[:, h, :], in0=o_h[:, h, :], scalar=vec("hg_norm_g", 0),
                                            in1=hg_rs[:, h // 2 % 2, h % 2 * SEQ:h % 2 * SEQ + SEQ], op0=ALU.mult, op1=ALU.mult))
                v.tensor_tensor(y_hg[:, h, :], o_h[:, h, :], hg[:, h, :], ALU.mult).then_inc(sem("y_hg"), 1)
            for c in range(4, DC):
                gate_mla(c)

            dve.wait_ge(sem("b_gated"), DC)
            dve.wait_ge(sem("chunk_done"), CHUNK["mlo3", 1] + 1)
            for c in range(DC):
                out_of_psum(dve, *part("hgo", c))
                link(v.tensor_tensor(ya[:, c, :], ya[:, c, :], gates[:, c, :], ALU.mult))
                link(v.tensor_tensor(ya[:, c, :], ya[:, c, :], y_mla[:, c, :], ALU.add))
                split("mix", x_hi[:, c, META:L], ya[:, c, :])
            rstd("post", 1, nrm[:, 0, 0:SEQ])
            for c in range(DC):
                link(v.scalar_tensor_tensor(out=mixed[:, c, :], in0=mixed[:, c, :], scalar=vec("mix_post_g", c),
                                            in1=nrm[:, 0, 0:SEQ], op0=ALU.mult, op1=ALU.mult))
                v.tensor_tensor(hT[:, c, META:L], hT[:, c, META:L], mixed[:, c, :], ALU.add).then_inc(sem("h_mid"), 1)
            rstd("fpre", 1, nrm[:, 1, 0:SEQ])
            norm("fpre", "ffn_pre_g", lambda c: hT[:, c, META:L], nrm[:, 1, 0:SEQ], SEQ)
            for j in range(FC):
                out_of_psum(dve, *ffi_chunk(j, 1))
                link(v.tensor_tensor(hid[:, j % 4, :], hid[:, j % 4, :], up[:, j % 2, :], ALU.mult))
                split("hid", hid_hi[:, j, :], hid[:, j % 4, :])
            rstd("fpost", 1, nrm[:, 0, 0:SEQ])
            link(v.tensor_copy(hT[:, :, 0:META], vec_rows[:, 0, :].rearrange("p (c t) -> p c t", c=DC)))
            for c in range(DC):
                link(v.scalar_tensor_tensor(out=ffo[:, c, :], in0=ffo[:, c, :], scalar=vec("ffn_post_g", c),
                                            in1=nrm[:, 0, 0:SEQ], op0=ALU.mult, op1=ALU.mult))
                v.tensor_tensor(hT[:, c, META:L], hT[:, c, META:L], ffo[:, c, :], ALU.add).then_inc(sem("h_ready"), 1)

            v.memset(upad[:, :, 0:TAPS - 1], 0.0)
            v.memset(top8[:, :, :], NEG)
            for l in range(DEPTH2):
                T = f"L{l}"
                q_from = 0 if l == 0 else META
                n_all = L - q_from
                if l:
                    for c in range(DC):
                        dve.wait_ge(sem("h_post"), c + 1)
                        split(f"{T}h", x_hi[:, c, :], hT[:, c, :])
                out_of_psum(dve, f"{T}kw", 0)
                rope("i", 5 * l, kiT, kir, 0, L, rope2_a, rope2_b)
                for i in range(4):
                    out_of_psum(dve, *part(f"{T}qi", i))
                    rope("i", 5 * l + 1 + i, qiT[:, i, q_from:L], qir[:, i, q_from:L], q_from, n_all, rope2_a, rope2_b)
                for s in range(16):
                    t, h = divmod(s, HEADS)
                    q0, nq, nk = Q_TILES[t]
                    dve.wait_ge(sem("relu"), 16 * l + s + 1)
                    if s:
                        dve.wait_ge(sem("score"), 16 * l + s)
                    v.scalar_tensor_tensor(out=score[:, t, 0:nk], in0=relu[:, s % 2, 0:nk], scalar=idx_w[:, t, h:h + 1],
                                           in1=cst(CAUSAL[q0]) if h == 0 else score[:, t, 0:nk],
                                           op0=ALU.mult, op1=ALU.add).then_inc(sem("score"), 1)
                dve.wait_ge(sem("score"), 16 * (l + 1))
                for r in range(ROUNDS):
                    for t in range(2):
                        nk = Q_TILES[t][2]
                        v.max(top8[:, t, :], score[:, t, 0:nk]).then_inc(sem("top"), 1)
                    for t in range(2):
                        nk = Q_TILES[t][2]
                        dve.wait_ge(sem("top"), 4 * (ROUNDS * l + r) + 2)
                        if r == ROUNDS - 1 and TOPK % 8:
                            link(v.memset(top8[:, t, TOPK % 8:8], NEG))
                        v.match_replace(score[:, t, 0:nk], in_to_replace=top8[:, t, :], in_values=score[:, t, 0:nk],
                                        imm_value=NEG).then_inc(sem("top"), 1)
                    dve.wait_ge(sem("top"), 4 * (ROUNDS * l + r) + 4)
                    if r >= ROUNDS - CC:
                        c = r - (ROUNDS - CC)
                        out_of_psum(dve, *part(f"{T}g", c))
                        v.tensor_tensor(upad[:, c, TAPS - 1:TAPS - 1 + L], upad[:, c, TAPS - 1:TAPS - 1 + L],
                                        gsig[:, c, :], ALU.mult).then_inc(sem(f"{T}gated"), 1)
                for t in range(2):
                    q0, nq, nk = Q_TILES[t]
                    link(v.tensor_scalar(sel[:, t, 0:nk], score[:, t, 0:nk], NEG, NEG, ALU.not_equal, ALU.mult))
                    link(v.tensor_tensor(sel[:, t, 0:nk], sel[:, t, 0:nk], cst(CAUSAL[q0]), ALU.min))

                def taps(first, last):
                    for j in range(first, last):
                        for c in range(CC):
                            w = tap_weight(l, j, c)
                            if j == 0:
                                ins = v.tensor_scalar(acc[:, c, :], upad[:, c, 0:L], w, vec("conv_b_2", 4 * l + c),
                                                      ALU.mult, ALU.add)
                            else:
                                dve.wait_ge(sem(f"{T}tap"), CC * (j - 1) + c + 1)
                                ins = v.scalar_tensor_tensor(out=acc[:, c, :], in0=upad[:, c, j:j + L], scalar=w,
                                                             in1=acc[:, c, :], op0=ALU.mult, op1=ALU.add)
                            ins.then_inc(sem(f"{T}tap"), 1)

                dve.wait_ge(sem(f"{T}gated"), CC)
                for i in range(8):
                    if i >= 4:
                        taps(i - 4, i - 3)
                    src, dst = (q2, q2r) if i < 4 else (k2, k2r)
                    t0 = q_from if i < 4 else 0
                    out_of_psum(dve, *part(f"{T}{'q' if i < 4 else 'k'}", i % 4))
                    rope("q", 8 * l + i, src[:, i % 4, t0:L], dst[:, i % 4, t0:L], t0, L - t0, rope2_a, rope2_b)
                def centre(tag, count, src, bank_):
                    dve.wait_ge(sem(f"{tag}_mean"), 1)
                    for c in range(count):
                        v.tensor_tensor(src(c), src(c), PS[:, bank_, 0:n_all], ALU.subtract).then_inc(sem(f"{tag}_centred"), 1)

                def scale(tag, count, src):
                    rstd(tag, 1, nrm[:, 0, 0:n_all])
                    dve.wait_ge(sem(f"sq_{tag}"), count)
                    for c in range(count):
                        v.tensor_tensor(src(c), src(c), nrm[:, 0, 0:n_all], ALU.mult).then_inc(sem(f"{tag}_scaled"), 1)

                for s in range(max(CLN_STEP[l] + 6, DSA_N[l] + 1)):
                    attention_step(s, f"{T}att", DSA_STEPS[l], ATT_SCALE,
                                   lambda q0, nq, nk: cst("causal_m")[0:nq, :] if q0 == 0
                                   else sel[:, (q0 - META) // P, 0:nk], at2_s, at2_r, 1)
                    if s < CLN_STEP[l]:
                        a_, b_ = (4 + x * (TAPS - 4) // CLN_STEP[l] for x in (s, s + 1))
                        taps(a_, b_)
                    if s == CLN_STEP[l] + 1:
                        centre(f"{T}cln", CC, lambda c: acc[:, c, q_from:L], 7)
                    if s == CLN_STEP[l] + 5:
                        scale(f"{T}cln", CC, lambda c: acc[:, c, q_from:L])

                dve.wait_ge(sem(f"{T}gates"), 1)
                for c in range(CC):
                    dve.wait_ge(sem(f"{T}silu"), c + 1)
                    v.tensor_tensor(ycat[:, c, q_from:L], ycat[:, c, q_from:L], szc[:, c, q_from:L], ALU.mult)\
                        .then_inc(sem("y"), 1)
                dve.wait_ge(sem(f"{T}gates"), 2)
                out_of_psum(dve, *part(f"{T}za", 3))
                for c in range(CC):
                    dve.wait_ge(sem(f"{T}o_turned"), c + 1)
                    v.tensor_tensor(ycat[:, CC + c, q_from:L], PS[:, TURN_BANKS[c], q_from:L], sza[:, c, q_from:L],
                                    ALU.mult).then_inc(sem("y"), 1)
                for c in range(DC):
                    out_of_psum(dve, *part(f"{T}wo", c))
                    v.scalar_tensor_tensor(out=zT[:, c, q_from:L], in0=hT[:, c, q_from:L], scalar=ALPHA,
                                           in1=zT[:, c, q_from:L], op0=ALU.mult, op1=ALU.add)\
                        .then_inc(sem(f"{T}pln_in"), 1)
                dve.wait_ge(sem(f"{T}pln_in"), DC)
                centre(f"{T}pln", DC, lambda c: zT[:, c, q_from:L], 4)
                scale(f"{T}pln", DC, lambda c: zT[:, c, q_from:L])


_INS = ["x", "meta_tokens", "w_in", "b_gate", "lb_logits", "hg_norm_g", "w_hg_o", "q_a_norm_g", "w_q_b",
        "kv_a_norm_g", "w_kv_b", "w_mla_o", "w_out", "mix_pre_g", "mix_post_g", "ffn_pre_g", "ffn_post_g",
        "w_ffn_in", "w_ffn_out", "meta_tokens_2", "w_in_2", "conv_w_2", "conv_b_2", "conv_ln_g_2",
        "conv_ln_b_2", "w_out_2", "post_ln_g_2", "post_ln_b_2"]


def kernel(**inputs):
    import numpy as _np
    import concourse.bacc as _bacc
    from concourse import mybir as _mybir
    from concourse.bass_utils import run_bass_kernel_spmd as _run

    nc = _bacc.Bacc("TRN2", target_bir_lowering=False, num_devices=1)
    arrays, args = {}, {}
    for name in _INS + ["constants"]:
        arr = shape_constants() if name == "constants" else _np.ascontiguousarray(inputs[name])
        arrays[f"in_{name}"] = arr
        args[name] = nc.dram_tensor(f"in_{name}", arr.shape, _mybir.dt.from_np(arr.dtype), kind="ExternalInput").ap()
    out = nc.dram_tensor("out", (1, SEQ, D), F32, kind="ExternalOutput").ap()
    bass_blocks(nc, args, out)
    r = _run(nc, [arrays], core_ids=[0])
    return r.results[0]["out"]
```
